# Optimizing a Trainium2 kernel written in Bass

```python
import jax, jax.numpy as jnp
from jax import lax
import numpy as np

D_MODEL = 1024
BATCH = 1
SEQ = 2048
DEPTH = 1

N_MIXERS = 2
N_CONV_LAYERS = (DEPTH + N_MIXERS - 1) // N_MIXERS
N_RWKV_LAYERS = DEPTH // N_MIXERS
CONV_WIDTH = 3
RWKV_HEAD_DIM = 64
RWKV_HEADS = D_MODEL // RWKV_HEAD_DIM
DECAY_LORA = 64
ICLR_LORA = 64
GATE_LORA = 128
N_DIRECTIONS = 2
N_TOKEN_SHIFT_MIX = 6
GN_EPS = 64e-5
MEM_LEN = 256
XATTN_HEADS = 4
XATTN_HEAD_DIM = D_MODEL // XATTN_HEADS
N_EXPERTS = 16
CAPACITY_FACTOR = 2
EXPERT_D_FF = 1024
RMS_EPS = 1e-6

kernel_name = "hybrid_conv_rwkv7_ecmoe_encoder"

def rms_norm(x, g):
    xf = x.astype(jnp.float32)
    y = xf * lax.rsqrt(jnp.mean(xf * xf, axis=-1, keepdims=True) + RMS_EPS)
    return (y * g.astype(jnp.float32)).astype(x.dtype)

def short_conv_mixer(xn, w_in, conv_w, w_out):
    s = xn.shape[1]
    b_gate, c_gate, hx = jnp.split(xn @ w_in, 3, axis=-1)
    u = c_gate * hx
    up = jnp.pad(u, ((0, 0), (1, 1), (0, 0)))
    conv = up[:, :s] * conv_w[0] + up[:, 1:s + 1] * conv_w[1] + up[:, 2:] * conv_w[2]
    return (b_gate * conv) @ w_out

def wkv_scan(r, w, k, v, kk, a, reverse):
    b, s, h, n = r.shape
    seqs = tuple(jnp.moveaxis(t, 1, 0) for t in (r, w, k, v, kk, kk * a))

    def step(state, inp):
        r_t, w_t, k_t, v_t, kk_t, b_t = inp
        sa = jnp.einsum('bhvk,bhk->bhv', state, kk_t)
        state = (state * w_t[:, :, None, :]
                 - sa[..., None] * b_t[:, :, None, :]
                 + v_t[..., None] * k_t[:, :, None, :])
        y_t = jnp.einsum('bhvk,bhk->bhv', state, r_t)
        return state, y_t

    state0 = jnp.zeros((b, h, n, n), jnp.float32)
    _, ys = lax.scan(step, state0, seqs, reverse=reverse)
    return jnp.moveaxis(ys, 0, 1)

def rwkv7_bidirectional(xn, mu, w_rkv, w0, w1, w2, a0, a1, a2, g1, g2,
                        k_k, k_a, r_k, ln_w, ln_b, w_out):
    b, s, d = xn.shape
    h, n = RWKV_HEADS, RWKV_HEAD_DIM
    f32 = jnp.float32
    xp = jnp.pad(xn, ((0, 0), (1, 1), (0, 0)))
    xx = 0.5 * (xp[:, :s] + xp[:, 2:]) - xn
    x_rkv = xn[None] + xx[None] * mu[:3, None, None, :]
    rkv = jnp.einsum('nbsd,nde->nbse', x_rkv, w_rkv)
    r, k, v = rkv[0], rkv[1], rkv[2]
    xw = xn + xx * mu[3]
    xa = xn + xx * mu[4]
    xg = xn + xx * mu[5]
    w_raw = w0[:, None, None, :] + jnp.einsum(
        'nbsl,nld->nbsd', jnp.tanh(jnp.einsum('bsd,ndl->nbsl', xw, w1)), w2)
    log_w = -jax.nn.softplus(-w_raw.astype(f32)) - 0.5
    decay = jnp.exp(-jnp.exp(log_w))
    iclr = jax.nn.sigmoid((a0[:, None, None, :] + jnp.einsum(
        'nbsl,nld->nbsd', jnp.einsum('bsd,ndl->nbsl', xa, a1), a2)).astype(f32))
    gate = jax.nn.sigmoid(xg @ g1) @ g2
    kk = (k * k_k).astype(f32).reshape(b, s, h, n)
    kk = kk / jnp.maximum(jnp.linalg.norm(kk, axis=-1, keepdims=True), 1e-12)
    k_dir = k.astype(f32)[None] * (1.0 + (iclr - 1.0) * k_a.astype(f32))

    def heads(t):
        return t.reshape(t.shape[:-1] + (h, n))

    r_h, v_h = heads(r.astype(f32)), heads(v.astype(f32))
    k_h, w_h, a_h = heads(k_dir), heads(decay), heads(iclr)
    y = (wkv_scan(r_h, w_h[0], k_h[0], v_h, kk, a_h[0], False)
         + wkv_scan(r_h, w_h[1], k_h[1], v_h, kk, a_h[1], True))
    mean = jnp.mean(y, axis=-1, keepdims=True)
    var = jnp.mean(jnp.square(y - mean), axis=-1, keepdims=True)
    y = ((y - mean) * lax.rsqrt(var + GN_EPS)).reshape(b, s, d)
    y = y * ln_w.astype(f32) + ln_b.astype(f32)
    bonus = jnp.sum(r_h[None] * k_h * r_k.astype(f32), axis=(0, -1))[..., None] * v_h
    y = y + bonus.reshape(b, s, d)
    return (y.astype(xn.dtype) * gate) @ w_out

def memory_cross_attention(xn, memn, w_q, w_kv, w_o):
    b, s, d = xn.shape
    m = memn.shape[1]
    q = (xn @ w_q).reshape(b, s, XATTN_HEADS, XATTN_HEAD_DIM)
    kv = (memn @ w_kv).reshape(b, m, 2, XATTN_HEADS, XATTN_HEAD_DIM)
    k, v = kv[:, :, 0], kv[:, :, 1]
    scores = jnp.einsum('bshd,bmhd->bhsm', q, k).astype(jnp.float32) * XATTN_HEAD_DIM ** -0.5
    p = jax.nn.softmax(scores, axis=-1).astype(v.dtype)
    o = jnp.einsum('bhsm,bmhd->bshd', p, v).reshape(b, s, d)
    return o @ w_o

def expert_choice_moe(xn, router, w_gate, w_up, w_down):
    b, s, d = xn.shape
    cap = CAPACITY_FACTOR * s // N_EXPERTS
    probs = jax.nn.softmax((xn @ router).astype(jnp.float32), axis=-1)
    aff, idx = lax.top_k(jnp.swapaxes(probs, 1, 2), cap)
    bidx = jnp.arange(b)[:, None, None]
    xe = xn[bidx, idx]
    hid = jax.nn.silu(jnp.einsum('becd,edf->becf', xe, w_gate)) * jnp.einsum('becd,edf->becf', xe, w_up)
    ye = jnp.einsum('becf,efd->becd', hid, w_down) * aff[..., None].astype(xn.dtype)
    return jnp.zeros_like(xn).at[bidx, idx].add(ye)

def setup_inputs(seed: int = 0) -> dict:
    key = jax.random.key(seed)
    keys = iter(jax.random.split(key, 48))
    D, NC, NR, ND = D_MODEL, N_CONV_LAYERS, N_RWKV_LAYERS, N_DIRECTIONS
    E, F = N_EXPERTS, EXPERT_D_FF

    def nrm(shape, scale):
        return jax.random.normal(next(keys), shape, jnp.float32) * scale

    def gain(shape):
        return 1.0 + nrm(shape, 0.02)

    return {
        "x": nrm((BATCH, SEQ, D), 1.0),
        "mem": nrm((BATCH, MEM_LEN, D), 1.0),
        "norm_mix": gain((DEPTH, D)),
        "norm_xattn": gain((DEPTH, D)),
        "norm_mem": gain((DEPTH, D)),
        "norm_ffn": gain((DEPTH, D)),
        "norm_final": gain((D,)),
        "conv_w_in": nrm((NC, D, 3 * D), D ** -0.5),
        "conv_w": nrm((NC, CONV_WIDTH, D), 0.5),
        "conv_w_out": nrm((NC, D, D), D ** -0.5),
        "rwkv_mu": jax.random.uniform(next(keys), (NR, N_TOKEN_SHIFT_MIX, D), jnp.float32),
        "rwkv_w_rkv": nrm((NR, 3, D, D), D ** -0.5),
        "rwkv_w0": nrm((NR, ND, D), 1.0),
        "rwkv_w1": nrm((NR, ND, D, DECAY_LORA), D ** -0.5),
        "rwkv_w2": nrm((NR, ND, DECAY_LORA, D), 0.5 * DECAY_LORA ** -0.5),
        "rwkv_a0": nrm((NR, ND, D), 0.5),
        "rwkv_a1": nrm((NR, ND, D, ICLR_LORA), D ** -0.5),
        "rwkv_a2": nrm((NR, ND, ICLR_LORA, D), 0.5 * ICLR_LORA ** -0.5),
        "rwkv_g1": nrm((NR, D, GATE_LORA), D ** -0.5),
        "rwkv_g2": nrm((NR, GATE_LORA, D), GATE_LORA ** -0.5),
        "rwkv_k_k": 0.85 + nrm((NR, D), 0.05),
        "rwkv_k_a": 1.0 + nrm((NR, D), 0.05),
        "rwkv_r_k": nrm((NR, RWKV_HEADS, RWKV_HEAD_DIM), 0.1),
        "rwkv_ln_w": gain((NR, D)),
        "rwkv_ln_b": nrm((NR, D), 0.02),
        "rwkv_w_out": nrm((NR, D, D), D ** -0.5),
        "xattn_w_q": nrm((DEPTH, D, D), D ** -0.5),
        "xattn_w_kv": nrm((DEPTH, D, 2 * D), D ** -0.5),
        "xattn_w_o": nrm((DEPTH, D, D), D ** -0.5),
        "moe_router": nrm((DEPTH, D, E), D ** -0.5),
        "moe_w_gate": nrm((DEPTH, E, D, F), D ** -0.5),
        "moe_w_up": nrm((DEPTH, E, D, F), D ** -0.5),
        "moe_w_down": nrm((DEPTH, E, F, D), F ** -0.5),
    }

def reference(x, mem, norm_mix, norm_xattn, norm_mem, norm_ffn, norm_final,
              conv_w_in, conv_w, conv_w_out,
              rwkv_mu, rwkv_w_rkv, rwkv_w0, rwkv_w1, rwkv_w2, rwkv_a0, rwkv_a1, rwkv_a2,
              rwkv_g1, rwkv_g2, rwkv_k_k, rwkv_k_a, rwkv_r_k, rwkv_ln_w, rwkv_ln_b, rwkv_w_out,
              xattn_w_q, xattn_w_kv, xattn_w_o,
              moe_router, moe_w_gate, moe_w_up, moe_w_down):
    h = x
    for i in range(DEPTH):
        j = i // N_MIXERS
        xn = rms_norm(h, norm_mix[i])
        if i % N_MIXERS == 0:
            h = h + short_conv_mixer(xn, conv_w_in[j], conv_w[j], conv_w_out[j])
        else:
            h = h + rwkv7_bidirectional(
                xn, rwkv_mu[j], rwkv_w_rkv[j], rwkv_w0[j], rwkv_w1[j], rwkv_w2[j],
                rwkv_a0[j], rwkv_a1[j], rwkv_a2[j], rwkv_g1[j], rwkv_g2[j],
                rwkv_k_k[j], rwkv_k_a[j], rwkv_r_k[j], rwkv_ln_w[j], rwkv_ln_b[j], rwkv_w_out[j])
        h = h + memory_cross_attention(rms_norm(h, norm_xattn[i]), rms_norm(mem, norm_mem[i]),
                                       xattn_w_q[i], xattn_w_kv[i], xattn_w_o[i])
        h = h + expert_choice_moe(rms_norm(h, norm_ffn[i]), moe_router[i],
                                  moe_w_gate[i], moe_w_up[i], moe_w_down[i])
    return rms_norm(h, norm_final)


_drawn_inputs = setup_inputs


def setup_inputs(seed=0):
    import zlib

    import numpy as np

    out = dict(_drawn_inputs(seed))
    spreads = {}
    factors = {'norm_xattn': 8.0, 'norm_mem': 8.0, 'norm_ffn': 4.311, 'norm_final': 2.743}
    for name, (base, spread) in spreads.items():
        noise = np.random.default_rng([zlib.crc32(name.encode()), seed]).standard_normal(out[name].shape)
        drawn = base * np.exp(spread * noise) if base else spread * noise
        out[name] = __import__('jax').numpy.asarray(drawn.astype(out[name].dtype))
    for name, factor in factors.items():
        out[name] = (out[name] * factor).astype(out[name].dtype)
    return out
```

```python
from contextlib import ExitStack

import concourse.bass as bass
from concourse import mybir

F32 = mybir.dt.float32
F32R = mybir.dt.float32r
BF16 = mybir.dt.bfloat16
I32 = mybir.dt.int32
U32 = mybir.dt.uint32
ALU = mybir.AluOpType
ACT = mybir.ActivationFunctionType
X = mybir.AxisListType.X

P = 128
D = 1024
SEQ = 2048
KB = D // P
T = 512
TB = T // P
TILES = SEQ // T
MEM = 256
MB = MEM // P
HEADS = 4
HD = D // HEADS
HB = HD // P
E = 16
CAP = 2 * SEQ // E
CB = CAP // P
FF = 1024
FB = FF // P
RMS_EPS = 1e-6
ROW = D + E
STRIP = 2048
POOL_PART = 512
STEP = 16
CONV_COLS = SEQ + 1


class Strips:

    def __init__(self, nc, ctx, name, raw, hi, lo):
        self.raw, self.hi, self.lo = raw, hi, lo
        self.loaded = [ctx.enter_context(nc.semaphore(f"{name}_strip_loaded{i}")) for i in range(2)]
        self.hi_done = ctx.enter_context(nc.semaphore(f"{name}_strip_hi"))
        self.lo_vector = ctx.enter_context(nc.semaphore(f"{name}_strip_lo_vector"))
        self.lo_pool = ctx.enter_context(nc.semaphore(f"{name}_strip_lo_pool"))
        self.used = ctx.enter_context(nc.semaphore(f"{name}_strip_used"))

    def load(self, sp, g, slot, source, blocks):
        sp.wait_ge(self.lo_vector, g + 1)
        sp.wait_ge(self.lo_pool, g + 1)
        sp.dma_start(self.raw[:, slot, :].rearrange("p (k n) -> p k n", k=blocks), source).then_inc(
            self.loaded[slot], STEP)

    def split_hi(self, act, g, slot, turn):
        act.wait_ge(self.loaded[slot], turn * STEP)
        act.wait_ge(self.used, g + 1)
        act.activation(self.hi[:, slot, :], self.raw[:, slot, :], ACT.Copy).then_inc(self.hi_done, 1)

    def split_lo(self, dve, g, slot):
        dve.wait_ge(self.hi_done, g + 1)
        a = STRIP - POOL_PART
        dve.tensor_tensor(self.lo[:, slot, 0:a], self.raw[:, slot, 0:a], self.hi[:, slot, 0:a].bitcast(F32),
                          ALU.subtract).then_inc(self.lo_vector, 1)

    def split_lo_pool(self, pool, g, slot):
        pool.wait_ge(self.hi_done, g + 1)
        a = STRIP - POOL_PART
        pool.tensor_tensor(self.lo[:, slot, a:], self.raw[:, slot, a:], self.hi[:, slot, a:].bitcast(F32),
                           ALU.subtract).then_inc(self.lo_pool, 1)

    def ready(self, pe, g):
        pe.wait_ge(self.lo_vector, g + 3)
        pe.wait_ge(self.lo_pool, g + 3)

    def done(self, engine, g):
        engine.wait_ge(self.used, g + 3)

    def views(self, slot, blocks):
        return (self.hi[:, slot, :].rearrange("p (k n) -> p k n", k=blocks),
                self.lo[:, slot, :].rearrange("p (k n) -> p k n", k=blocks))

    def open(self, dve=None, pool=None, pe=None):
        if dve is not None:
            dve.sem_inc(self.lo_vector, 2)
        if pool is not None:
            pool.sem_inc(self.lo_pool, 2)
        if pe is not None:
            pe.sem_inc(self.used, 2)


def apart(engine, spare):
    engine.sem_inc(spare, 1)


class Chain:

    def __init__(self, dve, sem, base=0):
        self.dve, self.sem, self.base, self.n = dve, sem, base, 0

    def __call__(self, instruction):
        self.n += 1
        instruction.then_inc(self.sem, 1)
        self.dve.wait_ge(self.sem, self.base + self.n)


def build(nc, x, mem, norm_mix, norm_xattn, norm_mem, norm_ffn, norm_final, conv_w_in, conv_w, conv_w_out,
          w_q, w_kv, w_o, router, w_gate, w_up, w_down, out):
    ctx = ExitStack()

    def sb(name, shape, dt=F32):
        return ctx.enter_context(nc.sbuf_tensor(name, shape, dt))

    w_raw = sb("w_raw", [P, 2, STRIP])
    w_hi = sb("w_hi", [P, 2, STRIP], F32R)
    w_lo = sb("w_lo", [P, 2, STRIP], F32R)
    act_hi = sb("act_hi", [P, KB, T], F32R)
    act_lo = sb("act_lo", [P, KB, T], F32R)
    q_hi = sb("q_hi", [P, KB, T], F32R)
    q_lo = sb("q_lo", [P, KB, T], F32R)
    h = sb("h", [P, TB * D])
    xs = sb("xs", [P, TB * D])
    vin = sb("vin", [P, KB * T])
    k_hi = sb("k_hi", [P, KB, MEM], F32R)
    k_lo = sb("k_lo", [P, KB, MEM], F32R)
    v_hi = sb("v_hi", [P, MB, D], F32R)
    v_lo = sb("v_lo", [P, MB, D], F32R)
    ident = sb("ident", [P, P])
    ones = sb("ones", [P, P])
    upper = sb("upper", [P, P])
    same_expert = sb("same_expert", [P, P])
    ramp = sb("ramp", [P, E])
    token_id = sb("token_id", [P, SEQ // P])
    ints = sb("ints", [P, P], I32)
    ints2 = sb("ints2", [P, P], I32)
    own_block = sb("own_block", [P, P])
    gains = sb("gains", [P, 3, KB])
    taps = sb("taps", [P, 3, KB])
    gain_row = sb("gain_row", [P, D])
    r_raw = sb("r_raw", [P, KB, E])
    r_hi = sb("r_hi", [P, KB, E], F32R)
    r_lo = sb("r_lo", [P, KB, E], F32R)
    probs = sb("probs", [P, SEQ // P * E])
    index = sb("index", [P, E * CB], U32)
    stat = sb("stat", [P, 64])
    junk = sb("junk", [P, TB, D], mybir.dt.uint8)
    indices = sb("indices", [P, 4 * CB], U32)
    primed = sb("primed", [16, CB, 16])
    r_buf = sb("r_buf", [P, TB * E])
    spare = ctx.enter_context(nc.semaphore("spare"))
    ps = ctx.enter_context(nc.psum_tensor("ps", [P, 8, T], F32))

    v_d = nc.dram_tensor("conv_v", [D, CONV_COLS], F32).ap()
    sum_d = nc.dram_tensor("residual", [SEQ, D], F32).ap()
    row_d = nc.dram_tensor("normed_rows", [SEQ, ROW], F32).ap()
    index_d = nc.dram_tensor("index_lists", [E, CAP], F32).ap()

    ss, var, root, rstd, tmp, tmp2 = (stat[:, 4 * i:4 * i + 4] for i in range(6))

    def bank(group, b=None):
        return ps[:, 4 * group:4 * group + 4, :] if b is None else ps[:, 4 * group + b, :]

    def product(pe, o, lhs, rhs, first, last):
        pe.matmul(o, lhs[0], rhs[0], start=first, stop=False)
        pe.matmul(o, lhs[0], rhs[1], start=False, stop=False)
        return pe.matmul(o, lhs[1], rhs[0], start=False, stop=last)

    def refine_rstd(dve, chain, n):
        chain(dve.reciprocal(rstd[:, 0:n], root[:, 0:n]))
        chain(dve.tensor_tensor(tmp[:, 0:n], rstd[:, 0:n], rstd[:, 0:n], ALU.mult))
        chain(dve.tensor_tensor(tmp2[:, 0:n], tmp[:, 0:n], var[:, 0:n], ALU.mult))
        chain(dve.tensor_scalar(tmp[:, 0:n], tmp2[:, 0:n], -0.5, 1.5, ALU.mult, ALU.add))
        chain(dve.tensor_tensor(rstd[:, 0:n], rstd[:, 0:n], tmp[:, 0:n], ALU.mult))

    def setup():
        pctx = ExitStack()
        sem = lambda name: pctx.enter_context(nc.semaphore(name))
        strips = Strips(nc, pctx, "setup", w_raw, w_hi, w_lo)
        mem_loaded, consts_loaded, router_loaded = sem("mem_loaded"), sem("consts_loaded"), sem("router_loaded")
        const_step, consts_made, zeros_made = sem("const_step"), sem("consts_made"), sem("zeros_made")
        squares, var_done, root_done, chain_sem, xs_done = (
            sem("su_squares"), sem("su_var"), sem("su_root"), sem("su_chain"), sem("su_xs"))
        filled, hi_done, lo_done, router_hi = sem("su_filled"), sem("su_hi"), sem("su_lo"), sem("su_router_hi")
        memx = h[:, 0:MB * D].rearrange("p (t d) -> p t d", t=MB)
        mxs = xs[:, 0:MB * D].rearrange("p (t d) -> p t d", t=MB)
        kv = w_kv[0].rearrange("(k p) n -> p k n", p=P)
        SOURCES = [(half, kh) for half in range(4) for kh in range(2)]

        with nc.Block() as block:
            @block.sync
            def _(sp):
                sp.dma_start(memx, mem[0].rearrange("(t p) d -> p t d", p=P)).then_inc(mem_loaded, STEP)
                for g, (half, kh) in enumerate(SOURCES):
                    strips.load(sp, g, g % 2, kv[:, 4 * kh:4 * kh + 4, T * half:T * half + T], 4)

            @block.gpsimd
            def _(pool):
                strips.open(pool=pool)
                pool.memset(ones[:, :], 1.0).then_inc(const_step, 1)
                pool.memset(ident[:, :], 0.0).then_inc(const_step, 1)
                pool.wait_ge(const_step, 2)
                pool.affine_select(out=ident[:, :], in_=ident[:, :], compare_op=ALU.not_equal, fill=1.0, base=0,
                                   pattern=[[-1, P]], channel_multiplier=1).then_inc(consts_made, 1)
                pool.affine_select(out=upper[:, :], in_=ones[:, :], compare_op=ALU.is_ge, fill=0.0, base=-1,
                                   pattern=[[1, P]], channel_multiplier=-1).then_inc(consts_made, 1)
                pool.iota(ints[:, :], pattern=[[-1, P]], base=P, channel_multiplier=1).then_inc(consts_made, 1)
                pool.iota(ints2[:, :], pattern=[[-16, 8], [0, 16]], base=P, channel_multiplier=1).then_inc(
                    consts_made, 1)
                pool.iota(ramp[:, :], pattern=[[1, E]], base=0, channel_multiplier=0,
                          allow_small_or_imprecise_dtypes=True).then_inc(consts_made, 1)
                pool.iota(token_id[:, :], pattern=[[P, SEQ // P]], base=0, channel_multiplier=1,
                          allow_small_or_imprecise_dtypes=True).then_inc(consts_made, 1)
                for g in range(len(SOURCES)):
                    strips.split_lo_pool(pool, g, g % 2)

            @block.scalar
            def _(act):
                for n, gain in enumerate((norm_mix, norm_xattn, norm_mem)):
                    act.dma_start(gains[:, n, :], gain[0].rearrange("(k p) -> p k", p=P),
                                  allow_slow_non_contiguous=True).then_inc(consts_loaded, STEP)
                for n in range(3):
                    act.dma_start(taps[:, n, :], conv_w[0, n].rearrange("(k p) -> p k", p=P),
                                  allow_slow_non_contiguous=True).then_inc(consts_loaded, STEP)
                act.dma_start(gain_row[:, :], norm_ffn[0:1, :].to_broadcast([P, D])).then_inc(consts_loaded, STEP)
                act.dma_start(r_raw[:, :, :], router[0].rearrange("(k p) e -> p k e", p=P)).then_inc(
                    router_loaded, STEP)
                act.wait_ge(mem_loaded, STEP)
                for t in range(MB):
                    act.activation(junk[:, t, :], memx[:, t, :], ACT.Square, accum_out=ss[:, t:t + 1]).then_inc(squares, 1)
                act.wait_ge(var_done, 1)
                act.activation(root[:, 0:MB], var[:, 0:MB], ACT.Sqrt).then_inc(root_done, 1)
                act.wait_ge(router_loaded, STEP)
                act.activation(r_hi[:, :, :], r_raw[:, :, :], ACT.Copy).then_inc(router_hi, 1)
                strips.split_hi(act, 0, 0, 1)
                strips.split_hi(act, 1, 1, 1)
                act.wait_ge(consts_loaded, 7 * STEP)
                for k in range(KB):
                    act.wait_ge(filled, 1 + k // 4)
                    act.activation(act_hi[:, k, 0:MEM], bank(k // 4, k % 4)[:, 0:MEM], ACT.Copy,
                                   scale=gains[:, 2, k:k + 1]).then_inc(hi_done, 1)
                for half in range(4):
                    if half < 3:
                        strips.split_hi(act, 2 * half + 2, 0, half + 2)
                        strips.split_hi(act, 2 * half + 3, 1, half + 2)
                    strips.done(act, 2 * half + 1)
                    if half < 2:
                        act.activation(k_hi[:, 4 * half:4 * half + 4, :], bank(half % 2)[:, :, 0:MEM],
                                       ACT.Copy).then_inc(hi_done, 1)
                    else:
                        act.activation(v_hi[:, :, T * (half - 2):T * (half - 1)], bank(half % 2)[:, 0:MB, :],
                                       ACT.Copy).then_inc(hi_done, 1)

            @block.vector
            def _(dve):
                strips.open(dve=dve)
                chain = Chain(dve, chain_sem)
                dve.wait_ge(squares, MB)
                dve.tensor_scalar(var[:, 0:MB], ss[:, 0:MB], 1.0 / D, RMS_EPS, ALU.mult, ALU.add).then_inc(var_done, 1)
                dve.wait_ge(root_done, 1)
                refine_rstd(dve, chain, MB)
                for t in range(MB):
                    dve.tensor_scalar(mxs[:, t, :], memx[:, t, :], rstd[:, t:t + 1], None, ALU.mult).then_inc(xs_done, 1)
                dve.wait_ge(router_hi, 1)
                chain(dve.tensor_tensor(r_lo[:, :, :], r_raw[:, :, :], r_hi[:, :, :].bitcast(F32), ALU.subtract))
                dve.wait_ge(consts_made, 6)
                chain(dve.tensor_scalar(ints[:, :], ints[:, :], 15, None, ALU.bitwise_and))
                chain(dve.tensor_scalar(same_expert[:, :], ints[:, :], 0.0, None, ALU.is_equal))
                chain(dve.tensor_scalar(ints2[:, :], ints2[:, :], 4, None, ALU.logical_shift_right))
                chain(dve.tensor_scalar(own_block[:, :], ints2[:, :], 8.0, None, ALU.is_equal))
                strips.split_lo(dve, 0, 0)
                strips.split_lo(dve, 1, 1)
                for k in range(KB):
                    dve.wait_ge(hi_done, k + 1)
                    dve.scalar_tensor_tensor(act_lo[:, k, 0:MEM], bank(k // 4, k % 4)[:, 0:MEM],
                                             gains[:, 2, k:k + 1], act_hi[:, k, 0:MEM].bitcast(F32),
                                             ALU.mult, ALU.subtract).then_inc(lo_done, 1)
                for half in range(4):
                    if half < 3:
                        strips.split_lo(dve, 2 * half + 2, 0)
                        strips.split_lo(dve, 2 * half + 3, 1)
                    dve.wait_ge(hi_done, KB + half + 1)
                    if half < 2:
                        b = slice(4 * half, 4 * half + 4)
                        dve.tensor_tensor(k_lo[:, b, :], bank(half % 2)[:, :, 0:MEM], k_hi[:, b, :].bitcast(F32),
                                          ALU.subtract).then_inc(lo_done, 1)
                    else:
                        c = slice(T * (half - 2), T * (half - 1))
                        dve.tensor_tensor(v_lo[:, :, c], bank(half % 2)[:, 0:MB, :], v_hi[:, :, c].bitcast(F32),
                                          ALU.subtract).then_inc(lo_done, 1)

            @block.tensor
            def _(pe):
                strips.open(pe=pe)
                pe.wait_ge(consts_made, 1)
                pe.wait_ge(xs_done, MB)
                for k in range(KB):
                    for t in range(MB):
                        last = pe.transpose(bank(k // 4, k % 4)[:, t * P:(t + 1) * P], mxs[:, t, k * P:(k + 1) * P],
                                            ident[:, :])
                    if k % 4 == 3:
                        last.then_inc(filled, 1)
                for half in range(4):
                    pe.wait_ge(lo_done, (4, KB, KB + 1, KB + 2)[half])
                    for kh in range(2):
                        g = 2 * half + kh
                        strips.ready(pe, g)
                        pe.wait_ge(lo_done, max(4 * kh + 4, 4 + 4 * min(half, 1)))
                        hi, lo = strips.views(g % 2, 4)
                        for m in range(4 if half < 2 else MB):
                            for k in range(4):
                                kk = 4 * kh + k
                                if half < 2:
                                    f = slice(m * P, (m + 1) * P)
                                    last = product(pe, bank(half % 2, m)[:, 0:MEM], (hi[:, k, f], lo[:, k, f]),
                                                   (act_hi[:, kk, 0:MEM], act_lo[:, kk, 0:MEM]), kk == 0, kk == KB - 1)
                                else:
                                    t = slice(m * P, (m + 1) * P)
                                    last = product(pe, bank(half % 2, m), (act_hi[:, kk, t], act_lo[:, kk, t]),
                                                   (hi[:, k, :], lo[:, k, :]), kk == 0, kk == KB - 1)
                        last.then_inc(strips.used, 1)
        pctx.close()

    def conv():
        pctx = ExitStack()
        sem = lambda name: pctx.enter_context(nc.semaphore(name))
        strips = Strips(nc, pctx, "conv", w_raw, w_hi, w_lo)
        NS = 12
        x_loaded, x_free = sem("x_loaded"), sem("x_free")
        squares, var_done, root_done, chain_sem, xs_done = (
            sem("cv_squares"), sem("cv_var"), sem("cv_root"), sem("cv_chain"), sem("cv_xs"))
        transposed, xn_hi, xn_lo = sem("cv_transposed"), sem("xn_hi"), sem("xn_lo")
        c_read, u_done, v_done, v_free, v_stored = (
            sem("c_read"), sem("u_done"), sem("v_done"), sem("v_free"), sem("v_stored"))
        xt = h[:, :].rearrange("p (t d) -> p t d", t=TB)
        xn = xs[:, :].rearrange("p (t d) -> p t d", t=TB)
        u = xs[:, 0:4 * (T + 2)].rearrange("p (m c) -> p m c", m=4)
        cgate = vin[:, 0:4 * T].rearrange("p (m c) -> p m c", m=4)
        cv = vin[:, 4 * T:].rearrange("p (m c) -> p m c", m=4)
        u_carry = stat[:, 24:40].rearrange("p (m c) -> p m c", c=2)
        b_carry = stat[:, 40:48]
        last_v = stat[:, 48:56]
        last_t = stat[:, 56:64]
        w_in = conv_w_in[0].rearrange("(k p) n -> p k n", p=P)
        x_v = x[0].rearrange("(i t p) d -> p i t d", p=P, t=TB)
        v_v = v_d.rearrange("(m p) c -> p m c", p=P)
        COLUMNS = [part * D + half * T for half in range(2) for part in (1, 2, 0)]

        with nc.Block() as block:
            @block.sync
            def _(sp):
                with sp.Fori(0, TILES) as i:
                    sp.wait_ge(x_free, i + 1)
                    sp.dma_start(xt, x_v[:, bass.ds(i, 1), :, :].rearrange("p i t d -> p (i t) d")).then_inc(
                        x_loaded, STEP)
                    for s in range(NS):
                        c, kh = COLUMNS[s // 2], s % 2
                        strips.load(sp, i * NS + s, s % 2, w_in[:, 4 * kh:4 * kh + 4, c:c + T], 4)

            @block.gpsimd
            def _(pool):
                strips.open(pool=pool)
                pool.sem_inc(v_free, 1)
                with pool.Fori(0, TILES) as i:
                    for half in range(2):
                        for s in range(6 * half, 6 * half + 6):
                            strips.split_lo_pool(pool, i * NS + s, s % 2)
                        pool.wait_ge(v_done, i * 2 + half + 2)
                        apart(pool, spare)
                        pool.dma_start(v_v[:, 4 * half:4 * half + 4, bass.ds(i * T, T)], cv).then_inc(v_stored, STEP)
                        pool.wait_ge(v_stored, i * 2 * STEP + (half + 1) * STEP)
                        pool.sem_inc(v_free, 1)
                pool.wait_ge(v_done, 2 * TILES + 2)
                pool.dma_start(v_v[:, :, SEQ:SEQ + 1], last_v.rearrange("p (m o) -> p m o", o=1),
                               allow_slow_non_contiguous=True).then_inc(v_stored, STEP)
                pool.wait_ge(v_stored, (2 * TILES + 1) * STEP)

            @block.scalar
            def _(act):
                with act.Fori(0, TILES) as i:
                    def split(s):
                        strips.split_hi(act, i * NS + s, s % 2, i * (NS // 2) + s // 2 + 1)

                    act.wait_ge(x_loaded, i * STEP + STEP)
                    for t in range(TB):
                        act.activation(junk[:, t, :], xt[:, t, :], ACT.Square, accum_out=ss[:, t:t + 1]).then_inc(squares, 1)
                    split(0)
                    act.wait_ge(var_done, i + 1)
                    act.activation(root, var, ACT.Sqrt).then_inc(root_done, 1)
                    split(1)
                    strips.done(act, i * NS - 1)
                    for k in range(KB):
                        act.wait_ge(transposed, i * 2 + 1 + k // 4)
                        act.activation(act_hi[:, k, :], bank(k // 4, k % 4), ACT.Copy,
                                       scale=gains[:, 0, k:k + 1]).then_inc(xn_hi, 1)
                    for f in range(6):
                        if f < 5:
                            split(2 * f + 2)
                            split(2 * f + 3)
                        if f % 3 == 0:
                            half = f // 3
                            strips.done(act, i * NS + 2 * f + 1)
                            act.wait_ge(u_done, i * 2 + half + 1)
                            act.activation(cgate, bank(f % 2), ACT.Copy).then_inc(c_read, 1)

            @block.vector
            def _(dve):
                strips.open(dve=dve)
                PER = 5 + 2 * 5
                dve.memset(stat[:, 24:64], 0.0).then_inc(chain_sem, 1)
                dve.wait_ge(chain_sem, 1)
                dve.sem_inc(u_done, 1)
                dve.sem_inc(v_done, 1)
                dve.sem_inc(x_free, 1)
                with dve.Fori(0, TILES) as i:
                    chain = Chain(dve, chain_sem, i * PER + 1)
                    strips.split_lo(dve, i * NS, 0)
                    dve.wait_ge(squares, i * TB + TB)
                    dve.tensor_scalar(var, ss, 1.0 / D, RMS_EPS, ALU.mult, ALU.add).then_inc(var_done, 1)
                    strips.split_lo(dve, i * NS + 1, 1)
                    dve.wait_ge(root_done, i + 1)
                    refine_rstd(dve, chain, TB)
                    for t in range(TB):
                        ins = dve.tensor_scalar(xn[:, t, :], xt[:, t, :], rstd[:, t:t + 1], None, ALU.mult)
                        ins.then_inc(xs_done, 1)
                    dve.wait_ge(xs_done, i * TB + TB)
                    dve.sem_inc(x_free, 1)
                    for k in range(KB):
                        dve.wait_ge(xn_hi, i * KB + k + 1)
                        dve.scalar_tensor_tensor(act_lo[:, k, :], bank(k // 4, k % 4), gains[:, 0, k:k + 1],
                                                 act_hi[:, k, :].bitcast(F32), ALU.mult, ALU.subtract).then_inc(xn_lo, 1)
                    for half in range(2):
                        mb = slice(4 * half, 4 * half + 4)
                        f = 3 * half
                        strips.split_lo(dve, i * NS + 2 * f + 2, 0)
                        strips.split_lo(dve, i * NS + 2 * f + 3, 1)
                        dve.tensor_copy(u[:, :, 0:2], u_carry[:, mb, :])
                        strips.split_lo(dve, i * NS + 2 * f + 4, 0)
                        strips.split_lo(dve, i * NS + 2 * f + 5, 1)
                        strips.done(dve, i * NS + 2 * f + 3)
                        dve.wait_ge(c_read, i * 2 + half + 1)
                        dve.tensor_tensor(u[:, :, 2:T + 2], bank((f + 1) % 2), cgate, ALU.mult).then_inc(u_done, 1)
                        dve.wait_ge(u_done, i * 2 + half + 2)
                        dve.wait_ge(v_free, i * 2 + half + 1)
                        for m in range(4):
                            ins = dve.tensor_scalar(cv[:, m, :], u[:, m, 0:T], taps[:, 0, 4 * half + m:4 * half + m + 1],
                                                    None, ALU.mult)
                        chain(ins)
                        for tap in (1, 2):
                            for m in range(4):
                                ins = dve.scalar_tensor_tensor(cv[:, m, :], u[:, m, tap:T + tap],
                                                               taps[:, tap, 4 * half + m:4 * half + m + 1], cv[:, m, :],
                                                               ALU.mult, ALU.add)
                            chain(ins)
                        if half == 0:
                            strips.split_lo(dve, i * NS + 2 * f + 6, 0)
                            strips.split_lo(dve, i * NS + 2 * f + 7, 1)
                        dve.tensor_copy(u_carry[:, mb, :], u[:, :, T:T + 2])
                        chain(dve.tensor_tensor(cv[:, :, 0], cv[:, :, 0], b_carry[:, mb], ALU.mult))
                        strips.done(dve, i * NS + 2 * f + 5)
                        dve.tensor_tensor(cv[:, :, 1:T], cv[:, :, 1:T], bank(f % 2)[:, :, 0:T - 1], ALU.mult)
                        chain(dve.tensor_copy(b_carry[:, mb], bank(f % 2)[:, :, T - 1]))
                        dve.sem_inc(v_done, 1)
                    assert chain.n == PER, chain.n
                chain = Chain(dve, chain_sem, TILES * PER + 1)
                chain(dve.tensor_tensor(last_v, u_carry[:, :, 0], taps[:, 0, :], ALU.mult))
                chain(dve.tensor_tensor(last_t, u_carry[:, :, 1], taps[:, 1, :], ALU.mult))
                chain(dve.tensor_tensor(last_v, last_v, last_t, ALU.add))
                dve.tensor_tensor(last_v, last_v, b_carry, ALU.mult).then_inc(v_done, 1)

            @block.tensor
            def _(pe):
                strips.open(pe=pe)
                with pe.Fori(0, TILES) as i:
                    pe.wait_ge(xs_done, i * TB + TB)
                    pe.wait_ge(u_done, i * 2 + 1)
                    for k in range(KB):
                        if k == 4:
                            pe.wait_ge(v_done, i * 2 + 1)
                        for t in range(TB):
                            last = pe.transpose(bank(k // 4, k % 4)[:, t * P:(t + 1) * P],
                                                xn[:, t, k * P:(k + 1) * P], ident[:, :])
                        if k % 4 == 3:
                            last.then_inc(transposed, 1)
                    for f in range(6):
                        half, part = f // 3, f % 3
                        if f < 2:
                            pe.wait_ge(xn_lo, i * KB + 4 * f + 4)
                        elif part == 2:
                            pe.wait_ge(c_read, i * 2 + half + 1)
                        elif part == 0:
                            pe.wait_ge(u_done, i * 2 + 2)
                        else:
                            pe.wait_ge(v_done, i * 2 + 2)
                        for kh in range(2):
                            s = 2 * f + kh
                            strips.ready(pe, i * NS + s)
                            if f == 0:
                                pe.wait_ge(xn_lo, i * KB + 4 * kh + 4)
                            hi, lo = strips.views(s % 2, 4)
                            for m in range(4):
                                c = slice(m * P, (m + 1) * P)
                                for k in range(4):
                                    kk = 4 * kh + k
                                    last = product(pe, bank(f % 2, m), (hi[:, k, c], lo[:, k, c]),
                                                   (act_hi[:, kk, :], act_lo[:, kk, :]), kk == 0, kk == KB - 1)
                            last.then_inc(strips.used, 1)
        pctx.close()

    def attend():
        pctx = ExitStack()
        sem = lambda name: pctx.enter_context(nc.semaphore(name))
        strips = Strips(nc, pctx, "attend", w_raw, w_hi, w_lo)
        NS = 12
        x_loaded, v_loaded, v_free, stored = sem("at_x_loaded"), sem("at_v_loaded"), sem("at_v_free"), sem("at_stored")
        squares, var_done, root_done, chain_sem, xs_done = (
            sem("at_squares"), sem("at_var"), sem("at_root"), sem("at_chain"), sem("at_xs"))
        v_hi_done, v_lo_done = sem("at_v_hi"), sem("at_v_lo")
        n1_hi, n1_lo, qh, ql = sem("n1_hi"), sem("n1_lo"), sem("q_hi_done"), sem("q_lo_done")
        pt_hi, pt_lo, o_hi, o_lo, n3_hi, n3_lo = (
            sem("pt_hi"), sem("pt_lo"), sem("o_hi"), sem("o_lo"), sem("n3_hi"), sem("n3_lo"))
        added, h_done = sem("at_added"), sem("at_h_done")
        turned, scored, maxed, exped, p_done = (
            sem("turned"), sem("scored"), sem("maxed"), sem("exped"), sem("p_done"))
        valued, routed, shifted, r_exp, probs_done = (
            sem("valued"), sem("routed"), sem("shifted"), sem("r_exp"), sem("probs_done"))
        xt = h[:, :].rearrange("p (t d) -> p t d", t=TB)
        xn = xs[:, :].rearrange("p (t d) -> p t d", t=TB)
        vt = vin[:, :].rearrange("p (k c) -> p k c", k=KB)
        pr = xs[:, :].rearrange("p (h t m) -> p h t m", h=HEADS, t=TB)
        neg_max = stat[:, 24:40].rearrange("p (h t) -> p h t", h=HEADS)
        sums = stat[:, 40:56].rearrange("p (h t) -> p h t", h=HEADS)
        r_max = stat[:, 56:60]
        r_sum = stat[:, 60:64]
        r_tmp = r_buf[:, :]
        x_v = x[0].rearrange("(i t p) d -> p i t d", p=P, t=TB)
        v_v = v_d.rearrange("(k p) c -> p k c", p=P)
        sum_v = sum_d.rearrange("(i t p) d -> p i t d", p=P, t=TB)
        row_v = row_d.rearrange("(i t p) d -> p i t d", p=P, t=TB)
        w_co = conv_w_out[0].rearrange("(k p) n -> p k n", p=P)
        w_qv = w_q[0].rearrange("(k p) n -> p k n", p=P)
        w_ov = w_o[0].rearrange("(k p) n -> p k n", p=P)

        def scores_bank(head):
            return bank(head // 2)[:, 2 * (head % 2):2 * (head % 2) + 2, :].rearrange("p b (t m) -> p (b t) m", m=MEM)

        with nc.Block() as block:
            @block.sync
            def _(sp):
                with sp.Fori(0, TILES) as i:
                    sp.wait_ge(v_free, i + 1)
                    sp.dma_start(vt, v_v[:, :, bass.ds(i * T + 1, T)]).then_inc(v_loaded, STEP)
                    for s in range(NS):
                        w = (w_co, w_qv, w_ov)[s // 4]
                        half, kh = s // 2 % 2, s % 2
                        strips.load(sp, i * NS + s, s % 2, w[:, 4 * kh:4 * kh + 4, T * half:T * half + T], 4)

            @block.gpsimd
            def _(pool):
                strips.open(pool=pool)
                with pool.Fori(0, TILES) as i:
                    tile = bass.ds(i, 1)
                    pool.dma_start(xt, x_v[:, tile, :, :].rearrange("p i t d -> p (i t) d")).then_inc(x_loaded, STEP)
                    for s in range(NS):
                        strips.split_lo_pool(pool, i * NS + s, s % 2)
                    pool.wait_ge(h_done, i * 2 + 2)
                    apart(pool, spare)
                    pool.dma_start(sum_v[:, tile, :, :].rearrange("p i t d -> p (i t) d"), xt).then_inc(stored, STEP)
                    pool.wait_ge(xs_done, i * 2 * TB + 2 * TB)
                    apart(pool, spare)
                    pool.dma_start(row_v[:, tile, :, 0:D].rearrange("p i t d -> p (i t) d"), xn).then_inc(stored, STEP)
                    pool.wait_ge(probs_done, i + 1)
                    apart(pool, spare)
                    pool.dma_start(row_v[:, tile, :, D:ROW].rearrange("p i t e -> p (i t) e"),
                                   r_tmp.rearrange("p (t e) -> p t e", t=TB)).then_inc(stored, STEP)
                    pool.wait_ge(stored, i * 3 * STEP + 3 * STEP)

            @block.scalar
            def _(act):
                with act.Fori(0, TILES) as i:
                    def split(s):
                        strips.split_hi(act, i * NS + s, s % 2, i * (NS // 2) + s // 2 + 1)

                    def stats(n):
                        act.wait_ge(h_done, i * 2 + n + 1)
                        for t in range(TB):
                            act.activation(junk[:, t, :], xt[:, t, :], ACT.Square,
                                           accum_out=ss[:, t:t + 1]).then_inc(squares, 1)
                        act.wait_ge(var_done, i * 2 + n + 1)
                        act.activation(root, var, ACT.Sqrt).then_inc(root_done, 1)

                    split(0)
                    split(1)
                    act.wait_ge(v_loaded, i * STEP + STEP)
                    act.wait_ge(routed, i + 1)
                    for k in range(KB):
                        act.activation(act_hi[:, k, :], vt[:, k, :], ACT.Copy).then_inc(v_hi_done, 1)
                    for s in (2, 3, 4, 5):
                        split(s)
                    stats(0)
                    for k in range(KB):
                        act.wait_ge(turned, i * 6 + 1 + k // 4)
                        act.activation(act_hi[:, k, :], bank(k // 4, k % 4), ACT.Copy,
                                       scale=gains[:, 1, k:k + 1]).then_inc(n1_hi, 1)
                    for half in range(2):
                        split(6 + 2 * half)
                        split(7 + 2 * half)
                        strips.done(act, i * NS + 5 + 2 * half)
                        for m in range(4):
                            act.activation(q_hi[:, 4 * half + m, :], bank(half, m), ACT.Copy,
                                           scale=HD ** -0.5).then_inc(qh, 1)
                    for hd in range(HEADS):
                        act.wait_ge(maxed, i * HEADS + hd + 1)
                        for t in range(TB):
                            act.activation(pr[:, hd, t, :], scores_bank(hd)[:, t, :], ACT.Exp,
                                           bias=neg_max[:, hd, t:t + 1], accum_out=sums[:, hd, t:t + 1]).then_inc(exped, 1)
                    for n in range(KB):
                        act.wait_ge(turned, i * 6 + 3 + n // 4)
                        act.activation(q_hi[:, n, :], bank(n // 4, n % 4), ACT.Copy).then_inc(pt_hi, 1)
                    for n in range(KB):
                        act.wait_ge(valued, i * 2 + 1 + n // 4)
                        act.activation(act_hi[:, n, :], bank(n // 4, n % 4), ACT.Copy).then_inc(o_hi, 1)
                    split(10)
                    split(11)
                    stats(1)
                    for k in range(KB):
                        act.wait_ge(turned, i * 6 + 5 + k // 4)
                        act.activation(act_hi[:, k, :], bank(k // 4, k % 4), ACT.Copy).then_inc(n3_hi, 1)
                    act.wait_ge(shifted, i + 2)
                    act.activation(r_tmp, r_tmp, ACT.Exp).then_inc(r_exp, 1)

            @block.vector
            def _(dve):
                strips.open(dve=dve)
                PER = 5 + 5 + HEADS + 5
                dve.sem_inc(v_free, 1)
                dve.sem_inc(added, 1)
                dve.sem_inc(shifted, 1)
                with dve.Fori(0, TILES) as i:
                    chain = Chain(dve, chain_sem, i * PER)

                    def split(s):
                        strips.split_lo(dve, i * NS + s, s % 2)

                    def rms(n):
                        dve.wait_ge(squares, i * 2 * TB + n * TB + TB)
                        dve.tensor_scalar(var, ss, 1.0 / D, RMS_EPS, ALU.mult, ALU.add).then_inc(var_done, 1)
                        dve.wait_ge(root_done, i * 2 + n + 1)
                        refine_rstd(dve, chain, TB)

                    def add_half(half):
                        c = slice(T * half, T * half + T)
                        return dve.tensor_tensor(xt[:, :, c], bank(half), xt[:, :, c], ALU.add)

                    split(0)
                    split(1)
                    for k in range(KB):
                        dve.wait_ge(v_hi_done, i * KB + k + 1)
                        dve.tensor_tensor(act_lo[:, k, :], vt[:, k, :], act_hi[:, k, :].bitcast(F32),
                                          ALU.subtract).then_inc(v_lo_done, 1)
                    split(2)
                    split(3)
                    dve.wait_ge(v_lo_done, i * KB + KB)
                    dve.sem_inc(v_free, 1)
                    dve.wait_ge(x_loaded, i * STEP + STEP)
                    strips.done(dve, i * NS + 1)
                    add_half(0).then_inc(added, 1)
                    split(4)
                    split(5)
                    strips.done(dve, i * NS + 3)
                    add_half(1).then_inc(added, 1)
                    dve.wait_ge(added, i * 4 + 3)
                    dve.sem_inc(h_done, 1)
                    rms(0)
                    for t in range(TB):
                        dve.tensor_scalar(xn[:, t, :], xt[:, t, :], rstd[:, t:t + 1], None, ALU.mult).then_inc(xs_done, 1)
                    for k in range(KB):
                        dve.wait_ge(n1_hi, i * KB + k + 1)
                        dve.scalar_tensor_tensor(act_lo[:, k, :], bank(k // 4, k % 4), gains[:, 1, k:k + 1],
                                                 act_hi[:, k, :].bitcast(F32), ALU.mult, ALU.subtract).then_inc(n1_lo, 1)
                    for half in range(2):
                        split(6 + 2 * half)
                        split(7 + 2 * half)
                        for m in range(4):
                            dve.wait_ge(qh, i * KB + 4 * half + m + 1)
                            dve.scalar_tensor_tensor(q_lo[:, 4 * half + m, :], bank(half, m), HD ** -0.5,
                                                     q_hi[:, 4 * half + m, :].bitcast(F32), ALU.mult,
                                                     ALU.subtract).then_inc(ql, 1)
                    for hd in range(HEADS):
                        dve.wait_ge(scored, i * HEADS + hd + 1)
                        dve.tensor_reduce(neg_max[:, hd, :], scores_bank(hd), axis=X, op=ALU.max,
                                          negate=True).then_inc(maxed, 1)
                    for hd in range(HEADS):
                        dve.wait_ge(exped, i * HEADS * TB + hd * TB + TB)
                        chain(dve.reciprocal(sums[:, hd, :], sums[:, hd, :]))
                        dve.tensor_tensor(pr[:, hd, :, :], pr[:, hd, :, :],
                                          sums[:, hd, :].unsqueeze(2).to_broadcast([P, TB, MEM]),
                                          ALU.mult).then_inc(p_done, 1)
                    for n in range(KB):
                        dve.wait_ge(pt_hi, i * KB + n + 1)
                        dve.tensor_tensor(q_lo[:, n, :], bank(n // 4, n % 4), q_hi[:, n, :].bitcast(F32),
                                          ALU.subtract).then_inc(pt_lo, 1)
                    for n in range(KB):
                        dve.wait_ge(o_hi, i * KB + n + 1)
                        dve.tensor_tensor(act_lo[:, n, :], bank(n // 4, n % 4), act_hi[:, n, :].bitcast(F32),
                                          ALU.subtract).then_inc(o_lo, 1)
                    split(10)
                    split(11)
                    strips.done(dve, i * NS + 9)
                    add_half(0).then_inc(added, 1)
                    strips.done(dve, i * NS + 11)
                    add_half(1).then_inc(added, 1)
                    dve.wait_ge(added, i * 4 + 5)
                    dve.sem_inc(h_done, 1)
                    rms(1)
                    for t in range(TB):
                        dve.scalar_tensor_tensor(xn[:, t, :], xt[:, t, :], rstd[:, t:t + 1], gain_row[:, :],
                                                 ALU.mult, ALU.mult).then_inc(xs_done, 1)
                    for k in range(KB):
                        dve.wait_ge(n3_hi, i * KB + k + 1)
                        dve.tensor_tensor(act_lo[:, k, :], bank(k // 4, k % 4), act_hi[:, k, :].bitcast(F32),
                                          ALU.subtract).then_inc(n3_lo, 1)
                    dve.wait_ge(routed, i + 2)
                    logits = bank(0, 0)[:, 0:TB * E].rearrange("p (t e) -> p t e", t=TB)
                    rt = r_tmp.rearrange("p (t e) -> p t e", t=TB)
                    chain(dve.tensor_reduce(r_max, logits, axis=X, op=ALU.max))
                    dve.tensor_tensor(rt, logits, r_max.unsqueeze(2).to_broadcast([P, TB, E]),
                                      ALU.subtract).then_inc(shifted, 1)
                    dve.wait_ge(r_exp, i + 1)
                    chain(dve.tensor_reduce(r_sum, rt, axis=X, op=ALU.add))
                    chain(dve.reciprocal(r_sum, r_sum))
                    chain(dve.tensor_tensor(rt, rt, r_sum.unsqueeze(2).to_broadcast([P, TB, E]), ALU.mult))
                    chain(dve.tensor_copy(probs[:, bass.ds(i * TB * E, TB * E)], r_tmp))
                    dve.sem_inc(probs_done, 1)
                    assert chain.n == PER, chain.n

            @block.tensor
            def _(pe):
                strips.open(pe=pe)
                pe.sem_inc(routed, 1)
                with pe.Fori(0, TILES) as i:
                    def turn_rows(n, data_ready):
                        for k in range(KB):
                            data_ready(k)
                            for t in range(TB):
                                last = pe.transpose(bank(k // 4, k % 4)[:, t * P:(t + 1) * P],
                                                    xn[:, t, k * P:(k + 1) * P], ident[:, :])
                            if k % 4 == 3:
                                last.then_inc(turned, 1)

                    def rows_out(first_strip, lo_sem, half):
                        for kh in range(2):
                            s = first_strip + kh
                            strips.ready(pe, i * NS + s)
                            hi, lo = strips.views(s % 2, 4)
                            for t in range(TB):
                                c = slice(t * P, (t + 1) * P)
                                for k in range(4):
                                    kk = 4 * kh + k
                                    if half == 0 and t == 0:
                                        pe.wait_ge(lo_sem, i * KB + kk + 1)
                                    last = product(pe, bank(half, t), (act_hi[:, kk, c], act_lo[:, kk, c]),
                                                   (hi[:, k, :], lo[:, k, :]), kk == 0, kk == KB - 1)
                            last.then_inc(strips.used, 1)

                    pe.wait_ge(shifted, i + 1)
                    rows_out(0, v_lo_done, 0)
                    rows_out(2, v_lo_done, 1)

                    def after_conv(k):
                        if k == 0:
                            pe.wait_ge(xs_done, i * 2 * TB + TB)
                    turn_rows(0, after_conv)
                    for half in range(2):
                        pe.wait_ge(n1_lo, i * KB + 4 * half + 4)
                        for kh in range(2):
                            s = 4 + 2 * half + kh
                            strips.ready(pe, i * NS + s)
                            pe.wait_ge(n1_lo, i * KB + max(4 * kh, 4 * half) + 4)
                            hi, lo = strips.views(s % 2, 4)
                            for m in range(4):
                                c = slice(m * P, (m + 1) * P)
                                for k in range(4):
                                    kk = 4 * kh + k
                                    last = product(pe, bank(half, m), (hi[:, k, c], lo[:, k, c]),
                                                   (act_hi[:, kk, :], act_lo[:, kk, :]), kk == 0, kk == KB - 1)
                            last.then_inc(strips.used, 1)
                    for hd in range(HEADS):
                        if hd % 2 == 0:
                            pe.wait_ge(ql, i * KB + 4 * (hd // 2) + 4)
                        sc = scores_bank(hd)
                        for t in range(TB):
                            c = slice(t * P, (t + 1) * P)
                            for b in range(HB):
                                n = HB * hd + b
                                last = product(pe, sc[:, t, :], (q_hi[:, n, c], q_lo[:, n, c]),
                                               (k_hi[:, n, :], k_lo[:, n, :]), b == 0, b == HB - 1)
                        last.then_inc(scored, 1)
                    for hd in range(HEADS):
                        if hd % 2 == 0:
                            pe.wait_ge(exped, i * HEADS * TB + (hd + 2) * TB)
                        pe.wait_ge(p_done, i * HEADS + hd + 1)
                        for m in range(MB):
                            for t in range(TB):
                                last = pe.transpose(bank(hd // 2, MB * (hd % 2) + m)[:, t * P:(t + 1) * P],
                                                    pr[:, hd, t, m * P:(m + 1) * P], ident[:, :])
                        if hd % 2 == 1:
                            last.then_inc(turned, 1)
                    for hd in range(HEADS):
                        if hd % 2 == 0:
                            pe.wait_ge(pt_lo, i * KB + 4 * (hd // 2) + 4)
                        for b in range(HB):
                            c = slice(hd * HD + b * P, hd * HD + (b + 1) * P)
                            for m in range(MB):
                                n = MB * hd + m
                                last = product(pe, bank(hd // 2, HB * (hd % 2) + b), (v_hi[:, m, c], v_lo[:, m, c]),
                                               (q_hi[:, n, :], q_lo[:, n, :]), m == 0, m == MB - 1)
                        if hd % 2 == 1:
                            last.then_inc(valued, 1)
                    pe.wait_ge(o_lo, i * KB + 4)
                    rows_out(8, o_lo, 0)
                    rows_out(10, o_lo, 1)

                    def after_output(k):
                        if k == 0:
                            pe.wait_ge(xs_done, i * 2 * TB + 2 * TB)
                    turn_rows(1, after_output)
                    pe.wait_ge(n3_lo, i * KB + KB)
                    for t in range(TB):
                        c = slice(t * P, (t + 1) * P)
                        for k in range(KB):
                            last = product(pe, bank(0, 0)[:, t * E:(t + 1) * E], (act_hi[:, k, c], act_lo[:, k, c]),
                                           (r_hi[:, k, :], r_lo[:, k, :]), k == 0, k == KB - 1)
                    last.then_inc(routed, 1)
        pctx.close()

    def select():
        pctx = ExitStack()
        sem = lambda name: pctx.enter_context(nc.semaphore(name))
        BITS = 30
        NT = SEQ // P
        BIG = 4096.0
        turned, counted, totalled, bit_step, chain_sem = (
            sem("sl_turned"), sem("counted"), sem("totalled"), sem("bit_step"), sem("sl_chain"))
        spread_in, spread, masks_done, prefixed, hots_done, listed = (
            sem("spread_in"), sem("spread"), sem("masks_done"), sem("prefixed"), sem("hots_done"), sem("listed"))
        z_done, z_stored, z_loaded, z_turned = sem("z_done"), sem("z_stored"), sem("z_loaded"), sem("z_turned")
        by_expert = vin[:, 0:256]
        compared = vin[:, 256:512]
        count = stat[:, 24:25]
        words = ints[:, 0:4].bitcast(U32)
        thr, cand, bit, take = (words[:, n:n + 1] for n in range(4))
        spread_rhs = vin[:, 512:528]
        thr_row = vin[:, 528:544]
        above_total = vin[:, 544:560]
        masks = vin[:, 1024:1536].rearrange("p (s t e) -> p s t e", s=2, t=NT)
        before = h[:, 0:2 * (NT + 1) * E].rearrange("p (t s e) -> p t s e", t=NT + 1, s=2)
        a1 = vin[:, 1536:1792]
        b1 = vin[:, 1792:2048]
        pos = h[:, 1024:1280].bitcast(I32)
        low = h[:, 1280:1536].bitcast(I32)
        high = h[:, 1536:1792].bitcast(I32)
        hot = xs[:, :].rearrange("p (n b) -> p n b", b=E)
        hot_high = q_hi[:, :, :].rearrange("p k c -> p (k c)")
        hot_low = q_lo[:, :, :].rearrange("p k c -> p (k c)")
        z_all = vin[:, 2048:2304].rearrange("p (h n) -> p h n", h=2)
        z = vin[:, 2304:2336].rearrange("p (h b) -> p h b", h=2)
        lists = h[0:E * CB, 2048:2048 + P]
        flat = index_d.rearrange("e c -> (e c)")
        prefix = bank(0, 1)
        with nc.Block() as block:
            @block.sync
            def _(sp):
                sp.wait_ge(z_done, 1)
                sp.dma_start(flat.rearrange("(h r b) -> r h b", h=2, b=E), z).then_inc(z_stored, STEP)
                sp.wait_ge(z_stored, STEP)
                sp.dma_start(lists, flat.rearrange("(r c) -> r c", c=P)).then_inc(z_loaded, STEP)

            @block.tensor
            def _(pe):
                for n in range(2):
                    last = pe.transpose(bank(0, 0)[:, n * P:(n + 1) * P], probs[:, n * P:(n + 1) * P], ident[:, :])
                last.then_inc(turned, 1)
                with pe.Fori(0, BITS) as b:
                    pe.wait_ge(counted, b + 1)
                    pe.matmul(bank(1, 0)[:, 0:1], same_expert[:, :], count, start=True, stop=True).then_inc(totalled, 1)
                pe.wait_ge(spread_in, 1)
                pe.matmul(bank(1, 1)[:, 0:E], ones[:, :], spread_rhs, start=True, stop=True).then_inc(spread, 1)
                pe.wait_ge(masks_done, 1)
                pe.matmul(prefix, upper[:, :], masks.rearrange("p s t e -> p (s t e)"), start=True, stop=False)
                pe.matmul(prefix.rearrange("p (s t e) -> p s t e", s=2, t=NT)[:, 0, :, :], ones[:, :],
                          before[:, 0:NT, 0, :], start=False, stop=False)
                pe.matmul(prefix.rearrange("p (s t e) -> p s t e", s=2, t=NT)[:, 1, :, :], ones[:, :],
                          before[:, 0:NT, 1, :], start=False, stop=True)
                pe.matmul(bank(1, 2)[:, 0:E], ones[:, :], before[:, NT, 0, :], start=True, stop=True).then_inc(prefixed, 1)
                pe.wait_ge(hots_done, 1)
                for half in range(2):
                    for t in range(NT):
                        c = slice(t * 256 + half * P, t * 256 + half * P + P)
                        c2 = [slice((t * E + 8 * half) * E, (t * E + 8 * half + 8) * E)]
                        last = pe.matmul(bank(0, 2 + half)[:, 0:P], hot_high[:, c2[0]], hot_low[:, c2[0]],
                                         start=t == 0, stop=t == NT - 1)
                last.then_inc(listed, 1)
                pe.wait_ge(z_loaded, STEP)
                pe.transpose(bank(1, 3)[:, 0:E * CB], lists, ident[0:E * CB, 0:E * CB]).then_inc(z_turned, 1)

            @block.vector
            def _(dve):
                chain = Chain(dve, chain_sem)
                chain(dve.memset(words, 0))
                chain(dve.memset(bit, 1 << (BITS - 1)))
                chain(dve.memset(cand, 1 << (BITS - 1)))
                dve.wait_ge(turned, 1)
                chain(dve.tensor_copy(by_expert, bank(0, 0)[:, 0:256]))
                with dve.Fori(0, BITS) as b:
                    dve.tensor_scalar(compared, by_expert, cand.bitcast(F32), None, ALU.is_ge, ALU.add,
                                      accum_out=count).then_inc(counted, 1)
                    dve.tensor_scalar(bit, bit, 1, None, ALU.logical_shift_right).then_inc(bit_step, 1)
                    dve.wait_ge(totalled, b + 1)
                    dve.tensor_scalar(take, bank(1, 0)[:, 0:1], CAP - 0.5, None, ALU.is_ge).then_inc(bit_step, 1)
                    dve.wait_ge(bit_step, b * 4 + 2)
                    apart(dve, spare)
                    dve.copy_predicated(thr, take, cand).then_inc(bit_step, 1)
                    dve.wait_ge(bit_step, b * 4 + 3)
                    dve.tensor_tensor(cand, thr, bit, ALU.bitwise_or).then_inc(bit_step, 1)
                    dve.wait_ge(bit_step, b * 4 + 4)
                dve.tensor_scalar(spread_rhs, ident[:, 0:E], thr.bitcast(F32), None, ALU.mult).then_inc(spread_in, 1)
                chain(dve.memset(before[:, 0, :, :], 0.0))
                dve.wait_ge(spread, 1)
                chain(dve.tensor_copy(thr_row, bank(1, 1)[:, 0:E]))
                by_token = probs[:, :].rearrange("p (t e) -> p t e", e=E)
                row = thr_row.unsqueeze(1).to_broadcast([P, NT, E])
                dve.tensor_tensor(masks[:, 0, :, :], by_token, row, ALU.is_gt)
                chain(dve.tensor_tensor(masks[:, 1, :, :], by_token, row, ALU.is_equal))
                for t in range(NT):
                    chain(dve.tensor_tensor(before[:, t + 1, :, :], before[:, t, :, :], masks[:, :, t, :], ALU.add))
                dve.sem_inc(masks_done, 1)
                dve.wait_ge(prefixed, 1)
                above = masks[:, 0, :, :].rearrange("p t e -> p (t e)")
                equal = masks[:, 1, :, :].rearrange("p t e -> p (t e)")
                chain(dve.tensor_copy(above_total, bank(1, 2)[:, 0:E]))
                dve.scalar_tensor_tensor(a1, prefix[:, 0:256], -BIG, above, ALU.add, ALU.mult)
                chain(dve.tensor_tensor(b1.rearrange("p (t e) -> p t e", e=E),
                                        prefix[:, 256:512].rearrange("p (t e) -> p t e", e=E),
                                        above_total.unsqueeze(1).to_broadcast([P, NT, E]), ALU.add))
                chain(dve.scalar_tensor_tensor(b1, b1, -BIG, equal, ALU.add, ALU.mult))
                chain(dve.scalar_tensor_tensor(pos, a1, BIG, b1, ALU.add, ALU.add))
                dve.tensor_scalar(low, pos, 15, None, ALU.bitwise_and)
                chain(dve.tensor_scalar(high, pos, 4, None, ALU.logical_shift_right))
                ramps = ramp[:, :].unsqueeze(1).to_broadcast([P, NT * E, E])
                dve.tensor_tensor(hot_high.rearrange("p (n a) -> p n a", a=E),
                                  high.unsqueeze(2).to_broadcast([P, NT * E, E]), ramps, ALU.is_equal)
                chain(dve.tensor_tensor(hot, low.unsqueeze(2).to_broadcast([P, NT * E, E]), ramps, ALU.is_equal))
                chain(dve.tensor_tensor(hot_low.rearrange("p (t n) -> p t n", t=NT),
                                        xs[:, :].rearrange("p (t n) -> p t n", t=NT),
                                        token_id[:, :].unsqueeze(2).to_broadcast([P, NT, E * E]), ALU.mult))
                dve.sem_inc(hots_done, 1)
                dve.wait_ge(listed, 1)
                for half in range(2):
                    chain(dve.tensor_tensor(z_all[:, half, :], bank(0, 2 + half)[:, 0:P], own_block[:, :], ALU.mult))
                    chain(dve.tensor_reduce(z[:, half, :], z_all[:, half, :].rearrange("p (e b) -> p b e", b=E),
                                            axis=X, op=ALU.add))
                dve.sem_inc(z_done, 1)
                dve.wait_ge(z_turned, 1)
                chain(dve.tensor_copy(index[:, :], bank(1, 3)[:, 0:E * CB]))
        pctx.close()

    def experts():
        pctx = ExitStack()
        sem = lambda name: pctx.enter_context(nc.semaphore(name))
        strips = Strips(nc, pctx, "experts", w_raw, w_hi, w_lo)
        NS = 12
        NF = 8
        gathered = [sem("gathered0"), sem("gathered1")]
        index_step, scattered, y_free = sem("index_step"), sem("scattered"), sem("y_free")
        turned, freed = sem("ex_turned"), sem("ex_freed")
        x_hi, low_copied, silu_done, hid_done, hid_hi_done, hid_lo_done, aff_done = (
            sem("ex_x_hi"), sem("low_copied"), sem("silu_done"), sem("hid_done"), sem("hid_hi_done"),
            sem("hid_lo_done"), sem("aff_done"))
        RW = CB * ROW
        xg = [t[:, 0:RW].rearrange("p (c r) -> p c r", c=CB) for t in (h, vin)]
        xt = [act_hi, act_lo]
        hid_hi = q_hi[:, :, 0:CAP]
        hid_lo = q_lo[:, :, 0:CAP]
        low_half = h[:, RW:RW + 4 * CAP].rearrange("p (b c) -> p b c", b=4)
        sums = vin[:, RW:RW + 4 * CAP].rearrange("p (b c) -> p b c", b=4)
        silu = h[:, RW + 4 * CAP:RW + 6 * CAP].rearrange("p (b c) -> p b c", b=2)
        hid = vin[:, RW + 4 * CAP:RW + 6 * CAP].rearrange("p (b c) -> p b c", b=2)
        y = [xs[:, n * CB * D:(n + 1) * CB * D].rearrange("p (c d) -> p c d", c=CB) for n in range(2)]
        aff = stat[:, 24:24 + CB]
        gather_index = [indices[:, 2 * n:2 * n + 2] for n in range(2)]
        scatter_index = [indices[:, 4 + 2 * n:6 + 2 * n] for n in range(2)]
        wg = w_gate[0].rearrange("e (k p) n -> p e k n", p=P)
        wu = w_up[0].rearrange("e (k p) n -> p e k n", p=P)
        wd = w_down[0].rearrange("e (k p) n -> p e k n", p=P)

        def turned_rows(j):
            return bank(j)[:, 0:2, :].rearrange("p b (t c) -> p (b t) c", c=CAP)

        with nc.Block() as block:
            @block.sync
            def _(sp):
                with sp.Fori(0, E) as e:
                    ex = bass.ds(e, 1)
                    for s in range(NS):
                        if s < 8:
                            w, c = (wg, wu)[s % 2], s // 2 * 256
                            source, blocks = w[:, ex, :, c:c + 256].rearrange("p e k n -> p (e k) n"), KB
                        else:
                            half, kh = (s - 8) // 2, s % 2
                            source = wd[:, ex, 4 * kh:4 * kh + 4, T * half:T * half + T].rearrange("p e k n -> p (e k) n")
                            blocks = 4
                        strips.load(sp, e * NS + s, s % 2, source, blocks)

            @block.gpsimd
            def _(pool):
                strips.open(pool=pool)
                pool.sem_inc(y_free, 1)

                def gather(n):
                    for c in range(CB):
                        pool.indirect_dma_start(xg[n][:, c, :], None, row_d, bass.IndirectOffsetOnAxis(
                            ap=gather_index[n][:, c:c + 1], axis=0)).then_inc(gathered[n], STEP)

                for c in range(CB):
                    pool.dma_start(primed[:, c, :], row_d[0:16, 0:16]).then_inc(scattered, STEP)
                for n in range(2):
                    pool.tensor_copy(gather_index[n], index[:, CB * n:CB * n + CB]).then_inc(index_step, 1)
                pool.wait_ge(index_step, 2)
                for n in range(2):
                    gather(n)
                for n in range(2):
                    strips.split_lo_pool(pool, n, n)

                def expert(e, n, steps, fills, has_next, has_second):
                    for s in range(2, NS + 2 if has_next else NS):
                        strips.split_lo_pool(pool, e * NS + s, s % 2)
                    pool.tensor_copy(scatter_index[n], index[:, bass.ds(e * CB, CB)]).then_inc(index_step, 1)
                    pool.wait_ge(index_step, steps + 1)
                    pool.wait_ge(freed, fills)
                    pool.wait_ge(scattered, e * CB * STEP + CB * STEP)
                    pool.sem_inc(y_free, 1)
                    for c in range(CB):
                        pool.indirect_dma_start(sum_d, bass.IndirectOffsetOnAxis(ap=scatter_index[n][:, c:c + 1], axis=0),
                                                y[n][:, c, :], None, compute_op=ALU.add).then_inc(scattered, STEP)
                    if has_second:
                        pool.tensor_copy(gather_index[n], index[:, bass.ds(e * CB + 2 * CB, CB)]).then_inc(index_step, 1)
                        pool.wait_ge(index_step, steps + 2)
                        apart(pool, spare)
                        gather(n)

                with pool.Fori(0, E // 2 - 1) as i:
                    for n in range(2):
                        e = i * 2 + n
                        expert(e, n, e * 2 + 2, e * NF + NF + 2, True, True)
                expert(E - 2, 0, 2 * E - 2, (E - 1) * NF + 2, True, False)
                expert(E - 1, 1, 2 * E - 1, E * NF, False, False)
                pool.wait_ge(scattered, E * CB * STEP + CB * STEP)

            @block.scalar
            def _(act):
                def turn_hi(n, at):
                    for j in range(2):
                        act.wait_ge(turned, at + j + 1)
                        act.activation(xt[n][:, 4 * j:4 * j + 4, 0:CAP], turned_rows(j), ACT.Copy).then_inc(x_hi, 1)

                def split(e, s):
                    g = e * NS + s
                    strips.split_hi(act, g, s % 2, e * (NS // 2) + s // 2 + 1)

                def expert(e, n, has_next):
                    for f in range(4):
                        split(e, 2 * f + 2)
                        split(e, 2 * f + 3)
                        strips.done(act, e * NS + 2 * f + 1)
                        act.activation(low_half, bank(f % 2)[:, :, CAP:2 * CAP], ACT.Copy).then_inc(low_copied, 1)
                        act.wait_ge(freed, e * NF + f + 3)
                        act.activation(silu, sums[:, 0:2, :], ACT.Silu).then_inc(silu_done, 1)
                        act.wait_ge(hid_done, e * 4 + f + 1)
                        act.activation(hid_hi[:, 2 * f:2 * f + 2, :], hid, ACT.Copy).then_inc(hid_hi_done, 1)
                    if has_next:
                        turn_hi(1 - n, e * 2 + 2)
                    split(e, 10)
                    split(e, 11)
                    if has_next:
                        split(e, 12)
                        split(e, 13)

                split(0, 0)
                split(0, 1)
                turn_hi(0, 0)
                with act.Fori(0, E // 2 - 1) as i:
                    for n in range(2):
                        expert(i * 2 + n, n, True)
                expert(E - 2, 0, True)
                expert(E - 1, 1, False)

            @block.vector
            def _(dve):
                strips.open(dve=dve)

                def turn_lo(n, at):
                    for j in range(2):
                        dve.wait_ge(x_hi, at + j + 1)
                        dve.tensor_tensor(xt[n][:, 4 * j:4 * j + 4, CAP:2 * CAP], turned_rows(j),
                                          xt[n][:, 4 * j:4 * j + 4, 0:CAP].bitcast(F32), ALU.subtract).then_inc(freed, 1)

                def split(e, s):
                    strips.split_lo(dve, e * NS + s, s % 2)

                def expert(e, n, has_next):
                    for f in range(4):
                        split(e, 2 * f + 2)
                        split(e, 2 * f + 3)
                        dve.wait_ge(low_copied, e * 4 + f + 1)
                        dve.tensor_tensor(sums, bank(f % 2)[:, :, 0:CAP], low_half, ALU.add).then_inc(freed, 1)
                        dve.wait_ge(silu_done, e * 4 + f + 1)
                        dve.tensor_tensor(hid, silu, sums[:, 2:4, :], ALU.mult).then_inc(hid_done, 1)
                        dve.wait_ge(hid_hi_done, e * 4 + f + 1)
                        dve.tensor_tensor(hid_lo[:, 2 * f:2 * f + 2, :], hid,
                                          hid_hi[:, 2 * f:2 * f + 2, :].bitcast(F32), ALU.subtract).then_inc(hid_lo_done, 1)
                    if has_next:
                        turn_lo(1 - n, e * 2 + 2)
                    dve.tensor_copy(aff.rearrange("p (c o) -> p c o", o=1),
                                    xg[n][:, :, bass.ds(e + D, 1)]).then_inc(aff_done, 1)
                    dve.wait_ge(aff_done, e + 1)
                    dve.wait_ge(y_free, e + 1)
                    for half in range(2):
                        if half == 0:
                            split(e, 10)
                            split(e, 11)
                        elif has_next:
                            split(e, 12)
                        strips.done(dve, e * NS + 9 + 2 * half)
                        for c in range(CB):
                            ins = dve.tensor_scalar(y[n][:, c, T * half:T * half + T], bank(half, c), aff[:, c:c + 1],
                                                    None, ALU.mult)
                        ins.then_inc(freed, 1)
                    if has_next:
                        split(e, 13)

                split(0, 0)
                split(0, 1)
                turn_lo(0, 0)
                with dve.Fori(0, E // 2 - 1) as i:
                    for n in range(2):
                        expert(i * 2 + n, n, True)
                expert(E - 2, 0, True)
                expert(E - 1, 1, False)

            @block.tensor
            def _(pe):
                strips.open(pe=pe)

                def turn(n, wait_rows, at):
                    wait_rows()
                    for j in range(2):
                        if at is not None:
                            pe.wait_ge(freed, at + j + 1)
                        for k in range(4 * j, 4 * j + 4):
                            for c in range(CB):
                                last = pe.transpose(turned_rows(j)[:, k - 4 * j, c * P:(c + 1) * P],
                                                    xg[n][:, c, k * P:(k + 1) * P], ident[:, :])
                        last.then_inc(turned, 1)

                def expert(e, n, gathers, has_next):
                    for f in range(4):
                        pe.wait_ge(freed, e * NF + f + 1)
                        for part in range(2):
                            s = 2 * f + part
                            strips.ready(pe, e * NS + s)
                            hi, lo = strips.views(s % 2, KB)
                            for m in range(2):
                                o = bank(f % 2, 2 * part + m)
                                c = slice(m * P, (m + 1) * P)
                                for k in range(KB):
                                    pe.matmul(o, hi[:, k, c], xt[n][:, k, :], start=k == 0, stop=False)
                                    last = pe.matmul(o[:, 0:CAP], lo[:, k, c], xt[n][:, k, 0:CAP], start=False,
                                                     stop=k == KB - 1)
                            last.then_inc(strips.used, 1)
                    if has_next:
                        turn(1 - n, gathers, e * NF + 4)
                    less = 0 if has_next else 2
                    for half in range(2):
                        pe.wait_ge(freed, e * NF + 6 + half + 1 - less)
                        for kh in range(2):
                            s = 8 + 2 * half + kh
                            strips.ready(pe, e * NS + s)
                            pe.wait_ge(hid_lo_done, e * 4 + 2 * kh + 2)
                            hi, lo = strips.views(s % 2, 4)
                            for c in range(CB):
                                t = slice(c * P, (c + 1) * P)
                                for k in range(4):
                                    kk = 4 * kh + k
                                    last = product(pe, bank(half, c), (hid_hi[:, kk, t], hid_lo[:, kk, t]),
                                                   (hi[:, k, :], lo[:, k, :]), kk == 0, kk == FB - 1)
                            last.then_inc(strips.used, 1)

                turn(0, lambda: pe.wait_ge(gathered[0], CB * STEP), None)
                pe.wait_ge(freed, 2)
                with pe.Fori(0, E // 2 - 1) as i:
                    expert(i * 2, 0, lambda: pe.wait_ge(gathered[1], i * CB * STEP + CB * STEP), True)
                    expert(i * 2 + 1, 1, lambda: pe.wait_ge(gathered[0], i * CB * STEP + 2 * CB * STEP), True)
                expert(E - 2, 0, lambda: pe.wait_ge(gathered[1], E // 2 * CB * STEP), True)
                expert(E - 1, 1, None, False)
        pctx.close()

    def final():
        pctx = ExitStack()
        sem = lambda name: pctx.enter_context(nc.semaphore(name))
        loaded = [sem("fn_loaded0"), sem("fn_loaded1")]
        stored = [sem("fn_stored0"), sem("fn_stored1")]
        gain_loaded, squares, var_done, root_done, chain_sem, normed = (
            sem("fn_gain"), sem("fn_squares"), sem("fn_var"), sem("fn_root"), sem("fn_chain"), sem("fn_normed"))
        tiles = [t[:, :].rearrange("p (t d) -> p t d", t=TB) for t in (h, xs)]
        sum_v = sum_d.rearrange("(i t p) d -> i p t d", p=P, t=TB)
        out_v = out[0].rearrange("(i t p) d -> i p t d", p=P, t=TB)
        with nc.Block() as block:
            @block.sync
            def _(sp):
                sp.dma_start(gain_row[:, :], norm_final.rearrange("(o d) -> o d", o=1).to_broadcast([P, D])).then_inc(
                    gain_loaded, STEP)
                for i in range(TILES):
                    if i >= 2:
                        sp.wait_ge(stored[i % 2], STEP * (i // 2))
                    sp.dma_start(tiles[i % 2], sum_v[i]).then_inc(loaded[i % 2], STEP)

            @block.scalar
            def _(act):
                for i in range(TILES):
                    act.wait_ge(loaded[i % 2], STEP * (i // 2 + 1))
                    for t in range(TB):
                        act.activation(junk[:, t, :], tiles[i % 2][:, t, :], ACT.Square,
                                       accum_out=ss[:, t:t + 1]).then_inc(squares, 1)
                    act.wait_ge(var_done, i + 1)
                    act.activation(root, var, ACT.Sqrt).then_inc(root_done, 1)
                    act.wait_ge(normed, TB * (i + 1))
                    act.dma_start(out_v[i], tiles[i % 2]).then_inc(stored[i % 2], STEP)
                for n in range(2):
                    act.wait_ge(stored[n], STEP * TILES // 2)

            @block.vector
            def _(dve):
                dve.wait_ge(gain_loaded, STEP)
                for i in range(TILES):
                    chain = Chain(dve, chain_sem, 5 * i)
                    dve.wait_ge(squares, TB * (i + 1))
                    dve.tensor_scalar(var, ss, 1.0 / D, RMS_EPS, ALU.mult, ALU.add).then_inc(var_done, 1)
                    dve.wait_ge(root_done, i + 1)
                    refine_rstd(dve, chain, TB)
                    for t in range(TB):
                        dve.scalar_tensor_tensor(tiles[i % 2][:, t, :], tiles[i % 2][:, t, :], rstd[:, t:t + 1],
                                                 gain_row[:, :], ALU.mult, ALU.mult).then_inc(normed, 1)
        pctx.close()

    setup()
    conv()
    attend()
    select()
    experts()
    final()
    ctx.close()


_INS = ["x", "mem", "norm_mix", "norm_xattn", "norm_mem", "norm_ffn", "norm_final", "conv_w_in", "conv_w",
        "conv_w_out", "xattn_w_q", "xattn_w_kv", "xattn_w_o", "moe_router", "moe_w_gate", "moe_w_up", "moe_w_down"]


def kernel(**inputs):
    import numpy as np
    import concourse.bacc as bacc
    from concourse.bass_utils import run_bass_kernel_spmd

    nc = bacc.Bacc("TRN2", target_bir_lowering=False, num_devices=1)
    arrays, args = {}, []
    for name in _INS:
        a = np.ascontiguousarray(inputs[name])
        arrays[f"in_{name}"] = a
        args.append(nc.dram_tensor(f"in_{name}", a.shape, mybir.dt.from_np(a.dtype), kind="ExternalInput").ap())
    out = nc.dram_tensor("out", (1, SEQ, D), F32, kind="ExternalOutput").ap()
    build(nc, *args, out)
    return run_bass_kernel_spmd(nc, [arrays], core_ids=[0]).results[0]["out"]
```

```python
from contextlib import ExitStack

import concourse.bass as bass
from concourse import mybir

F32 = mybir.dt.float32
F32R = mybir.dt.float32r
BF16 = mybir.dt.bfloat16
I32 = mybir.dt.int32
U32 = mybir.dt.uint32
ALU = mybir.AluOpType
ACT = mybir.ActivationFunctionType
X = mybir.AxisListType.X

P = 128
D = 1024
SEQ = 2048
KB = D // P
T = 512
TB = T // P
TILES = SEQ // T
MEM = 256
MB = MEM // P
HEADS = 4
HD = D // HEADS
HB = HD // P
E = 16
CAP = 2 * SEQ // E
CB = CAP // P
FF = 1024
FB = FF // P
RMS_EPS = 1e-6
ROW = D + E
STRIP = 2048
POOL_PART = 512
STEP = 16
CONV_COLS = SEQ + 1


class Strips:

    def __init__(self, nc, ctx, name, raw, hi, lo):
        self.raw, self.hi, self.lo = raw, hi, lo
        self.loaded = [ctx.enter_context(nc.semaphore(f"{name}_strip_loaded{i}")) for i in range(2)]
        self.hi_done = ctx.enter_context(nc.semaphore(f"{name}_strip_hi"))
        self.lo_vector = ctx.enter_context(nc.semaphore(f"{name}_strip_lo_vector"))
        self.lo_pool = ctx.enter_context(nc.semaphore(f"{name}_strip_lo_pool"))
        self.used = ctx.enter_context(nc.semaphore(f"{name}_strip_used"))

    def load(self, sp, g, slot, source, blocks):
        sp.wait_ge(self.lo_vector, g + 1)
        sp.wait_ge(self.lo_pool, g + 1)
        sp.dma_start(self.raw[:, slot, :].rearrange("p (k n) -> p k n", k=blocks), source).then_inc(
            self.loaded[slot], STEP)

    def split_hi(self, act, g, slot):
        act.wait_ge(self.loaded[slot], g * (STEP // 2) + (STEP - slot * STEP // 2))
        act.wait_ge(self.used, g + 1)
        act.activation(self.hi[:, slot, :], self.raw[:, slot, :], ACT.Copy).then_inc(self.hi_done, 1)

    def split_lo(self, dve, g, slot):
        dve.wait_ge(self.hi_done, g + 1)
        a = STRIP - POOL_PART
        dve.tensor_tensor(self.lo[:, slot, 0:a], self.raw[:, slot, 0:a], self.hi[:, slot, 0:a].bitcast(F32),
                          ALU.subtract).then_inc(self.lo_vector, 1)

    def split_lo_pool(self, pool, g, slot):
        pool.wait_ge(self.hi_done, g + 1)
        a = STRIP - POOL_PART
        pool.tensor_tensor(self.lo[:, slot, a:], self.raw[:, slot, a:], self.hi[:, slot, a:].bitcast(F32),
                           ALU.subtract).then_inc(self.lo_pool, 1)

    def ready(self, pe, g):
        pe.wait_ge(self.lo_vector, g + 3)
        pe.wait_ge(self.lo_pool, g + 3)

    def done(self, engine, g):
        engine.wait_ge(self.used, g + 3)

    def views(self, slot, blocks):
        return (self.hi[:, slot, :].rearrange("p (k n) -> p k n", k=blocks),
                self.lo[:, slot, :].rearrange("p (k n) -> p k n", k=blocks))

    def open(self, dve=None, pool=None, pe=None):
        if dve is not None:
            dve.sem_inc(self.lo_vector, 2)
        if pool is not None:
            pool.sem_inc(self.lo_pool, 2)
        if pe is not None:
            pe.sem_inc(self.used, 2)


def apart(engine, spare):
    engine.sem_inc(spare, 1)


class Chain:

    def __init__(self, dve, sem, base=0):
        self.dve, self.sem, self.base, self.n = dve, sem, base, 0

    def __call__(self, instruction):
        self.n += 1
        instruction.then_inc(self.sem, 1)
        self.dve.wait_ge(self.sem, self.base + self.n)


def build(nc, x, mem, norm_mix, norm_xattn, norm_mem, norm_ffn, norm_final, conv_w_in, conv_w, conv_w_out,
          w_q, w_kv, w_o, router, w_gate, w_up, w_down, out):
    ctx = ExitStack()

    def sb(name, shape, dt=F32):
        return ctx.enter_context(nc.sbuf_tensor(name, shape, dt))

    w_raw = sb("w_raw", [P, 2, STRIP])
    w_hi = sb("w_hi", [P, 2, STRIP], F32R)
    w_lo = sb("w_lo", [P, 2, STRIP], F32R)
    act_hi = sb("act_hi", [P, KB, T], F32R)
    act_lo = sb("act_lo", [P, KB, T], F32R)
    q_hi = sb("q_hi", [P, KB, T], F32R)
    q_lo = sb("q_lo", [P, KB, T], F32R)
    h = sb("h", [P, TB * D])
    xs = sb("xs", [P, TB * D])
    vin = sb("vin", [P, KB * T])
    k_hi = sb("k_hi", [P, KB, MEM], F32R)
    k_lo = sb("k_lo", [P, KB, MEM], F32R)
    v_hi = sb("v_hi", [P, MB, D], F32R)
    v_lo = sb("v_lo", [P, MB, D], F32R)
    ident = sb("ident", [P, P])
    ones = sb("ones", [P, P])
    upper = sb("upper", [P, P])
    same_expert = sb("same_expert", [P, P])
    ramp = sb("ramp", [P, E])
    token_id = sb("token_id", [P, SEQ // P])
    ints = sb("ints", [P, P], I32)
    ints2 = sb("ints2", [P, P], I32)
    own_block = sb("own_block", [P, P])
    gains = sb("gains", [P, 3, KB])
    taps = sb("taps", [P, 3, KB])
    gain_row = sb("gain_row", [P, D])
    r_raw = sb("r_raw", [P, KB, E])
    r_hi = sb("r_hi", [P, KB, E], F32R)
    r_lo = sb("r_lo", [P, KB, E], F32R)
    probs = sb("probs", [P, SEQ // P * E])
    index = sb("index", [P, E * CB], U32)
    stat = sb("stat", [P, 68])
    junk = sb("junk", [P, TB, D], mybir.dt.uint8)
    indices = sb("indices", [P, 4 * CB], U32)
    primed = sb("primed", [16, CB, 16])
    r_buf = sb("r_buf", [P, TB * E])
    spare = ctx.enter_context(nc.semaphore("spare"))
    ps = ctx.enter_context(nc.psum_tensor("ps", [P, 8, T], F32))

    v_d = nc.dram_tensor("conv_v", [D, CONV_COLS], F32).ap()
    sum_d = nc.dram_tensor("residual", [SEQ, D], F32).ap()
    row_d = nc.dram_tensor("normed_rows", [SEQ, ROW], F32).ap()
    index_d = nc.dram_tensor("index_lists", [E, CAP], F32).ap()

    ss, var, root, rstd, tmp, tmp2 = (stat[:, 4 * i:4 * i + 4] for i in range(6))

    def bank(group, b=None):
        return ps[:, 4 * group:4 * group + 4, :] if b is None else ps[:, 4 * group + b, :]

    def product(pe, o, lhs, rhs, first, last):
        pe.matmul(o, lhs[0], rhs[0], start=first, stop=False)
        pe.matmul(o, lhs[0], rhs[1], start=False, stop=False)
        return pe.matmul(o, lhs[1], rhs[0], start=False, stop=last)

    def refine_rstd(dve, chain, n):
        chain(dve.reciprocal(rstd[:, 0:n], root[:, 0:n]))
        chain(dve.tensor_tensor(tmp[:, 0:n], rstd[:, 0:n], rstd[:, 0:n], ALU.mult))
        chain(dve.tensor_tensor(tmp2[:, 0:n], tmp[:, 0:n], var[:, 0:n], ALU.mult))
        chain(dve.tensor_scalar(tmp[:, 0:n], tmp2[:, 0:n], -0.5, 1.5, ALU.mult, ALU.add))
        chain(dve.tensor_tensor(rstd[:, 0:n], rstd[:, 0:n], tmp[:, 0:n], ALU.mult))

    def front():
        pctx = ExitStack()
        sem = lambda name: pctx.enter_context(nc.semaphore(name))
        strips = Strips(nc, pctx, "front", w_raw, w_hi, w_lo)
        NS = 12
        CONV0 = 8
        ATT0 = CONV0 + NS * TILES
        BODY0 = ATT0 + 4

        mem_loaded, consts_loaded, router_loaded = sem("mem_loaded"), sem("consts_loaded"), sem("router_loaded")
        const_step, consts_made, const_chain = sem("const_step"), sem("consts_made"), sem("const_chain")
        mem_squares, mem_var, mem_root, mem_chain, mem_done = (
            sem("mem_squares"), sem("mem_var"), sem("mem_root"), sem("mem_chain"), sem("mem_done"))
        filled, kv_hi, kv_lo, router_hi = sem("su_filled"), sem("kv_hi"), sem("kv_lo"), sem("su_router_hi")
        memx = vin[:, 0:MB * D].rearrange("p (t d) -> p t d", t=MB)
        kv = w_kv[0].rearrange("(k p) n -> p k n", p=P)

        x_loaded = sem("x_loaded")
        squares, var_done, root_done, chain_sem, xs_done = (
            sem("cv_squares"), sem("cv_var"), sem("cv_root"), sem("cv_chain"), sem("cv_xs"))
        transposed, xn_hi, xn_lo = sem("cv_transposed"), sem("xn_hi"), sem("xn_lo")
        c_read, u_done, v_done, v_free, v_stored = (
            sem("c_read"), sem("u_done"), sem("v_done"), sem("v_free"), sem("v_stored"))
        xt = h[:, :].rearrange("p (t d) -> p t d", t=TB)
        pairs = [(q_hi, q_lo), (act_hi, act_lo)]
        u = xs[:, 0:4 * (T + 2)].rearrange("p (m c) -> p m c", m=4)
        cgate = vin[:, 0:4 * T].rearrange("p (m c) -> p m c", m=4)
        cv = vin[:, 4 * T:].rearrange("p (m c) -> p m c", m=4)
        u_carry = stat[:, 24:40].rearrange("p (m c) -> p m c", c=2)
        b_carry = stat[:, 40:48]
        last_v = stat[:, 48:56]
        last_t = stat[:, 56:64]
        w_in = conv_w_in[0].rearrange("(k p) n -> p k n", p=P)
        x_v = x[0].rearrange("(i t p) d -> p i t d", p=P, t=TB)
        v_v = v_d.rearrange("(m p) c -> p m c", p=P)
        COLUMNS = [part * D + half * T for half in range(2) for part in (1, 2, 0)]
        GROUP = (0, 1, 0, 1, 1, 0)

        at_x_loaded, v_loaded, tile_free, rows_free, stored = (
            sem("at_x_loaded"), sem("at_v_loaded"), sem("tile_free"), sem("rows_free"), sem("at_stored"))
        at_squares, at_var, at_root, at_chain, at_rstd = (
            sem("at_squares"), sem("at_var"), sem("at_root"), sem("at_chain"), sem("at_rstd"))
        rows_vector, rows_scalar = sem("rows_vector"), sem("rows_scalar")
        v_hi_done, v_lo_done = sem("at_v_hi"), sem("at_v_lo")
        n1_hi, n1_lo, qh, ql = sem("n1_hi"), sem("n1_lo"), sem("q_hi_done"), sem("q_lo_done")
        pt_hi, pt_lo, o_hi, o_lo, n3_hi, n3_lo = (
            sem("pt_hi"), sem("pt_lo"), sem("o_hi"), sem("o_lo"), sem("n3_hi"), sem("n3_lo"))
        added = sem("at_added")
        turned, scored, maxed, exped, p_done = (
            sem("turned"), sem("scored"), sem("maxed"), sem("exped"), sem("p_done"))
        valued, routed, shifted, r_exp, probs_done = (
            sem("valued"), sem("routed"), sem("shifted"), sem("r_exp"), sem("probs_done"))
        tiles = [b[:, :].rearrange("p (t d) -> p t d", t=TB) for b in (h, vin)]
        v_tiles = [b[:, :].rearrange("p (k c) -> p k c", k=KB) for b in (h, vin)]
        xn = xs[:, :].rearrange("p (t d) -> p t d", t=TB)
        pr = xs[:, :].rearrange("p (h t m) -> p h t m", h=HEADS, t=TB)
        neg_max = stat[:, 24:40].rearrange("p (h t) -> p h t", h=HEADS)
        sums = stat[:, 40:56].rearrange("p (h t) -> p h t", h=HEADS)
        r_max = stat[:, 56:60]
        r_sum = stat[:, 60:64]
        ss_b = stat[:, 64:68]
        r_tmp = r_buf[:, :]
        sum_v = sum_d.rearrange("(i t p) d -> p i t d", p=P, t=TB)
        row_v = row_d.rearrange("(i t p) d -> p i t d", p=P, t=TB)
        w_co = conv_w_out[0].rearrange("(k p) n -> p k n", p=P)
        w_qv = w_q[0].rearrange("(k p) n -> p k n", p=P)
        w_ov = w_o[0].rearrange("(k p) n -> p k n", p=P)
        BODY_CHAIN = 6 + 6 + HEADS + 5

        def scores_bank(head):
            return bank(head // 2)[:, 2 * (head % 2):2 * (head % 2) + 2, :].rearrange("p b (t m) -> p (b t) m", m=MEM)

        def tiles_loop(engine, tile):
            with engine.Fori(0, TILES // 2 - 1) as j:
                for n in range(2):
                    tile(j * 2 + n, n, False)
            tile(TILES - 2, 0, False)
            tile(TILES - 1, 1, True)

        def rows(i):
            return bass.ds(i, 1)

        with nc.Block() as block:
            @block.sync
            def _(sp):
                sp.dma_start(memx, mem[0].rearrange("(t p) d -> p t d", p=P)).then_inc(mem_loaded, STEP)
                for g in range(CONV0):
                    half, kh = g // 2, g % 2
                    strips.load(sp, g, g % 2, kv[:, 4 * kh:4 * kh + 4, T * half:T * half + T], 4)
                    if g == 1:
                        sp.dma_start(xt, x_v[:, 0]).then_inc(x_loaded, STEP)

                def conv_tile(i, n, last):
                    for s in range(NS):
                        c, kh = COLUMNS[s // 2], s % 2
                        strips.load(sp, i * NS + (CONV0 + s), s % 2, w_in[:, 4 * kh:4 * kh + 4, c:c + T], 4)
                        if s == 3 and not last:
                            sp.wait_ge(transposed, i * 2 + 2)
                            sp.dma_start(xt, x_v[:, rows(i + 1), :, :].rearrange("p i t d -> p (i t) d")).then_inc(
                                x_loaded, STEP)
                        if s == 6 and last:
                            sp.wait_ge(transposed, 2 * TILES)
                            sp.wait_ge(v_stored, 4 * STEP)
                            sp.dma_start(v_tiles[0], v_v[:, :, 1:T + 1]).then_inc(v_loaded, STEP)
                        if s == 11 and last:
                            sp.wait_ge(v_lo_done, KB)
                            sp.dma_start(tiles[0], x_v[:, 0]).then_inc(at_x_loaded, STEP)
                tiles_loop(sp, conv_tile)

                for s in range(4):
                    half, kh = s // 2, s % 2
                    strips.load(sp, ATT0 + s, s % 2, w_co[:, 4 * kh:4 * kh + 4, T * half:T * half + T], 4)

                def attend_tile(i, n, last):
                    for s in range(8 if last else NS):
                        w = (w_qv, w_ov, w_co)[s // 4]
                        half, kh = s // 2 % 2, s % 2
                        strips.load(sp, i * NS + (BODY0 + s), s % 2, w[:, 4 * kh:4 * kh + 4, T * half:T * half + T], 4)
                        if s == 3 and not last:
                            sp.wait_ge(tile_free, i + 1)
                            sp.dma_start(v_tiles[1 - n], v_v[:, :, bass.ds(i * T + (T + 1), T)]).then_inc(v_loaded, STEP)
                        if s == 8:
                            sp.wait_ge(v_lo_done, i * KB + 2 * KB)
                            sp.dma_start(tiles[1 - n], x_v[:, rows(i + 1), :, :].rearrange("p i t d -> p (i t) d")
                                         ).then_inc(at_x_loaded, STEP)
                tiles_loop(sp, attend_tile)

            @block.gpsimd
            def _(pool):
                strips.open(pool=pool)
                pool.sem_inc(v_free, 1)
                pool.memset(ones[:, :], 1.0).then_inc(const_step, 1)
                pool.memset(ident[:, :], 0.0).then_inc(const_step, 1)
                pool.wait_ge(const_step, 2)
                pool.affine_select(out=ident[:, :], in_=ident[:, :], compare_op=ALU.not_equal, fill=1.0, base=0,
                                   pattern=[[-1, P]], channel_multiplier=1).then_inc(consts_made, 1)
                for g in range(2):
                    strips.split_lo_pool(pool, g, g % 2)
                pool.affine_select(out=upper[:, :], in_=ones[:, :], compare_op=ALU.is_ge, fill=0.0, base=-1,
                                   pattern=[[1, P]], channel_multiplier=-1).then_inc(consts_made, 1)
                pool.iota(ints[:, :], pattern=[[-1, P]], base=P, channel_multiplier=1).then_inc(consts_made, 1)
                pool.iota(ints2[:, :], pattern=[[-16, 8], [0, 16]], base=P, channel_multiplier=1).then_inc(
                    consts_made, 1)
                pool.iota(ramp[:, :], pattern=[[1, E]], base=0, channel_multiplier=0,
                          allow_small_or_imprecise_dtypes=True).then_inc(consts_made, 1)
                pool.iota(token_id[:, :], pattern=[[P, SEQ // P]], base=0, channel_multiplier=1,
                          allow_small_or_imprecise_dtypes=True).then_inc(consts_made, 1)
                for g in range(2, CONV0 + 2):
                    strips.split_lo_pool(pool, g, g % 2)

                def conv_tile(i, n, last):
                    def split(s):
                        strips.split_lo_pool(pool, i * NS + (CONV0 + s), s % 2)

                    def store(half):
                        pool.wait_ge(v_done, i * 2 + (half + 2))
                        apart(pool, spare)
                        pool.dma_start(v_v[:, 4 * half:4 * half + 4, bass.ds(i * T, T)], cv).then_inc(v_stored, STEP)

                    def release(half):
                        pool.wait_ge(v_stored, i * 2 * STEP + (half + 1) * STEP)
                        pool.sem_inc(v_free, 1)

                    for s in range(2, 8):
                        split(s)
                    store(0)
                    split(8)
                    split(9)
                    release(0)
                    for s in range(10, 14):
                        split(s)
                    store(1)
                    release(1)
                tiles_loop(pool, conv_tile)
                pool.wait_ge(v_done, 2 * TILES + 2)
                pool.dma_start(v_v[:, :, SEQ:SEQ + 1], last_v.rearrange("p (m o) -> p m o", o=1),
                               allow_slow_non_contiguous=True).then_inc(v_stored, STEP)
                pool.wait_ge(v_stored, (2 * TILES + 1) * STEP)
                pool.sem_inc(tile_free, 1)

                for s in range(2, 6):
                    strips.split_lo_pool(pool, ATT0 + s, s % 2)

                def attend_tile(i, n, last):
                    def split(s):
                        if s < 8 or not last:
                            strips.split_lo_pool(pool, i * NS + (BODY0 + s), s % 2)

                    for s in range(2, 10):
                        split(s)
                    pool.wait_ge(added, i * 4 + 4)
                    apart(pool, spare)
                    pool.dma_start(sum_v[:, rows(i), :, :].rearrange("p i t d -> p (i t) d"), tiles[n]).then_inc(stored, STEP)
                    split(10)
                    pool.wait_ge(rows_vector, i * 6 + 6)
                    apart(pool, spare)
                    pool.dma_start(row_v[:, rows(i), :, 0:D].rearrange("p i t d -> p (i t) d"), xn).then_inc(stored, STEP)
                    split(11)
                    split(12)
                    pool.wait_ge(stored, i * 3 * STEP + 2 * STEP)
                    pool.sem_inc(tile_free, 1)
                    pool.sem_inc(rows_free, 1)
                    split(13)
                    pool.wait_ge(probs_done, i + 1)
                    apart(pool, spare)
                    pool.dma_start(row_v[:, rows(i), :, D:ROW].rearrange("p i t e -> p (i t) e"),
                                   r_tmp.rearrange("p (t e) -> p t e", t=TB)).then_inc(stored, STEP)
                    pool.wait_ge(stored, i * 3 * STEP + 3 * STEP)
                tiles_loop(pool, attend_tile)

            @block.scalar
            def _(act):
                for n, gain in enumerate((norm_mix, norm_xattn, norm_mem)):
                    act.dma_start(gains[:, n, :], gain[0].rearrange("(k p) -> p k", p=P),
                                  allow_slow_non_contiguous=True).then_inc(consts_loaded, STEP)
                for n in range(3):
                    act.dma_start(taps[:, n, :], conv_w[0, n].rearrange("(k p) -> p k", p=P),
                                  allow_slow_non_contiguous=True).then_inc(consts_loaded, STEP)
                act.dma_start(gain_row[:, :], norm_ffn[0:1, :].to_broadcast([P, D])).then_inc(consts_loaded, STEP)
                act.dma_start(r_raw[:, :, :], router[0].rearrange("(k p) e -> p k e", p=P)).then_inc(
                    router_loaded, STEP)
                act.wait_ge(mem_loaded, STEP)
                for t in range(MB):
                    act.activation(junk[:, t, :], memx[:, t, :], ACT.Square, accum_out=ss[:, t:t + 1]).then_inc(mem_squares, 1)
                act.wait_ge(mem_var, 1)
                act.activation(root[:, 0:MB], var[:, 0:MB], ACT.Sqrt).then_inc(mem_root, 1)
                strips.split_hi(act, 0, 0)
                strips.split_hi(act, 1, 1)
                act.wait_ge(consts_loaded, 7 * STEP)
                for k in range(KB):
                    act.wait_ge(filled, 1 + k // 4)
                    act.activation(act_hi[:, k, 0:MEM], bank(k // 4, k % 4)[:, 0:MEM], ACT.Copy,
                                   scale=gains[:, 2, k:k + 1]).then_inc(kv_hi, 1)

                def tile_stats(i):
                    act.wait_ge(x_loaded, i * STEP + STEP)
                    for t in range(TB):
                        act.activation(junk[:, t, :], xt[:, t, :], ACT.Square, accum_out=ss[:, t:t + 1]).then_inc(squares, 1)
                    act.wait_ge(var_done, i + 1)
                    act.activation(root, var, ACT.Sqrt).then_inc(root_done, 1)

                def tile_hi(i, n, half):
                    act.wait_ge(transposed, i * 2 + (1 + half))
                    for k in range(4 * half, 4 * half + 4):
                        act.activation(pairs[n][0][:, k, :], bank(half, k % 4), ACT.Copy,
                                       scale=gains[:, 0, k:k + 1]).then_inc(xn_hi, 1)

                for half in range(4):
                    strips.split_hi(act, 2 * half + 2, 0)
                    strips.done(act, 2 * half + 1)
                    if half < 2:
                        act.activation(k_hi[:, 4 * half:4 * half + 4, :], bank(half % 2)[:, :, 0:MEM],
                                       ACT.Copy).then_inc(kv_hi, 1)
                    else:
                        act.activation(v_hi[:, :, T * (half - 2):T * (half - 1)], bank(half % 2)[:, 0:MB, :],
                                       ACT.Copy).then_inc(kv_hi, 1)
                    strips.split_hi(act, 2 * half + 3, 1)
                    if half == 1:
                        tile_stats(0)
                    if half == 2:
                        act.wait_ge(router_loaded, STEP)
                        act.activation(r_hi[:, :, :], r_raw[:, :, :], ACT.Copy).then_inc(router_hi, 1)
                tile_hi(0, 0, 0)
                tile_hi(0, 0, 1)

                def conv_tile(i, n, last):
                    def split(s):
                        strips.split_hi(act, i * NS + (CONV0 + s), s % 2)

                    def read_c(half):
                        strips.done(act, i * NS + (CONV0 + 6 * half + 1))
                        act.wait_ge(u_done, i * 2 + (half + 1))
                        act.activation(cgate, bank(GROUP[3 * half]), ACT.Copy).then_inc(c_read, 1)

                    split(2)
                    read_c(0)
                    split(3)
                    split(4)
                    if not last:
                        tile_stats(i + 1)
                    for s in range(5, 9):
                        split(s)
                    if last:
                        act.wait_ge(v_loaded, STEP)
                        for k in range(KB):
                            act.activation(q_hi[:, k, :], v_tiles[0][:, k, :], ACT.Copy).then_inc(v_hi_done, 1)
                    read_c(1)
                    split(9)
                    if not last:
                        tile_hi(i + 1, 1 - n, 0)
                    for s in range(10, 14):
                        split(s)
                    if not last:
                        tile_hi(i + 1, 1 - n, 1)
                tiles_loop(act, conv_tile)

                def half_squares(n, half, count):
                    act.wait_ge(added, count)
                    c = slice(T * half, T * half + T)
                    for t in range(TB):
                        act.activation(junk[:, t, c], tiles[n][:, t, c], ACT.Square,
                                       accum_out=(ss, ss_b)[half][:, t:t + 1]).then_inc(at_squares, 1)

                def take_root(count):
                    act.wait_ge(at_var, count)
                    act.activation(root, var, ACT.Sqrt).then_inc(at_root, 1)

                def scale_rows(n, i):
                    act.wait_ge(at_rstd, i + 1)
                    for t in (2, 3):
                        act.activation(xn[:, t, :], tiles[n][:, t, :], ACT.Copy,
                                       scale=rstd[:, t:t + 1]).then_inc(rows_scalar, 1)

                strips.split_hi(act, ATT0 + 2, 0)
                strips.split_hi(act, ATT0 + 3, 1)
                half_squares(0, 0, 1)
                strips.split_hi(act, ATT0 + 4, 0)
                strips.split_hi(act, ATT0 + 5, 1)
                half_squares(0, 1, 2)
                take_root(1)
                scale_rows(0, 0)

                def attend_tile(i, n, last):
                    def split(s):
                        if s < 8 or not last:
                            strips.split_hi(act, i * NS + (BODY0 + s), s % 2)

                    for k in range(KB):
                        act.wait_ge(turned, i * 6 + (1 + k // 4))
                        act.activation(act_hi[:, k, :], bank(k // 4, k % 4), ACT.Copy,
                                       scale=gains[:, 1, k:k + 1]).then_inc(n1_hi, 1)
                    for half in range(2):
                        split(2 + 2 * half)
                        strips.done(act, i * NS + (BODY0 + 1 + 2 * half))
                        for m in range(4):
                            act.activation(q_hi[:, 4 * half + m, :], bank(half, m), ACT.Copy,
                                           scale=HD ** -0.5).then_inc(qh, 1)
                        split(3 + 2 * half)
                    for hd in range(HEADS):
                        act.wait_ge(maxed, i * HEADS + (hd + 1))
                        for t in range(TB):
                            act.activation(pr[:, hd, t, :], scores_bank(hd)[:, t, :], ACT.Exp,
                                           bias=neg_max[:, hd, t:t + 1], accum_out=sums[:, hd, t:t + 1]).then_inc(exped, 1)
                    for m in range(KB):
                        act.wait_ge(turned, i * 6 + (3 + m // 4))
                        act.activation(q_hi[:, m, :], bank(m // 4, m % 4), ACT.Copy).then_inc(pt_hi, 1)
                    for m in range(KB):
                        act.wait_ge(valued, i * 2 + (1 + m // 4))
                        act.activation(act_hi[:, m, :], bank(m // 4, m % 4), ACT.Copy).then_inc(o_hi, 1)
                    if not last:
                        act.wait_ge(v_loaded, i * STEP + 2 * STEP)
                        for k in range(KB):
                            act.activation(q_hi[:, k, :], v_tiles[1 - n][:, k, :], ACT.Copy).then_inc(v_hi_done, 1)
                    split(6)
                    split(7)
                    half_squares(n, 0, i * 4 + 3)
                    split(8)
                    split(9)
                    half_squares(n, 1, i * 4 + 4)
                    take_root(i * 2 + 2)
                    split(10)
                    split(11)
                    for k in range(KB):
                        act.wait_ge(turned, i * 6 + (5 + k // 4))
                        act.activation(act_hi[:, k, :], bank(1 - k // 4, k % 4), ACT.Copy).then_inc(n3_hi, 1)
                    if not last:
                        half_squares(1 - n, 0, i * 4 + 5)
                        split(12)
                        split(13)
                        half_squares(1 - n, 1, i * 4 + 6)
                        take_root(i * 2 + 3)
                        act.wait_ge(rows_free, i + 1)
                        scale_rows(1 - n, i + 1)
                    act.wait_ge(shifted, i + 2)
                    act.activation(r_tmp, r_tmp, ACT.Exp).then_inc(r_exp, 1)
                tiles_loop(act, attend_tile)

            @block.vector
            def _(dve):
                strips.open(dve=dve)
                chain = Chain(dve, mem_chain)
                dve.memset(stat[:, 24:64], 0.0).then_inc(chain_sem, 1)
                dve.wait_ge(chain_sem, 1)
                dve.sem_inc(u_done, 1)
                dve.sem_inc(v_done, 1)
                dve.wait_ge(mem_squares, MB)
                dve.tensor_scalar(var[:, 0:MB], ss[:, 0:MB], 1.0 / D, RMS_EPS, ALU.mult, ALU.add).then_inc(mem_var, 1)
                dve.wait_ge(mem_root, 1)
                refine_rstd(dve, chain, MB)
                for t in range(MB):
                    dve.tensor_scalar(memx[:, t, :], memx[:, t, :], rstd[:, t:t + 1], None, ALU.mult).then_inc(mem_done, 1)
                strips.split_lo(dve, 0, 0)
                strips.split_lo(dve, 1, 1)
                for k in range(KB):
                    dve.wait_ge(kv_hi, k + 1)
                    dve.scalar_tensor_tensor(act_lo[:, k, 0:MEM], bank(k // 4, k % 4)[:, 0:MEM],
                                             gains[:, 2, k:k + 1], act_hi[:, k, 0:MEM].bitcast(F32),
                                             ALU.mult, ALU.subtract).then_inc(kv_lo, 1)

                def tile_norm(i, chain):
                    dve.wait_ge(squares, i * TB + TB)
                    dve.tensor_scalar(var, ss, 1.0 / D, RMS_EPS, ALU.mult, ALU.add).then_inc(var_done, 1)
                    dve.wait_ge(root_done, i + 1)
                    refine_rstd(dve, chain, TB)
                    for t in range(TB):
                        dve.tensor_scalar(xt[:, t, :], xt[:, t, :], rstd[:, t:t + 1], None, ALU.mult).then_inc(xs_done, 1)

                def tile_lo(i, n, half):
                    for k in range(4 * half, 4 * half + 4):
                        dve.wait_ge(xn_hi, i * KB + (k + 1))
                        dve.scalar_tensor_tensor(pairs[n][1][:, k, :], bank(half, k % 4), gains[:, 0, k:k + 1],
                                                 pairs[n][0][:, k, :].bitcast(F32), ALU.mult, ALU.subtract).then_inc(xn_lo, 1)

                for half in range(4):
                    strips.split_lo(dve, 2 * half + 2, 0)
                    dve.wait_ge(kv_hi, KB + half + 1)
                    if half < 2:
                        b = slice(4 * half, 4 * half + 4)
                        dve.tensor_tensor(k_lo[:, b, :], bank(half % 2)[:, :, 0:MEM], k_hi[:, b, :].bitcast(F32),
                                          ALU.subtract).then_inc(kv_lo, 1)
                    else:
                        c = slice(T * (half - 2), T * (half - 1))
                        dve.tensor_tensor(v_lo[:, :, c], bank(half % 2)[:, 0:MB, :], v_hi[:, :, c].bitcast(F32),
                                          ALU.subtract).then_inc(kv_lo, 1)
                    strips.split_lo(dve, 2 * half + 3, 1)
                    if half == 1:
                        tile_norm(0, Chain(dve, chain_sem, 1))
                tile_lo(0, 0, 0)
                tile_lo(0, 0, 1)
                constants = Chain(dve, const_chain)
                dve.wait_ge(router_hi, 1)
                constants(dve.tensor_tensor(r_lo[:, :, :], r_raw[:, :, :], r_hi[:, :, :].bitcast(F32), ALU.subtract))
                dve.wait_ge(consts_made, 6)
                constants(dve.tensor_scalar(ints[:, :], ints[:, :], 15, None, ALU.bitwise_and))
                constants(dve.tensor_scalar(same_expert[:, :], ints[:, :], 0.0, None, ALU.is_equal))
                constants(dve.tensor_scalar(ints2[:, :], ints2[:, :], 4, None, ALU.logical_shift_right))
                constants(dve.tensor_scalar(own_block[:, :], ints2[:, :], 8.0, None, ALU.is_equal))

                PER = 5 + 2 * 6

                def conv_tile(i, n, last):
                    chain = Chain(dve, chain_sem, i * PER + 6)

                    def split(s):
                        strips.split_lo(dve, i * NS + (CONV0 + s), s % 2)

                    def half_work(half):
                        mb = slice(4 * half, 4 * half + 4)
                        f = 3 * half
                        chain(dve.tensor_copy(u[:, :, 0:2], u_carry[:, mb, :]))
                        strips.done(dve, i * NS + (CONV0 + 2 * f + 3))
                        dve.wait_ge(c_read, i * 2 + (half + 1))
                        dve.tensor_tensor(u[:, :, 2:T + 2], bank(GROUP[f + 1]), cgate, ALU.mult).then_inc(u_done, 1)
                        split(2 * f + 5)
                        dve.wait_ge(u_done, i * 2 + (half + 2))
                        dve.wait_ge(v_free, i * 2 + (half + 1))
                        for tap in range(3):
                            for m in range(4):
                                w = taps[:, tap, 4 * half + m:4 * half + m + 1]
                                if tap == 0:
                                    ins = dve.tensor_scalar(cv[:, m, :], u[:, m, 0:T], w, None, ALU.mult)
                                else:
                                    ins = dve.scalar_tensor_tensor(cv[:, m, :], u[:, m, tap:T + tap], w, cv[:, m, :],
                                                                   ALU.mult, ALU.add)
                            chain(ins)
                            if tap == 1:
                                split(2 * f + 6)
                        dve.tensor_copy(u_carry[:, mb, :], u[:, :, T:T + 2])
                        chain(dve.tensor_tensor(cv[:, :, 0], cv[:, :, 0], b_carry[:, mb], ALU.mult))
                        strips.done(dve, i * NS + (CONV0 + 2 * f + 5))
                        b = bank(GROUP[f + 2])
                        dve.tensor_tensor(cv[:, :, 1:T], cv[:, :, 1:T], b[:, :, 0:T - 1], ALU.mult)
                        chain(dve.tensor_copy(b_carry[:, mb], b[:, :, T - 1]))
                        dve.sem_inc(v_done, 1)
                        split(2 * f + 7)

                    split(2)
                    split(3)
                    split(4)
                    if not last:
                        tile_norm(i + 1, chain)
                    half_work(0)
                    split(8)
                    if last:
                        for k in range(KB):
                            dve.wait_ge(v_hi_done, k + 1)
                            dve.tensor_tensor(q_lo[:, k, :], v_tiles[0][:, k, :], q_hi[:, k, :].bitcast(F32),
                                              ALU.subtract).then_inc(v_lo_done, 1)
                    split(9)
                    if not last:
                        tile_lo(i + 1, 1 - n, 0)
                    split(10)
                    half_work(1)
                    if not last:
                        tile_lo(i + 1, 1 - n, 1)
                    assert last or chain.n == PER, chain.n
                tiles_loop(dve, conv_tile)
                chain = Chain(dve, chain_sem, (TILES - 1) * PER + 6 + 12)
                chain(dve.tensor_tensor(last_v, u_carry[:, :, 0], taps[:, 0, :], ALU.mult))
                chain(dve.tensor_tensor(last_t, u_carry[:, :, 1], taps[:, 1, :], ALU.mult))
                chain(dve.tensor_tensor(last_v, last_v, last_t, ALU.add))
                dve.tensor_tensor(last_v, last_v, b_carry, ALU.mult).then_inc(v_done, 1)

                dve.sem_inc(shifted, 1)

                def add_half(n, half):
                    c = slice(T * half, T * half + T)
                    dve.tensor_tensor(tiles[n][:, :, c], bank(half), tiles[n][:, :, c], ALU.add).then_inc(added, 1)

                def rms(chain, count, number):
                    dve.wait_ge(at_squares, count)
                    chain(dve.tensor_tensor(tmp, ss, ss_b, ALU.add))
                    dve.tensor_scalar(var, tmp, 1.0 / D, RMS_EPS, ALU.mult, ALU.add).then_inc(at_var, 1)
                    dve.wait_ge(at_root, number)
                    refine_rstd(dve, chain, TB)

                def scale_rows(n):
                    dve.sem_inc(at_rstd, 1)
                    for t in (0, 1):
                        dve.tensor_scalar(xn[:, t, :], tiles[n][:, t, :], rstd[:, t:t + 1], None, ALU.mult).then_inc(
                            rows_vector, 1)

                strips.split_lo(dve, ATT0 + 2, 0)
                strips.split_lo(dve, ATT0 + 3, 1)
                dve.wait_ge(at_x_loaded, STEP)
                strips.done(dve, ATT0 + 1)
                add_half(0, 0)
                strips.split_lo(dve, ATT0 + 4, 0)
                strips.done(dve, ATT0 + 3)
                add_half(0, 1)
                strips.split_lo(dve, ATT0 + 5, 1)
                rms(Chain(dve, at_chain), 2 * TB, 1)
                scale_rows(0)

                def attend_tile(i, n, last):
                    chain = Chain(dve, at_chain, i * BODY_CHAIN + 6)

                    def split(s):
                        if s < 8 or not last:
                            strips.split_lo(dve, i * NS + (BODY0 + s), s % 2)

                    for k in range(KB):
                        dve.wait_ge(n1_hi, i * KB + (k + 1))
                        dve.scalar_tensor_tensor(act_lo[:, k, :], bank(k // 4, k % 4), gains[:, 1, k:k + 1],
                                                 act_hi[:, k, :].bitcast(F32), ALU.mult, ALU.subtract).then_inc(n1_lo, 1)
                    for half in range(2):
                        split(2 + 2 * half)
                        for m in range(4):
                            dve.wait_ge(qh, i * KB + (4 * half + m + 1))
                            dve.scalar_tensor_tensor(q_lo[:, 4 * half + m, :], bank(half, m), HD ** -0.5,
                                                     q_hi[:, 4 * half + m, :].bitcast(F32), ALU.mult,
                                                     ALU.subtract).then_inc(ql, 1)
                        split(3 + 2 * half)
                    for hd in range(HEADS):
                        dve.wait_ge(scored, i * HEADS + (hd + 1))
                        dve.tensor_reduce(neg_max[:, hd, :], scores_bank(hd), axis=X, op=ALU.max,
                                          negate=True).then_inc(maxed, 1)
                    for hd in range(HEADS):
                        dve.wait_ge(exped, i * HEADS * TB + (hd * TB + TB))
                        chain(dve.reciprocal(sums[:, hd, :], sums[:, hd, :]))
                        dve.tensor_tensor(pr[:, hd, :, :], pr[:, hd, :, :],
                                          sums[:, hd, :].unsqueeze(2).to_broadcast([P, TB, MEM]),
                                          ALU.mult).then_inc(p_done, 1)
                    for m in range(KB):
                        dve.wait_ge(pt_hi, i * KB + (m + 1))
                        dve.tensor_tensor(q_lo[:, m, :], bank(m // 4, m % 4), q_hi[:, m, :].bitcast(F32),
                                          ALU.subtract).then_inc(pt_lo, 1)
                    for m in range(KB):
                        dve.wait_ge(o_hi, i * KB + (m + 1))
                        dve.tensor_tensor(act_lo[:, m, :], bank(m // 4, m % 4), act_hi[:, m, :].bitcast(F32),
                                          ALU.subtract).then_inc(o_lo, 1)
                    if not last:
                        for k in range(KB):
                            dve.wait_ge(v_hi_done, i * KB + (KB + k + 1))
                            dve.tensor_tensor(q_lo[:, k, :], v_tiles[1 - n][:, k, :], q_hi[:, k, :].bitcast(F32),
                                              ALU.subtract).then_inc(v_lo_done, 1)
                    split(6)
                    split(7)
                    strips.done(dve, i * NS + (BODY0 + 5))
                    add_half(n, 0)
                    split(8)
                    strips.done(dve, i * NS + (BODY0 + 7))
                    add_half(n, 1)
                    split(9)
                    rms(chain, i * 16 + 16, i * 2 + 2)
                    for t in range(TB):
                        dve.scalar_tensor_tensor(xn[:, t, :], tiles[n][:, t, :], rstd[:, t:t + 1], gain_row[:, :],
                                                 ALU.mult, ALU.mult).then_inc(rows_vector, 1)
                    split(10)
                    if not last:
                        dve.wait_ge(at_x_loaded, i * STEP + 2 * STEP)
                        strips.done(dve, i * NS + (BODY0 + 9))
                        add_half(1 - n, 0)
                    split(11)
                    for k in range(KB):
                        dve.wait_ge(n3_hi, i * KB + (k + 1))
                        dve.tensor_tensor(act_lo[:, k, :], bank(1 - k // 4, k % 4), act_hi[:, k, :].bitcast(F32),
                                          ALU.subtract).then_inc(n3_lo, 1)
                    split(12)
                    if not last:
                        strips.done(dve, i * NS + (BODY0 + 11))
                        add_half(1 - n, 1)
                        split(13)
                        rms(chain, i * 16 + 24, i * 2 + 3)
                        dve.wait_ge(rows_free, i + 1)
                        scale_rows(1 - n)
                    dve.wait_ge(routed, i + 1)
                    logits = bank(0, 0)[:, 0:TB * E].rearrange("p (t e) -> p t e", t=TB)
                    rt = r_tmp.rearrange("p (t e) -> p t e", t=TB)
                    chain(dve.tensor_reduce(r_max, logits, axis=X, op=ALU.max))
                    dve.tensor_tensor(rt, logits, r_max.unsqueeze(2).to_broadcast([P, TB, E]),
                                      ALU.subtract).then_inc(shifted, 1)
                    dve.wait_ge(r_exp, i + 1)
                    chain(dve.tensor_reduce(r_sum, rt, axis=X, op=ALU.add))
                    chain(dve.reciprocal(r_sum, r_sum))
                    chain(dve.tensor_tensor(rt, rt, r_sum.unsqueeze(2).to_broadcast([P, TB, E]), ALU.mult))
                    chain(dve.tensor_copy(probs[:, bass.ds(i * TB * E, TB * E)], r_tmp))
                    dve.sem_inc(probs_done, 1)
                    assert last or chain.n == BODY_CHAIN, chain.n
                tiles_loop(dve, attend_tile)

            @block.tensor
            def _(pe):
                strips.open(pe=pe)
                pe.wait_ge(consts_made, 1)
                pe.wait_ge(mem_done, MB)
                for k in range(KB):
                    for t in range(MB):
                        ins = pe.transpose(bank(k // 4, k % 4)[:, t * P:(t + 1) * P], memx[:, t, k * P:(k + 1) * P],
                                           ident[:, :])
                    if k % 4 == 3:
                        ins.then_inc(filled, 1)
                for half in range(4):
                    pe.wait_ge(kv_lo, (4, KB, KB + 1, KB + 2)[half])
                    for kh in range(2):
                        g = 2 * half + kh
                        strips.ready(pe, g)
                        pe.wait_ge(kv_lo, max(4 * kh + 4, 4 + 4 * min(half, 1)))
                        hi, lo = strips.views(g % 2, 4)
                        for m in range(4 if half < 2 else MB):
                            for k in range(4):
                                kk = 4 * kh + k
                                if half < 2:
                                    f = slice(m * P, (m + 1) * P)
                                    ins = product(pe, bank(half % 2, m)[:, 0:MEM], (hi[:, k, f], lo[:, k, f]),
                                                  (act_hi[:, kk, 0:MEM], act_lo[:, kk, 0:MEM]), kk == 0, kk == KB - 1)
                                else:
                                    t = slice(m * P, (m + 1) * P)
                                    ins = product(pe, bank(half % 2, m), (act_hi[:, kk, t], act_lo[:, kk, t]),
                                                  (hi[:, k, :], lo[:, k, :]), kk == 0, kk == KB - 1)
                        ins.then_inc(strips.used, 1)

                def turn_x(half):
                    for k in range(4 * half, 4 * half + 4):
                        for t in range(TB):
                            ins = pe.transpose(bank(half, k % 4)[:, t * P:(t + 1) * P], xt[:, t, k * P:(k + 1) * P],
                                               ident[:, :])
                    ins.then_inc(transposed, 1)

                pe.wait_ge(xs_done, TB)
                pe.wait_ge(kv_lo, KB + 3)
                turn_x(0)
                pe.wait_ge(kv_lo, KB + 4)
                turn_x(1)

                def columns(group, first, pair, wait_data):
                    for kh in range(2):
                        strips.ready(pe, first + kh)
                        wait_data(kh)
                        hi, lo = strips.views(kh, 4)
                        for m in range(4):
                            c = slice(m * P, (m + 1) * P)
                            for k in range(4):
                                kk = 4 * kh + k
                                ins = product(pe, bank(group, m), (hi[:, k, c], lo[:, k, c]),
                                              (pair[0][:, kk, :], pair[1][:, kk, :]), kk == 0, kk == KB - 1)
                        ins.then_inc(strips.used, 1)

                def conv_tile(i, n, last):
                    for f in range(6):
                        half, part = f // 3, f % 3
                        if f == 0:
                            pe.wait_ge(v_done, i * 2 + 1)
                            pe.wait_ge(xn_lo, i * KB + 4)
                        elif f == 1:
                            pe.wait_ge(xn_lo, i * KB + 8)
                        elif f == 5 and not last:
                            pe.wait_ge(xn_lo, i * KB + (KB + 4))
                        elif part == 2:
                            pe.wait_ge(c_read, i * 2 + 1)
                            if f == 5:
                                pe.wait_ge(v_done, i * 2 + 2)
                        elif part == 0:
                            pe.wait_ge(u_done, i * 2 + 2)
                        else:
                            pe.wait_ge(c_read, i * 2 + 2)

                        def normed(kh):
                            if f == 0:
                                pe.wait_ge(xn_lo, i * KB + (4 * kh + 4))
                        columns(GROUP[f], i * NS + (CONV0 + 2 * f), pairs[n], normed)
                        if f == 3 and not last:
                            pe.wait_ge(xs_done, i * TB + 2 * TB)
                            pe.wait_ge(v_done, i * 2 + 2)
                            turn_x(0)
                        if f == 5 and not last:
                            pe.wait_ge(u_done, i * 2 + 3)
                            turn_x(1)
                tiles_loop(pe, conv_tile)

                def turn_rows(half, group):
                    for k in range(4 * half, 4 * half + 4):
                        for t in range(TB):
                            ins = pe.transpose(bank(group, k % 4)[:, t * P:(t + 1) * P],
                                               xn[:, t, k * P:(k + 1) * P], ident[:, :])
                    ins.then_inc(turned, 1)

                def rows_out(first, pair, half, wait_data):
                    for kh in range(2):
                        strips.ready(pe, first + kh)
                        hi, lo = strips.views(kh, 4)
                        for t in range(TB):
                            c = slice(t * P, (t + 1) * P)
                            for k in range(4):
                                kk = 4 * kh + k
                                if half == 0 and t == 0:
                                    wait_data(kk)
                                ins = product(pe, bank(half, t), (pair[0][:, kk, c], pair[1][:, kk, c]),
                                              (hi[:, k, :], lo[:, k, :]), kk == 0, kk == KB - 1)
                        ins.then_inc(strips.used, 1)

                pe.wait_ge(v_done, 2 * TILES + 1)
                rows_out(ATT0, (q_hi, q_lo), 0, lambda kk: pe.wait_ge(v_lo_done, kk + 1))
                pe.wait_ge(u_done, 2 * TILES + 1)
                rows_out(ATT0 + 2, (q_hi, q_lo), 1, None)

                def attend_tile(i, n, last):
                    first = i * NS + BODY0
                    pe.wait_ge(rows_vector, i * 6 + 2)
                    pe.wait_ge(rows_scalar, i * 2 + 2)
                    pe.wait_ge(shifted, i + 1)
                    turn_rows(0, 0)
                    pe.wait_ge(added, i * 4 + 2)
                    turn_rows(1, 1)
                    for half in range(2):
                        pe.wait_ge(n1_lo, i * KB + (4 * half + 4))
                        columns(half, first + 2 * half, (act_hi, act_lo),
                                lambda kh: pe.wait_ge(n1_lo, i * KB + (max(4 * kh, 4 * half) + 4)))
                    for hd in range(HEADS):
                        if hd % 2 == 0:
                            pe.wait_ge(ql, i * KB + (4 * (hd // 2) + 4))
                        sc = scores_bank(hd)
                        for t in range(TB):
                            c = slice(t * P, (t + 1) * P)
                            for b in range(HB):
                                m = HB * hd + b
                                ins = product(pe, sc[:, t, :], (q_hi[:, m, c], q_lo[:, m, c]),
                                              (k_hi[:, m, :], k_lo[:, m, :]), b == 0, b == HB - 1)
                        ins.then_inc(scored, 1)
                    for hd in range(HEADS):
                        if hd % 2 == 0:
                            pe.wait_ge(exped, i * HEADS * TB + (hd + 2) * TB)
                        pe.wait_ge(p_done, i * HEADS + (hd + 1))
                        for m in range(MB):
                            for t in range(TB):
                                ins = pe.transpose(bank(hd // 2, MB * (hd % 2) + m)[:, t * P:(t + 1) * P],
                                                   pr[:, hd, t, m * P:(m + 1) * P], ident[:, :])
                        if hd % 2 == 1:
                            ins.then_inc(turned, 1)
                    for hd in range(HEADS):
                        if hd % 2 == 0:
                            pe.wait_ge(pt_lo, i * KB + (4 * (hd // 2) + 4))
                        for b in range(HB):
                            c = slice(hd * HD + b * P, hd * HD + (b + 1) * P)
                            for m in range(MB):
                                ins = product(pe, bank(hd // 2, HB * (hd % 2) + b), (v_hi[:, m, c], v_lo[:, m, c]),
                                              (q_hi[:, MB * hd + m, :], q_lo[:, MB * hd + m, :]), m == 0, m == MB - 1)
                        if hd % 2 == 1:
                            ins.then_inc(valued, 1)
                    pe.wait_ge(o_lo, i * KB + 4)
                    rows_out(first + 4, (act_hi, act_lo), 0, lambda kk: pe.wait_ge(o_lo, i * KB + (kk + 1)))
                    rows_out(first + 6, (act_hi, act_lo), 1, None)
                    if not last:
                        pe.wait_ge(added, i * 4 + 3)
                        rows_out(first + 8, (q_hi, q_lo), 0, lambda kk: pe.wait_ge(v_lo_done, i * KB + (KB + kk + 1)))
                    pe.wait_ge(added, i * 4 + 4)
                    pe.wait_ge(rows_vector, i * 6 + 6)
                    turn_rows(0, 1)
                    if not last:
                        pe.wait_ge(added, i * 4 + 5)
                    turn_rows(1, 0)
                    if not last:
                        pe.wait_ge(n3_lo, i * KB + 4)
                        rows_out(first + 10, (q_hi, q_lo), 1, None)
                    pe.wait_ge(n3_lo, i * KB + KB)
                    for t in range(TB):
                        c = slice(t * P, (t + 1) * P)
                        for k in range(KB):
                            ins = product(pe, bank(0, 0)[:, t * E:(t + 1) * E], (act_hi[:, k, c], act_lo[:, k, c]),
                                          (r_hi[:, k, :], r_lo[:, k, :]), k == 0, k == KB - 1)
                    ins.then_inc(routed, 1)
                tiles_loop(pe, attend_tile)
        pctx.close()

    def select():
        pctx = ExitStack()
        sem = lambda name: pctx.enter_context(nc.semaphore(name))
        BITS = 30
        NT = SEQ // P
        BIG = 4096.0
        turned, counted, totalled, bit_step, chain_sem = (
            sem("sl_turned"), sem("counted"), sem("totalled"), sem("bit_step"), sem("sl_chain"))
        spread_in, spread, masks_done, prefixed, hots_done, listed = (
            sem("spread_in"), sem("spread"), sem("masks_done"), sem("prefixed"), sem("hots_done"), sem("listed"))
        z_done, z_stored, z_loaded, z_turned = sem("z_done"), sem("z_stored"), sem("z_loaded"), sem("z_turned")
        by_expert = vin[:, 0:256]
        compared = vin[:, 256:512]
        count = stat[:, 24:25]
        words = ints[:, 0:4].bitcast(U32)
        thr, cand, bit, take = (words[:, n:n + 1] for n in range(4))
        spread_rhs = vin[:, 512:528]
        thr_row = vin[:, 528:544]
        above_total = vin[:, 544:560]
        masks = vin[:, 1024:1536].rearrange("p (s t e) -> p s t e", s=2, t=NT)
        before = h[:, 0:2 * (NT + 1) * E].rearrange("p (t s e) -> p t s e", t=NT + 1, s=2)
        a1 = vin[:, 1536:1792]
        b1 = vin[:, 1792:2048]
        pos = h[:, 1024:1280].bitcast(I32)
        low = h[:, 1280:1536].bitcast(I32)
        high = h[:, 1536:1792].bitcast(I32)
        hot = xs[:, :].rearrange("p (n b) -> p n b", b=E)
        hot_high = q_hi[:, :, :].rearrange("p k c -> p (k c)")
        hot_low = q_lo[:, :, :].rearrange("p k c -> p (k c)")
        z_all = vin[:, 2048:2304].rearrange("p (h n) -> p h n", h=2)
        z = vin[:, 2304:2336].rearrange("p (h b) -> p h b", h=2)
        lists = h[0:E * CB, 2048:2048 + P]
        flat = index_d.rearrange("e c -> (e c)")
        prefix = bank(0, 1)
        with nc.Block() as block:
            @block.sync
            def _(sp):
                sp.wait_ge(z_done, 1)
                sp.dma_start(flat.rearrange("(h r b) -> r h b", h=2, b=E), z).then_inc(z_stored, STEP)
                sp.wait_ge(z_stored, STEP)
                sp.dma_start(lists, flat.rearrange("(r c) -> r c", c=P)).then_inc(z_loaded, STEP)

            @block.tensor
            def _(pe):
                for n in range(2):
                    last = pe.transpose(bank(0, 0)[:, n * P:(n + 1) * P], probs[:, n * P:(n + 1) * P], ident[:, :])
                last.then_inc(turned, 1)
                with pe.Fori(0, BITS) as b:
                    pe.wait_ge(counted, b + 1)
                    pe.matmul(bank(1, 0)[:, 0:1], same_expert[:, :], count, start=True, stop=True).then_inc(totalled, 1)
                pe.wait_ge(spread_in, 1)
                pe.matmul(bank(1, 1)[:, 0:E], ones[:, :], spread_rhs, start=True, stop=True).then_inc(spread, 1)
                pe.wait_ge(masks_done, 1)
                pe.matmul(prefix, upper[:, :], masks.rearrange("p s t e -> p (s t e)"), start=True, stop=False)
                pe.matmul(prefix.rearrange("p (s t e) -> p s t e", s=2, t=NT)[:, 0, :, :], ones[:, :],
                          before[:, 0:NT, 0, :], start=False, stop=False)
                pe.matmul(prefix.rearrange("p (s t e) -> p s t e", s=2, t=NT)[:, 1, :, :], ones[:, :],
                          before[:, 0:NT, 1, :], start=False, stop=True)
                pe.matmul(bank(1, 2)[:, 0:E], ones[:, :], before[:, NT, 0, :], start=True, stop=True).then_inc(prefixed, 1)
                pe.wait_ge(hots_done, 1)
                for half in range(2):
                    for t in range(NT):
                        c = slice(t * 256 + half * P, t * 256 + half * P + P)
                        c2 = [slice((t * E + 8 * half) * E, (t * E + 8 * half + 8) * E)]
                        last = pe.matmul(bank(0, 2 + half)[:, 0:P], hot_high[:, c2[0]], hot_low[:, c2[0]],
                                         start=t == 0, stop=t == NT - 1)
                last.then_inc(listed, 1)
                pe.wait_ge(z_loaded, STEP)
                pe.transpose(bank(1, 3)[:, 0:E * CB], lists, ident[0:E * CB, 0:E * CB]).then_inc(z_turned, 1)

            @block.vector
            def _(dve):
                chain = Chain(dve, chain_sem)
                chain(dve.memset(words, 0))
                chain(dve.memset(bit, 1 << (BITS - 1)))
                chain(dve.memset(cand, 1 << (BITS - 1)))
                dve.wait_ge(turned, 1)
                chain(dve.tensor_copy(by_expert, bank(0, 0)[:, 0:256]))
                with dve.Fori(0, BITS) as b:
                    dve.tensor_scalar(compared, by_expert, cand.bitcast(F32), None, ALU.is_ge, ALU.add,
                                      accum_out=count).then_inc(counted, 1)
                    dve.tensor_scalar(bit, bit, 1, None, ALU.logical_shift_right).then_inc(bit_step, 1)
                    dve.wait_ge(totalled, b + 1)
                    dve.tensor_scalar(take, bank(1, 0)[:, 0:1], CAP - 0.5, None, ALU.is_ge).then_inc(bit_step, 1)
                    dve.wait_ge(bit_step, b * 4 + 2)
                    apart(dve, spare)
                    dve.copy_predicated(thr, take, cand).then_inc(bit_step, 1)
                    dve.wait_ge(bit_step, b * 4 + 3)
                    dve.tensor_tensor(cand, thr, bit, ALU.bitwise_or).then_inc(bit_step, 1)
                    dve.wait_ge(bit_step, b * 4 + 4)
                dve.tensor_scalar(spread_rhs, ident[:, 0:E], thr.bitcast(F32), None, ALU.mult).then_inc(spread_in, 1)
                chain(dve.memset(before[:, 0, :, :], 0.0))
                dve.wait_ge(spread, 1)
                chain(dve.tensor_copy(thr_row, bank(1, 1)[:, 0:E]))
                by_token = probs[:, :].rearrange("p (t e) -> p t e", e=E)
                row = thr_row.unsqueeze(1).to_broadcast([P, NT, E])
                dve.tensor_tensor(masks[:, 0, :, :], by_token, row, ALU.is_gt)
                chain(dve.tensor_tensor(masks[:, 1, :, :], by_token, row, ALU.is_equal))
                for t in range(NT):
                    chain(dve.tensor_tensor(before[:, t + 1, :, :], before[:, t, :, :], masks[:, :, t, :], ALU.add))
                dve.sem_inc(masks_done, 1)
                dve.wait_ge(prefixed, 1)
                above = masks[:, 0, :, :].rearrange("p t e -> p (t e)")
                equal = masks[:, 1, :, :].rearrange("p t e -> p (t e)")
                chain(dve.tensor_copy(above_total, bank(1, 2)[:, 0:E]))
                dve.scalar_tensor_tensor(a1, prefix[:, 0:256], -BIG, above, ALU.add, ALU.mult)
                chain(dve.tensor_tensor(b1.rearrange("p (t e) -> p t e", e=E),
                                        prefix[:, 256:512].rearrange("p (t e) -> p t e", e=E),
                                        above_total.unsqueeze(1).to_broadcast([P, NT, E]), ALU.add))
                chain(dve.scalar_tensor_tensor(b1, b1, -BIG, equal, ALU.add, ALU.mult))
                chain(dve.scalar_tensor_tensor(pos, a1, BIG, b1, ALU.add, ALU.add))
                dve.tensor_scalar(low, pos, 15, None, ALU.bitwise_and)
                chain(dve.tensor_scalar(high, pos, 4, None, ALU.logical_shift_right))
                ramps = ramp[:, :].unsqueeze(1).to_broadcast([P, NT * E, E])
                dve.tensor_tensor(hot_high.rearrange("p (n a) -> p n a", a=E),
                                  high.unsqueeze(2).to_broadcast([P, NT * E, E]), ramps, ALU.is_equal)
                chain(dve.tensor_tensor(hot, low.unsqueeze(2).to_broadcast([P, NT * E, E]), ramps, ALU.is_equal))
                chain(dve.tensor_tensor(hot_low.rearrange("p (t n) -> p t n", t=NT),
                                        xs[:, :].rearrange("p (t n) -> p t n", t=NT),
                                        token_id[:, :].unsqueeze(2).to_broadcast([P, NT, E * E]), ALU.mult))
                dve.sem_inc(hots_done, 1)
                dve.wait_ge(listed, 1)
                for half in range(2):
                    chain(dve.tensor_tensor(z_all[:, half, :], bank(0, 2 + half)[:, 0:P], own_block[:, :], ALU.mult))
                    chain(dve.tensor_reduce(z[:, half, :], z_all[:, half, :].rearrange("p (e b) -> p b e", b=E),
                                            axis=X, op=ALU.add))
                dve.sem_inc(z_done, 1)
                dve.wait_ge(z_turned, 1)
                chain(dve.tensor_copy(index[:, :], bank(1, 3)[:, 0:E * CB]))
        pctx.close()

    def experts():
        pctx = ExitStack()
        sem = lambda name: pctx.enter_context(nc.semaphore(name))
        strips = Strips(nc, pctx, "experts", w_raw, w_hi, w_lo)
        NS = 12
        NF = 8
        gathered = [sem("gathered0"), sem("gathered1")]
        index_step, scattered, y_free = sem("index_step"), sem("scattered"), sem("y_free")
        turned, freed = sem("ex_turned"), sem("ex_freed")
        x_hi, low_copied, silu_done, hid_done, hid_hi_done, hid_lo_done, aff_done = (
            sem("ex_x_hi"), sem("low_copied"), sem("silu_done"), sem("hid_done"), sem("hid_hi_done"),
            sem("hid_lo_done"), sem("aff_done"))
        RW = CB * ROW
        xg = [t[:, 0:RW].rearrange("p (c r) -> p c r", c=CB) for t in (h, vin)]
        xt = [act_hi, act_lo]
        hid_hi = q_hi[:, :, 0:CAP]
        hid_lo = q_lo[:, :, 0:CAP]
        low_half = h[:, RW:RW + 4 * CAP].rearrange("p (b c) -> p b c", b=4)
        sums = vin[:, RW:RW + 4 * CAP].rearrange("p (b c) -> p b c", b=4)
        silu = h[:, RW + 4 * CAP:RW + 6 * CAP].rearrange("p (b c) -> p b c", b=2)
        hid = vin[:, RW + 4 * CAP:RW + 6 * CAP].rearrange("p (b c) -> p b c", b=2)
        y = [xs[:, n * CB * D:(n + 1) * CB * D].rearrange("p (c d) -> p c d", c=CB) for n in range(2)]
        aff = stat[:, 24:24 + CB]
        gather_index = [indices[:, 2 * n:2 * n + 2] for n in range(2)]
        scatter_index = [indices[:, 4 + 2 * n:6 + 2 * n] for n in range(2)]
        wg = w_gate[0].rearrange("e (k p) n -> p e k n", p=P)
        wu = w_up[0].rearrange("e (k p) n -> p e k n", p=P)
        wd = w_down[0].rearrange("e (k p) n -> p e k n", p=P)

        def turned_rows(j):
            return bank(0)[:, 2 * j:2 * j + 2, :].rearrange("p b (t c) -> p (b t) c", c=CAP)

        with nc.Block() as block:
            @block.sync
            def _(sp):
                with sp.Fori(0, E) as e:
                    ex = bass.ds(e, 1)
                    for s in range(NS):
                        if s < 8:
                            w, c = (wg, wu)[s % 2], s // 2 * 256
                            source, blocks = w[:, ex, :, c:c + 256].rearrange("p e k n -> p (e k) n"), KB
                        else:
                            half, kh = s % 2, (s - 8) // 2
                            source = wd[:, ex, 4 * kh:4 * kh + 4, T * half:T * half + T].rearrange("p e k n -> p (e k) n")
                            blocks = 4
                        strips.load(sp, e * NS + s, s % 2, source, blocks)

            @block.gpsimd
            def _(pool):
                strips.open(pool=pool)
                pool.sem_inc(y_free, 1)

                def gather(n):
                    for c in range(CB):
                        pool.indirect_dma_start(xg[n][:, c, :], None, row_d, bass.IndirectOffsetOnAxis(
                            ap=gather_index[n][:, c:c + 1], axis=0)).then_inc(gathered[n], STEP)

                for c in range(CB):
                    pool.dma_start(primed[:, c, :], row_d[0:16, 0:16]).then_inc(scattered, STEP)
                for n in range(2):
                    pool.tensor_copy(gather_index[n], index[:, CB * n:CB * n + CB]).then_inc(index_step, 1)
                pool.wait_ge(index_step, 2)
                for n in range(2):
                    gather(n)
                for n in range(2):
                    strips.split_lo_pool(pool, n, n)

                def expert(e, n, steps, fills, has_next, has_second):
                    for s in range(2, NS + 2 if has_next else NS):
                        strips.split_lo_pool(pool, e * NS + s, s % 2)
                    pool.tensor_copy(scatter_index[n], index[:, bass.ds(e * CB, CB)]).then_inc(index_step, 1)
                    pool.wait_ge(index_step, steps + 1)
                    pool.wait_ge(freed, fills)
                    pool.wait_ge(scattered, e * CB * STEP + CB * STEP)
                    pool.sem_inc(y_free, 1)
                    for c in range(CB):
                        pool.indirect_dma_start(sum_d, bass.IndirectOffsetOnAxis(ap=scatter_index[n][:, c:c + 1], axis=0),
                                                y[n][:, c, :], None, compute_op=ALU.add).then_inc(scattered, STEP)
                    if has_second:
                        pool.tensor_copy(gather_index[n], index[:, bass.ds(e * CB + 2 * CB, CB)]).then_inc(index_step, 1)
                        pool.wait_ge(index_step, steps + 2)
                        apart(pool, spare)
                        gather(n)

                with pool.Fori(0, E // 2 - 1) as i:
                    for n in range(2):
                        e = i * 2 + n
                        expert(e, n, e * 2 + 2, e * NF + NF + 2, True, True)
                expert(E - 2, 0, 2 * E - 2, (E - 1) * NF + 2, True, False)
                expert(E - 1, 1, 2 * E - 1, E * NF, False, False)
                pool.wait_ge(scattered, E * CB * STEP + CB * STEP)

            @block.scalar
            def _(act):
                def turn_hi(n, at):
                    for j in range(2):
                        act.wait_ge(turned, at + j + 1)
                        act.activation(xt[n][:, 4 * j:4 * j + 4, 0:CAP], turned_rows(j), ACT.Copy).then_inc(x_hi, 1)

                def split(e, s):
                    g = e * NS + s
                    strips.split_hi(act, g, s % 2)

                def expert(e, n, has_next):
                    for f in range(4):
                        split(e, 2 * f + 2)
                        strips.done(act, e * NS + 2 * f + 1)
                        act.activation(low_half, bank(f % 2)[:, :, CAP:2 * CAP], ACT.Copy).then_inc(low_copied, 1)
                        split(e, 2 * f + 3)
                        act.wait_ge(freed, e * NF + f + 3)
                        act.activation(silu, sums[:, 0:2, :], ACT.Silu).then_inc(silu_done, 1)
                        act.wait_ge(hid_done, e * 4 + f + 1)
                        act.activation(hid_hi[:, 2 * f:2 * f + 2, :], hid, ACT.Copy).then_inc(hid_hi_done, 1)
                    if has_next:
                        turn_hi(1 - n, e * 2 + 2)
                    split(e, 10)
                    split(e, 11)
                    if has_next:
                        split(e, 12)
                        split(e, 13)

                split(0, 0)
                split(0, 1)
                turn_hi(0, 0)
                with act.Fori(0, E // 2 - 1) as i:
                    for n in range(2):
                        expert(i * 2 + n, n, True)
                expert(E - 2, 0, True)
                expert(E - 1, 1, False)

            @block.vector
            def _(dve):
                strips.open(dve=dve)

                def turn_lo(n, at):
                    for j in range(2):
                        dve.wait_ge(x_hi, at + j + 1)
                        dve.tensor_tensor(xt[n][:, 4 * j:4 * j + 4, CAP:2 * CAP], turned_rows(j),
                                          xt[n][:, 4 * j:4 * j + 4, 0:CAP].bitcast(F32), ALU.subtract).then_inc(freed, 1)

                def split(e, s):
                    strips.split_lo(dve, e * NS + s, s % 2)

                def expert(e, n, has_next):
                    for f in range(4):
                        split(e, 2 * f + 2)
                        dve.wait_ge(low_copied, e * 4 + f + 1)
                        dve.tensor_tensor(sums, bank(f % 2)[:, :, 0:CAP], low_half, ALU.add).then_inc(freed, 1)
                        split(e, 2 * f + 3)
                        dve.wait_ge(silu_done, e * 4 + f + 1)
                        dve.tensor_tensor(hid, silu, sums[:, 2:4, :], ALU.mult).then_inc(hid_done, 1)
                        dve.wait_ge(hid_hi_done, e * 4 + f + 1)
                        dve.tensor_tensor(hid_lo[:, 2 * f:2 * f + 2, :], hid,
                                          hid_hi[:, 2 * f:2 * f + 2, :].bitcast(F32), ALU.subtract).then_inc(hid_lo_done, 1)
                    if has_next:
                        turn_lo(1 - n, e * 2 + 2)
                    dve.tensor_copy(aff.rearrange("p (c o) -> p c o", o=1),
                                    xg[n][:, :, bass.ds(e + D, 1)]).then_inc(aff_done, 1)
                    dve.wait_ge(aff_done, e + 1)
                    split(e, 10)
                    split(e, 11)
                    if has_next:
                        split(e, 12)
                    dve.wait_ge(y_free, e + 1)
                    for half in range(2):
                        strips.done(dve, e * NS + 10 + half)
                        for c in range(CB):
                            ins = dve.tensor_scalar(y[n][:, c, T * half:T * half + T], bank(1, 2 * half + c), aff[:, c:c + 1],
                                                    None, ALU.mult)
                        ins.then_inc(freed, 1)
                    if has_next:
                        split(e, 13)

                split(0, 0)
                split(0, 1)
                turn_lo(0, 0)
                with dve.Fori(0, E // 2 - 1) as i:
                    for n in range(2):
                        expert(i * 2 + n, n, True)
                expert(E - 2, 0, True)
                expert(E - 1, 1, False)

            @block.tensor
            def _(pe):
                strips.open(pe=pe)

                def turn(n, wait_rows, at):
                    wait_rows()
                    if at is not None:
                        pe.wait_ge(freed, at)
                    for j in range(2):
                        for k in range(4 * j, 4 * j + 4):
                            for c in range(CB):
                                last = pe.transpose(turned_rows(j)[:, k - 4 * j, c * P:(c + 1) * P],
                                                    xg[n][:, c, k * P:(k + 1) * P], ident[:, :])
                        last.then_inc(turned, 1)

                def expert(e, n, gathers, has_next):
                    for f in range(4):
                        pe.wait_ge(freed, e * NF + f + 1)
                        for part in range(2):
                            s = 2 * f + part
                            strips.ready(pe, e * NS + s)
                            hi, lo = strips.views(s % 2, KB)
                            for m in range(2):
                                o = bank(f % 2, 2 * part + m)
                                c = slice(m * P, (m + 1) * P)
                                for k in range(KB):
                                    pe.matmul(o, hi[:, k, c], xt[n][:, k, :], start=k == 0, stop=False)
                                    last = pe.matmul(o[:, 0:CAP], lo[:, k, c], xt[n][:, k, 0:CAP], start=False,
                                                     stop=k == KB - 1)
                            last.then_inc(strips.used, 1)
                    if has_next:
                        turn(1 - n, gathers, e * NF + 5)
                    pe.wait_ge(freed, e * NF + 6)
                    for kh in range(2):
                        pe.wait_ge(hid_lo_done, e * 4 + 2 * kh + 2)
                        for half in range(2):
                            s = 8 + half + 2 * kh
                            strips.ready(pe, e * NS + s)
                            hi, lo = strips.views(s % 2, 4)
                            for c in range(CB):
                                t = slice(c * P, (c + 1) * P)
                                for k in range(4):
                                    kk = 4 * kh + k
                                    last = product(pe, bank(1, 2 * half + c), (hid_hi[:, kk, t], hid_lo[:, kk, t]),
                                                   (hi[:, k, :], lo[:, k, :]), kk == 0, kk == FB - 1)
                            last.then_inc(strips.used, 1)

                turn(0, lambda: pe.wait_ge(gathered[0], CB * STEP), None)
                pe.wait_ge(freed, 2)
                with pe.Fori(0, E // 2 - 1) as i:
                    expert(i * 2, 0, lambda: pe.wait_ge(gathered[1], i * CB * STEP + CB * STEP), True)
                    expert(i * 2 + 1, 1, lambda: pe.wait_ge(gathered[0], i * CB * STEP + 2 * CB * STEP), True)
                expert(E - 2, 0, lambda: pe.wait_ge(gathered[1], E // 2 * CB * STEP), True)
                expert(E - 1, 1, None, False)
        pctx.close()

    def final():
        pctx = ExitStack()
        sem = lambda name: pctx.enter_context(nc.semaphore(name))
        loaded = [sem("fn_loaded0"), sem("fn_loaded1")]
        stored = [sem("fn_stored0"), sem("fn_stored1")]
        gain_loaded, squares, var_done, root_done, chain_sem, normed = (
            sem("fn_gain"), sem("fn_squares"), sem("fn_var"), sem("fn_root"), sem("fn_chain"), sem("fn_normed"))
        tiles = [t[:, :].rearrange("p (t d) -> p t d", t=TB) for t in (h, xs)]
        sum_v = sum_d.rearrange("(i t p) d -> i p t d", p=P, t=TB)
        out_v = out[0].rearrange("(i t p) d -> i p t d", p=P, t=TB)
        with nc.Block() as block:
            @block.sync
            def _(sp):
                sp.dma_start(gain_row[:, :], norm_final.rearrange("(o d) -> o d", o=1).to_broadcast([P, D])).then_inc(
                    gain_loaded, STEP)
                for i in range(TILES):
                    if i >= 2:
                        sp.wait_ge(stored[i % 2], STEP * (i // 2))
                    sp.dma_start(tiles[i % 2], sum_v[i]).then_inc(loaded[i % 2], STEP)

            @block.scalar
            def _(act):
                for i in range(TILES):
                    act.wait_ge(loaded[i % 2], STEP * (i // 2 + 1))
                    for t in range(TB):
                        act.activation(junk[:, t, :], tiles[i % 2][:, t, :], ACT.Square,
                                       accum_out=ss[:, t:t + 1]).then_inc(squares, 1)
                    act.wait_ge(var_done, i + 1)
                    act.activation(root, var, ACT.Sqrt).then_inc(root_done, 1)
                    act.wait_ge(normed, TB * (i + 1))
                    act.dma_start(out_v[i], tiles[i % 2]).then_inc(stored[i % 2], STEP)
                for n in range(2):
                    act.wait_ge(stored[n], STEP * TILES // 2)

            @block.vector
            def _(dve):
                dve.wait_ge(gain_loaded, STEP)
                for i in range(TILES):
                    chain = Chain(dve, chain_sem, 5 * i)
                    dve.wait_ge(squares, TB * (i + 1))
                    dve.tensor_scalar(var, ss, 1.0 / D, RMS_EPS, ALU.mult, ALU.add).then_inc(var_done, 1)
                    dve.wait_ge(root_done, i + 1)
                    refine_rstd(dve, chain, TB)
                    for t in range(TB):
                        dve.scalar_tensor_tensor(tiles[i % 2][:, t, :], tiles[i % 2][:, t, :], rstd[:, t:t + 1],
                                                 gain_row[:, :], ALU.mult, ALU.mult).then_inc(normed, 1)
        pctx.close()

    front()
    select()
    experts()
    final()
    ctx.close()


_INS = ["x", "mem", "norm_mix", "norm_xattn", "norm_mem", "norm_ffn", "norm_final", "conv_w_in", "conv_w",
        "conv_w_out", "xattn_w_q", "xattn_w_kv", "xattn_w_o", "moe_router", "moe_w_gate", "moe_w_up", "moe_w_down"]


def kernel(**inputs):
    import numpy as np
    import concourse.bacc as bacc
    from concourse.bass_utils import run_bass_kernel_spmd

    nc = bacc.Bacc("TRN2", target_bir_lowering=False, num_devices=1)
    arrays, args = {}, []
    for name in _INS:
        a = np.ascontiguousarray(inputs[name])
        arrays[f"in_{name}"] = a
        args.append(nc.dram_tensor(f"in_{name}", a.shape, mybir.dt.from_np(a.dtype), kind="ExternalInput").ap())
    out = nc.dram_tensor("out", (1, SEQ, D), F32, kind="ExternalOutput").ap()
    build(nc, *args, out)
    return run_bass_kernel_spmd(nc, [arrays], core_ids=[0]).results[0]["out"]
```

```python
from contextlib import ExitStack

import concourse.bass as bass
from concourse import mybir

F32 = mybir.dt.float32
F32R = mybir.dt.float32r
BF16 = mybir.dt.bfloat16
I32 = mybir.dt.int32
U32 = mybir.dt.uint32
ALU = mybir.AluOpType
ACT = mybir.ActivationFunctionType
X = mybir.AxisListType.X

P = 128
D = 1024
SEQ = 2048
KB = D // P
T = 512
TB = T // P
TILES = SEQ // T
MEM = 256
MB = MEM // P
HEADS = 4
HD = D // HEADS
HB = HD // P
E = 16
CAP = 2 * SEQ // E
CB = CAP // P
FF = 1024
FB = FF // P
RMS_EPS = 1e-6
ROW = D + E
STRIP = 2048
POOL_PART = 512
STEP = 16
CONV_COLS = SEQ + 1


class Strips:

    def __init__(self, nc, ctx, name, raw, hi, lo):
        self.raw, self.hi, self.lo = raw, hi, lo
        self.loaded = [ctx.enter_context(nc.semaphore(f"{name}_strip_loaded{i}")) for i in range(2)]
        self.hi_done = ctx.enter_context(nc.semaphore(f"{name}_strip_hi"))
        self.lo_vector = ctx.enter_context(nc.semaphore(f"{name}_strip_lo_vector"))
        self.lo_pool = ctx.enter_context(nc.semaphore(f"{name}_strip_lo_pool"))
        self.used = ctx.enter_context(nc.semaphore(f"{name}_strip_used"))

    def load(self, sp, g, slot, source, blocks, spare=None):
        sp.wait_ge(self.lo_vector, g + 1)
        sp.wait_ge(self.lo_pool, g + 1)
        if spare is not None:
            apart(sp, spare)
        sp.dma_start(self.raw[:, slot, :].rearrange("p (k n) -> p k n", k=blocks), source).then_inc(
            self.loaded[slot], STEP)

    def split_hi(self, act, g, slot):
        act.wait_ge(self.loaded[slot], g * (STEP // 2) + (STEP - slot * STEP // 2))
        act.wait_ge(self.used, g + 1)
        act.activation(self.hi[:, slot, :], self.raw[:, slot, :], ACT.Copy).then_inc(self.hi_done, 1)

    def split_lo(self, dve, g, slot):
        dve.wait_ge(self.hi_done, g + 1)
        a = STRIP - POOL_PART
        dve.tensor_tensor(self.lo[:, slot, 0:a], self.raw[:, slot, 0:a], self.hi[:, slot, 0:a].bitcast(F32),
                          ALU.subtract).then_inc(self.lo_vector, 1)

    def split_lo_pool(self, pool, g, slot):
        pool.wait_ge(self.hi_done, g + 1)
        a = STRIP - POOL_PART
        pool.tensor_tensor(self.lo[:, slot, a:], self.raw[:, slot, a:], self.hi[:, slot, a:].bitcast(F32),
                           ALU.subtract).then_inc(self.lo_pool, 1)

    def ready(self, pe, g):
        pe.wait_ge(self.lo_vector, g + 3)
        pe.wait_ge(self.lo_pool, g + 3)

    def done(self, engine, g):
        engine.wait_ge(self.used, g + 3)

    def views(self, slot, blocks):
        return (self.hi[:, slot, :].rearrange("p (k n) -> p k n", k=blocks),
                self.lo[:, slot, :].rearrange("p (k n) -> p k n", k=blocks))

    def open(self, dve=None, pool=None, pe=None):
        if dve is not None:
            dve.sem_inc(self.lo_vector, 2)
        if pool is not None:
            pool.sem_inc(self.lo_pool, 2)
        if pe is not None:
            pe.sem_inc(self.used, 2)


def apart(engine, spare):
    engine.sem_inc(spare, 1)


def prime(act, primer, column, func):
    act.activation(primer[:, column:column + 1], primer[:, 0:1], func)


class Chain:

    def __init__(self, dve, sem, base=0):
        self.dve, self.sem, self.base, self.n = dve, sem, base, 0

    def __call__(self, instruction):
        self.n += 1
        instruction.then_inc(self.sem, 1)
        self.dve.wait_ge(self.sem, self.base + self.n)


def build(nc, x, mem, norm_mix, norm_xattn, norm_mem, norm_ffn, norm_final, conv_w_in, conv_w, conv_w_out,
          w_q, w_kv, w_o, router, w_gate, w_up, w_down, out):
    ctx = ExitStack()

    def sb(name, shape, dt=F32):
        return ctx.enter_context(nc.sbuf_tensor(name, shape, dt))

    w_raw = sb("w_raw", [P, 2, STRIP])
    w_hi = sb("w_hi", [P, 2, STRIP], F32R)
    w_lo = sb("w_lo", [P, 2, STRIP], F32R)
    act_hi = sb("act_hi", [P, KB, T], F32R)
    act_lo = sb("act_lo", [P, KB, T], F32R)
    q_hi = sb("q_hi", [P, KB, T], F32R)
    q_lo = sb("q_lo", [P, KB, T], F32R)
    h = sb("h", [P, TB * D])
    xs = sb("xs", [P, TB * D])
    vin = sb("vin", [P, KB * T])
    k_hi = sb("k_hi", [P, KB, MEM], F32R)
    k_lo = sb("k_lo", [P, KB, MEM], F32R)
    v_hi = sb("v_hi", [P, MB, D], F32R)
    v_lo = sb("v_lo", [P, MB, D], F32R)
    ident = sb("ident", [P, P])
    ones = sb("ones", [P, P])
    upper = sb("upper", [P, P], BF16)
    ones_b = sb("ones_b", [P, P], BF16)
    same_expert = sb("same_expert", [P, P])
    ramp = sb("ramp", [P, E])
    token_id = sb("token_id", [P, SEQ // P])
    ints = sb("ints", [P, P], I32)
    ints2 = sb("ints2", [P, P], I32)
    own_block = sb("own_block", [P, P])
    gains = sb("gains", [P, 3, KB])
    taps = sb("taps", [P, 3, KB])
    gain_row = sb("gain_row", [P, D])
    r_raw = sb("r_raw", [P, KB, E])
    r_hi = sb("r_hi", [P, KB, E], F32R)
    r_lo = sb("r_lo", [P, KB, E], F32R)
    probs = sb("probs", [P, SEQ // P * E])
    index = sb("index", [P, E * CB], U32)
    stat = sb("stat", [P, 68])
    junk = sb("junk", [P, TB, D], mybir.dt.uint8)
    indices = sb("indices", [P, 4 * CB], U32)
    primed = sb("primed", [16, CB, 16])
    primer = sb("primer", [P, 8])
    r_buf = sb("r_buf", [P, TB * E])
    rows_written = ctx.enter_context(nc.semaphore("rows_written"))
    last_written = ctx.enter_context(nc.semaphore("last_written"))
    spare = ctx.enter_context(nc.semaphore("spare"))
    ps = ctx.enter_context(nc.psum_tensor("ps", [P, 8, T], F32))

    v_d = nc.dram_tensor("conv_v", [D, CONV_COLS], F32).ap()
    sum_d = nc.dram_tensor("residual", [SEQ, D], F32).ap()
    row_d = nc.dram_tensor("normed_rows", [SEQ, ROW], F32).ap()
    index_d = nc.dram_tensor("index_lists", [E, CAP], F32).ap()

    ss, var, root, rstd, tmp, tmp2 = (stat[:, 4 * i:4 * i + 4] for i in range(6))

    def bank(group, b=None):
        return ps[:, 4 * group:4 * group + 4, :] if b is None else ps[:, 4 * group + b, :]

    def product(pe, o, lhs, rhs, first, last):
        pe.matmul(o, lhs[0], rhs[0], start=first, stop=False)
        pe.matmul(o, lhs[0], rhs[1], start=False, stop=False)
        return pe.matmul(o, lhs[1], rhs[0], start=False, stop=last)

    def refine_rstd(dve, chain, rstd, root, var, tmp, tmp2):
        chain(dve.reciprocal(rstd, root))
        chain(dve.tensor_tensor(tmp, rstd, rstd, ALU.mult))
        chain(dve.tensor_tensor(tmp2, tmp, var, ALU.mult))
        chain(dve.tensor_scalar(tmp, tmp2, -0.5, 1.5, ALU.mult, ALU.add))
        chain(dve.tensor_tensor(rstd, rstd, tmp, ALU.mult))

    def front():
        pctx = ExitStack()
        sem = lambda name: pctx.enter_context(nc.semaphore(name))
        strips = Strips(nc, pctx, "front", w_raw, w_hi, w_lo)
        NS = 12
        CONV0 = 8
        ATT0 = CONV0 + NS * TILES
        BODY0 = ATT0 + 4

        mem_loaded, gain_loaded, consts_loaded, router_loaded = (
            [sem("mem_loaded0"), sem("mem_loaded1")], sem("gain_loaded"), sem("consts_loaded"), sem("router_loaded"))
        const_step, consts_made, const_chain = sem("const_step"), sem("consts_made"), sem("const_chain")
        mem_squares, mem_var, mem_root, mem_chain, mem_done = (
            sem("mem_squares"), sem("mem_var"), sem("mem_root"), sem("mem_chain"), sem("mem_done"))
        filled, kv_hi, kv_lo, router_hi = sem("su_filled"), sem("kv_hi"), sem("kv_lo"), sem("su_router_hi")
        memx = vin[:, 0:MB * D].rearrange("p (t d) -> p t d", t=MB)
        kv = w_kv[0].rearrange("(k p) n -> p k n", p=P)

        x_loaded = sem("x_loaded")
        squares, var_done, root_done, chain_sem, xs_done = (
            sem("cv_squares"), sem("cv_var"), sem("cv_root"), sem("cv_chain"), sem("cv_xs"))
        transposed, xn_hi, xn_lo = sem("cv_transposed"), sem("xn_hi"), sem("xn_lo")
        c_read, u_done, v_done, v_free, v_stored = (
            sem("c_read"), sem("u_done"), sem("v_done"), sem("v_free"), sem("v_stored"))
        xt = h[:, :].rearrange("p (t d) -> p t d", t=TB)
        pairs = [(q_hi, q_lo), (act_hi, act_lo)]
        u = xs[:, 0:4 * (T + 2)].rearrange("p (m c) -> p m c", m=4)
        cgate = vin[:, 0:4 * T].rearrange("p (m c) -> p m c", m=4)
        cv = vin[:, 4 * T:].rearrange("p (m c) -> p m c", m=4)
        u_carry = stat[:, 24:40].rearrange("p (m c) -> p m c", c=2)
        b_carry = stat[:, 40:48]
        last_v = stat[:, 48:56]
        last_t = stat[:, 56:64]
        w_in = conv_w_in[0].rearrange("(k p) n -> p k n", p=P)
        x_v = x[0].rearrange("(i t p) d -> p i t d", p=P, t=TB)
        v_v = v_d.rearrange("(m p) c -> p m c", p=P)
        COLUMNS = [part * D + half * T for half in range(2) for part in (1, 2, 0)]
        GROUP = (0, 1, 0, 1, 1, 0)

        at_x_loaded, v_loaded, tile_free, rows_free = (
            sem("at_x_loaded"), sem("at_v_loaded"), sem("tile_free"), sem("rows_free"))
        stored = rows_written
        at_squares, at_var, at_root, at_chain, at_rstd = (
            sem("at_squares"), sem("at_var"), sem("at_root"), sem("at_chain"), sem("at_rstd"))
        rows_vector, rows_scalar = sem("rows_vector"), sem("rows_scalar")
        v_hi_done, v_lo_done = sem("at_v_hi"), sem("at_v_lo")
        n1_hi, n1_lo, qh, ql = sem("n1_hi"), sem("n1_lo"), sem("q_hi_done"), sem("q_lo_done")
        pt_hi, pt_lo, o_hi, o_lo, n3_hi, n3_lo = (
            sem("pt_hi"), sem("pt_lo"), sem("o_hi"), sem("o_lo"), sem("n3_hi"), sem("n3_lo"))
        added = sem("at_added")
        turned, scored, maxed, exped, p_done = (
            sem("turned"), sem("scored"), sem("maxed"), sem("exped"), sem("p_done"))
        valued, routed, logits_out, logits_turned, logits_read, shifted, r_exp, probs_done = (
            sem("valued"), sem("routed"), sem("logits_out"), sem("logits_turned"), sem("logits_read"), sem("shifted"), sem("r_exp"),
            sem("probs_done"))
        logits_t = junk[0:E, 0:2, :].rearrange("p t d -> p (t d)").bitcast(F32)
        tiles = [b[:, :].rearrange("p (t d) -> p t d", t=TB) for b in (h, vin)]
        v_tiles = [b[:, :].rearrange("p (k c) -> p k c", k=KB) for b in (h, vin)]
        xn = xs[:, :].rearrange("p (t d) -> p t d", t=TB)
        pr = xs[:, :].rearrange("p (h t m) -> p h t m", h=HEADS, t=TB)
        neg_max = stat[:, 24:40].rearrange("p (h t) -> p h t", h=HEADS)
        sums = stat[:, 40:56].rearrange("p (h t) -> p h t", h=HEADS)
        r_max = stat[:, 56:60]
        r_sum = stat[:, 60:64]
        ss_b = stat[:, 64:68]
        r_tmp = r_buf[:, :]
        sum_v = sum_d.rearrange("(i t p) d -> p i t d", p=P, t=TB)
        row_v = row_d.rearrange("(i t p) d -> p i t d", p=P, t=TB)
        w_co = conv_w_out[0].rearrange("(k p) n -> p k n", p=P)
        w_qv = w_q[0].rearrange("(k p) n -> p k n", p=P)
        w_ov = w_o[0].rearrange("(k p) n -> p k n", p=P)
        BODY_CHAIN = 6 + 6 + HEADS + 5

        def scores_bank(head):
            return bank(head // 2)[:, 2 * (head % 2):2 * (head % 2) + 2, :].rearrange("p b (t m) -> p (b t) m", m=MEM)

        def tiles_loop(engine, tile):
            with engine.Fori(0, TILES // 2 - 1) as j:
                for n in range(2):
                    tile(j * 2 + n, n, False)
            tile(TILES - 2, 0, False)
            tile(TILES - 1, 1, True)

        def rows(i):
            return bass.ds(i, 1)

        with nc.Block() as block:
            @block.sync
            def _(sp):
                for t in range(MB):
                    sp.dma_start(memx[:, t, :], mem[0, t * P:(t + 1) * P, :]).then_inc(mem_loaded[t], STEP)
                for g in range(CONV0):
                    half, kh = g // 2, g % 2
                    strips.load(sp, g, g % 2, kv[:, 4 * kh:4 * kh + 4, T * half:T * half + T], 4)
                    if g == 3:
                        sp.dma_start(xt, x_v[:, 0]).then_inc(x_loaded, STEP)

                def conv_tile(i, n, last):
                    for s in range(NS):
                        c, kh = COLUMNS[s // 2], s % 2
                        strips.load(sp, i * NS + (CONV0 + s), s % 2, w_in[:, 4 * kh:4 * kh + 4, c:c + T], 4)
                        if s == 3 and not last:
                            sp.wait_ge(transposed, i * 2 + 2)
                            sp.dma_start(xt, x_v[:, rows(i + 1), :, :].rearrange("p i t d -> p (i t) d")).then_inc(
                                x_loaded, STEP)
                        if s == 6 and last:
                            sp.wait_ge(transposed, 2 * TILES)
                            sp.wait_ge(v_stored, 4 * STEP)
                            sp.dma_start(v_tiles[0], v_v[:, :, 1:T + 1]).then_inc(v_loaded, STEP)
                        if s == 11 and last:
                            sp.wait_ge(v_lo_done, KB)
                            sp.dma_start(tiles[0], x_v[:, 0]).then_inc(at_x_loaded, STEP)
                tiles_loop(sp, conv_tile)

                for s in range(4):
                    half, kh = s // 2, s % 2
                    strips.load(sp, ATT0 + s, s % 2, w_co[:, 4 * kh:4 * kh + 4, T * half:T * half + T], 4)

                def attend_tile(i, n, last):
                    for s in range(8 if last else NS):
                        w = (w_qv, w_ov, w_co)[s // 4]
                        half, kh = s // 2 % 2, s % 2
                        strips.load(sp, i * NS + (BODY0 + s), s % 2, w[:, 4 * kh:4 * kh + 4, T * half:T * half + T], 4)
                        if s == 3 and not last:
                            sp.wait_ge(tile_free, i + 1)
                            sp.dma_start(v_tiles[1 - n], v_v[:, :, bass.ds(i * T + (T + 1), T)]).then_inc(v_loaded, STEP)
                        if s == 8:
                            sp.wait_ge(v_lo_done, i * KB + 2 * KB)
                            sp.dma_start(tiles[1 - n], x_v[:, rows(i + 1), :, :].rearrange("p i t d -> p (i t) d")
                                         ).then_inc(at_x_loaded, STEP)
                tiles_loop(sp, attend_tile)
                sp.wait_ge(probs_done, TILES)
                sp.dma_start(row_v[:, TILES - 1, :, D:ROW], r_tmp.rearrange("p (t e) -> p t e", t=TB)).then_inc(
                    last_written, STEP)

            @block.gpsimd
            def _(pool):
                strips.open(pool=pool)
                pool.sem_inc(v_free, 1)
                pool.memset(ones[:, :], 1.0).then_inc(const_step, 1)
                pool.memset(ident[:, :], 0.0).then_inc(const_step, 1)
                pool.wait_ge(const_step, 2)
                pool.affine_select(out=ident[:, :], in_=ident[:, :], compare_op=ALU.not_equal, fill=1.0, base=0,
                                   pattern=[[-1, P]], channel_multiplier=1).then_inc(consts_made, 1)
                for g in range(2):
                    strips.split_lo_pool(pool, g, g % 2)
                pool.memset(ones_b[:, :], 1.0).then_inc(const_step, 1)
                pool.wait_ge(const_step, 3)
                pool.affine_select(out=upper[:, :], in_=ones_b[:, :], compare_op=ALU.is_ge, fill=0.0, base=-1,
                                   pattern=[[1, P]], channel_multiplier=-1).then_inc(consts_made, 1)
                pool.iota(ints[:, :], pattern=[[-1, P]], base=P, channel_multiplier=1).then_inc(consts_made, 1)
                pool.iota(ints2[:, :], pattern=[[-16, 8], [0, 16]], base=P, channel_multiplier=1).then_inc(
                    consts_made, 1)
                pool.iota(ramp[:, :], pattern=[[1, E]], base=0, channel_multiplier=0,
                          allow_small_or_imprecise_dtypes=True).then_inc(consts_made, 1)
                pool.iota(token_id[:, :], pattern=[[P, SEQ // P]], base=0, channel_multiplier=1,
                          allow_small_or_imprecise_dtypes=True).then_inc(consts_made, 1)
                for g in range(2, CONV0 + 2):
                    strips.split_lo_pool(pool, g, g % 2)

                def conv_tile(i, n, last):
                    def split(s):
                        strips.split_lo_pool(pool, i * NS + (CONV0 + s), s % 2)

                    def store(half):
                        pool.wait_ge(v_done, i * 2 + (half + 2))
                        apart(pool, spare)
                        pool.dma_start(v_v[:, 4 * half:4 * half + 4, bass.ds(i * T, T)], cv).then_inc(v_stored, STEP)

                    def release(half):
                        pool.wait_ge(v_stored, i * 2 * STEP + (half + 1) * STEP)
                        pool.sem_inc(v_free, 1)

                    for s in range(2, 8):
                        split(s)
                    store(0)
                    split(8)
                    split(9)
                    release(0)
                    for s in range(10, 14):
                        split(s)
                    store(1)
                    release(1)
                tiles_loop(pool, conv_tile)
                pool.wait_ge(v_done, 2 * TILES + 2)
                pool.dma_start(v_v[:, :, SEQ:SEQ + 1], last_v.rearrange("p (m o) -> p m o", o=1),
                               allow_slow_non_contiguous=True).then_inc(v_stored, STEP)
                pool.wait_ge(v_stored, (2 * TILES + 1) * STEP)
                pool.sem_inc(tile_free, 1)

                for s in range(2, 6):
                    strips.split_lo_pool(pool, ATT0 + s, s % 2)

                def attend_tile(i, n, last):
                    def split(s):
                        if s < 8 or not last:
                            strips.split_lo_pool(pool, i * NS + (BODY0 + s), s % 2)

                    for s in range(2, 10):
                        split(s)
                    pool.wait_ge(added, i * 8 + 8)
                    apart(pool, spare)
                    pool.dma_start(sum_v[:, rows(i), :, :].rearrange("p i t d -> p (i t) d"), tiles[n]).then_inc(stored, STEP)
                    split(10)
                    pool.wait_ge(rows_vector, i * (2 * TB - 1) + (2 * TB - 1))
                    apart(pool, spare)
                    pool.dma_start(row_v[:, rows(i), :, 0:D].rearrange("p i t d -> p (i t) d"), xn).then_inc(stored, STEP)
                    split(11)
                    split(12)
                    pool.wait_ge(stored, i * 3 * STEP + 2 * STEP)
                    pool.sem_inc(tile_free, 1)
                    pool.sem_inc(rows_free, 1)
                    split(13)
                    if not last:
                        pool.wait_ge(probs_done, i + 1)
                        apart(pool, spare)
                        pool.dma_start(row_v[:, rows(i), :, D:ROW].rearrange("p i t e -> p (i t) e"),
                                       r_tmp.rearrange("p (t e) -> p t e", t=TB)).then_inc(stored, STEP)
                        pool.wait_ge(stored, i * 3 * STEP + 3 * STEP)
                tiles_loop(pool, attend_tile)

            @block.scalar
            def _(act):
                act.dma_start(gains[:, 2, :], norm_mem[0].rearrange("(k p) -> p k", p=P),
                              allow_slow_non_contiguous=True).then_inc(gain_loaded, STEP)
                act.wait_ge(chain_sem, 1)
                prime(act, primer, 1, ACT.Sqrt)
                for t in range(MB):
                    act.wait_ge(mem_loaded[t], STEP)
                    act.activation(junk[:, t, :], memx[:, t, :], ACT.Square, accum_out=ss[:, t:t + 1]).then_inc(mem_squares, 1)
                act.wait_ge(mem_var, 1)
                act.activation(root[:, 0:MB], var[:, 0:MB], ACT.Sqrt).then_inc(mem_root, 1)
                strips.split_hi(act, 0, 0)
                strips.split_hi(act, 1, 1)
                act.wait_ge(gain_loaded, STEP)
                for k in range(KB):
                    act.wait_ge(filled, 1 + k // 4)
                    act.activation(act_hi[:, k, 0:MEM], bank(k // 4, k % 4)[:, 0:MEM], ACT.Copy,
                                   scale=gains[:, 2, k:k + 1]).then_inc(kv_hi, 1)
                for n, gain in enumerate((norm_mix, norm_xattn)):
                    act.dma_start(gains[:, n, :], gain[0].rearrange("(k p) -> p k", p=P),
                                  allow_slow_non_contiguous=True).then_inc(consts_loaded, STEP)
                for n in range(3):
                    act.dma_start(taps[:, n, :], conv_w[0, n].rearrange("(k p) -> p k", p=P),
                                  allow_slow_non_contiguous=True).then_inc(consts_loaded, STEP)
                act.dma_start(gain_row[:, :], norm_ffn[0:1, :].to_broadcast([P, D])).then_inc(consts_loaded, STEP)
                act.dma_start(r_raw[:, :, :], router[0].rearrange("(k p) e -> p k e", p=P)).then_inc(
                    router_loaded, STEP)

                def tile_stats(i):
                    act.wait_ge(x_loaded, i * STEP + STEP)
                    for t in range(TB):
                        act.activation(junk[:, t, :], xt[:, t, :], ACT.Square, accum_out=ss[:, t:t + 1]).then_inc(squares, 1)
                    act.wait_ge(var_done, i + 1)
                    act.activation(root, var, ACT.Sqrt).then_inc(root_done, 1)

                def tile_hi(i, n, half):
                    act.wait_ge(transposed, i * 2 + (1 + half))
                    for k in range(4 * half, 4 * half + 4):
                        act.activation(pairs[n][0][:, k, :], bank(half, k % 4), ACT.Copy,
                                       scale=gains[:, 0, k:k + 1]).then_inc(xn_hi, 1)

                for half in range(4):
                    strips.split_hi(act, 2 * half + 2, 0)
                    strips.done(act, 2 * half + 1)
                    if half < 2:
                        act.activation(k_hi[:, 4 * half:4 * half + 4, :], bank(half % 2)[:, :, 0:MEM],
                                       ACT.Copy).then_inc(kv_hi, 1)
                    else:
                        act.activation(v_hi[:, :, T * (half - 2):T * (half - 1)], bank(half % 2)[:, 0:MB, :],
                                       ACT.Copy).then_inc(kv_hi, 1)
                    strips.split_hi(act, 2 * half + 3, 1)
                    if half == 1:
                        tile_stats(0)
                    if half == 2:
                        act.wait_ge(router_loaded, STEP)
                        act.activation(r_hi[:, :, :], r_raw[:, :, :], ACT.Copy).then_inc(router_hi, 1)
                act.wait_ge(consts_loaded, 6 * STEP)
                tile_hi(0, 0, 0)
                tile_hi(0, 0, 1)

                def conv_tile(i, n, last):
                    def split(s):
                        strips.split_hi(act, i * NS + (CONV0 + s), s % 2)

                    def read_c(half):
                        strips.done(act, i * NS + (CONV0 + 6 * half + 1))
                        act.wait_ge(u_done, i * 2 + (half + 1))
                        act.activation(cgate, bank(GROUP[3 * half]), ACT.Copy).then_inc(c_read, 1)

                    split(2)
                    read_c(0)
                    split(3)
                    split(4)
                    if not last:
                        tile_stats(i + 1)
                    for s in range(5, 9):
                        split(s)
                    if last:
                        act.wait_ge(v_loaded, STEP)
                        for k in range(KB):
                            act.activation(q_hi[:, k, :], v_tiles[0][:, k, :], ACT.Copy).then_inc(v_hi_done, 1)
                    read_c(1)
                    split(9)
                    if not last:
                        tile_hi(i + 1, 1 - n, 0)
                    for s in range(10, 14):
                        split(s)
                    if not last:
                        tile_hi(i + 1, 1 - n, 1)
                tiles_loop(act, conv_tile)

                def half_squares(n, half, count):
                    c = slice(T * half, T * half + T)
                    for t in range(TB):
                        if t % 2 == 0:
                            act.wait_ge(added, count * 2 + (t // 2 - 1))
                        act.activation(junk[:, t, c], tiles[n][:, t, c], ACT.Square,
                                       accum_out=(ss, ss_b)[half][:, t:t + 1]).then_inc(at_squares, 1)

                def take_root(count):
                    act.wait_ge(at_var, count)
                    act.activation(root, var, ACT.Sqrt).then_inc(at_root, 1)

                def scale_rows(n, i):
                    act.wait_ge(at_rstd, i + 1)
                    t = TB - 1
                    act.activation(xn[:, t, :], tiles[n][:, t, :], ACT.Copy,
                                   scale=rstd[:, t:t + 1]).then_inc(rows_scalar, 1)

                def turned_hi(i):
                    for k in range(KB):
                        act.wait_ge(turned, i * 24 + (k + 1))
                        act.activation(act_hi[:, k, :], bank(k // 4, k % 4), ACT.Copy,
                                       scale=gains[:, 1, k:k + 1]).then_inc(n1_hi, 1)

                strips.split_hi(act, ATT0 + 2, 0)
                strips.split_hi(act, ATT0 + 3, 1)
                half_squares(0, 0, 1)
                strips.split_hi(act, ATT0 + 4, 0)
                half_squares(0, 1, 2)
                take_root(1)
                scale_rows(0, 0)
                turned_hi(0)
                strips.split_hi(act, ATT0 + 5, 1)

                def attend_tile(i, n, last):
                    def split(s):
                        if s < 8 or not last:
                            strips.split_hi(act, i * NS + (BODY0 + s), s % 2)

                    for half in range(2):
                        split(2 + 2 * half)
                        strips.done(act, i * NS + (BODY0 + 1 + 2 * half))
                        for m in range(4):
                            act.activation(q_hi[:, 4 * half + m, :], bank(half, m), ACT.Copy,
                                           scale=HD ** -0.5).then_inc(qh, 1)
                        if half == 0:
                            split(3)
                    for hd in range(HEADS):
                        act.wait_ge(maxed, i * HEADS + (hd + 1))
                        for t in range(TB):
                            act.activation(pr[:, hd, t, :], scores_bank(hd)[:, t, :], ACT.Exp,
                                           bias=neg_max[:, hd, t:t + 1], accum_out=sums[:, hd, t:t + 1]).then_inc(exped, 1)
                    for m in range(KB):
                        act.wait_ge(turned, i * 24 + (KB + m + 1))
                        act.activation(q_hi[:, m, :], bank(m // 4, m % 4), ACT.Copy).then_inc(pt_hi, 1)
                    for m in range(KB):
                        act.wait_ge(valued, i * 2 + (1 + m // 4))
                        act.activation(act_hi[:, m, :], bank(m // 4, m % 4), ACT.Copy).then_inc(o_hi, 1)
                    prime(act, primer, 2, ACT.Sqrt)
                    split(5)
                    if not last:
                        act.wait_ge(v_loaded, i * STEP + 2 * STEP)
                        for k in range(KB):
                            act.activation(q_hi[:, k, :], v_tiles[1 - n][:, k, :], ACT.Copy).then_inc(v_hi_done, 1)
                    split(6)
                    split(7)
                    half_squares(n, 0, i * 4 + 3)
                    split(8)
                    half_squares(n, 1, i * 4 + 4)
                    take_root(i * 2 + 2)
                    if last:
                        prime(act, primer, 3, ACT.Exp)
                    split(9)
                    split(10)
                    for k in range(KB):
                        act.wait_ge(turned, i * 24 + (2 * KB + k + 1))
                        act.activation(act_hi[:, k, :], bank(1 - k // 4, k % 4), ACT.Copy).then_inc(n3_hi, 1)
                    split(11)
                    if not last:
                        half_squares(1 - n, 0, i * 4 + 5)
                        split(12)
                        half_squares(1 - n, 1, i * 4 + 6)
                        take_root(i * 2 + 3)
                    act.wait_ge(routed, i + 1)
                    act.activation(logits_t, bank(1 if last else 0, 0)[0:E, :], ACT.Copy).then_inc(logits_out, 1)
                    if not last:
                        act.wait_ge(rows_free, i + 1)
                        scale_rows(1 - n, i + 1)
                        turned_hi(i + 1)
                        split(13)
                    act.wait_ge(shifted, i + 1)
                    act.activation(r_tmp, r_tmp, ACT.Exp).then_inc(r_exp, 1)
                tiles_loop(act, attend_tile)

            @block.vector
            def _(dve):
                strips.open(dve=dve)
                chain = Chain(dve, mem_chain)
                dve.memset(primer[:, 0:1], 0.0)
                dve.memset(stat[:, 24:64], 0.0).then_inc(chain_sem, 1)
                dve.wait_ge(chain_sem, 1)
                dve.sem_inc(u_done, 1)
                dve.sem_inc(v_done, 1)
                dve.wait_ge(mem_squares, MB)
                dve.tensor_scalar(var[:, 0:MB], ss[:, 0:MB], 1.0 / D, RMS_EPS, ALU.mult, ALU.add).then_inc(mem_var, 1)
                dve.wait_ge(mem_root, 1)
                refine_rstd(dve, chain, *(v[:, 0:MB] for v in (rstd, root, var, tmp, tmp2)))
                for t in range(MB):
                    dve.tensor_scalar(memx[:, t, :], memx[:, t, :], rstd[:, t:t + 1], None, ALU.mult).then_inc(mem_done, 1)
                strips.split_lo(dve, 0, 0)
                strips.split_lo(dve, 1, 1)
                for k in range(KB):
                    dve.wait_ge(kv_hi, k + 1)
                    dve.scalar_tensor_tensor(act_lo[:, k, 0:MEM], bank(k // 4, k % 4)[:, 0:MEM],
                                             gains[:, 2, k:k + 1], act_hi[:, k, 0:MEM].bitcast(F32),
                                             ALU.mult, ALU.subtract).then_inc(kv_lo, 1)

                def tile_norm(i, chain):
                    dve.wait_ge(squares, i * TB + TB)
                    dve.tensor_scalar(var, ss, 1.0 / D, RMS_EPS, ALU.mult, ALU.add).then_inc(var_done, 1)
                    dve.wait_ge(root_done, i + 1)
                    refine_rstd(dve, chain, rstd, root, var, tmp, tmp2)
                    for t in range(TB):
                        dve.tensor_scalar(xt[:, t, :], xt[:, t, :], rstd[:, t:t + 1], None, ALU.mult).then_inc(xs_done, 1)

                def tile_lo(i, n, half):
                    for k in range(4 * half, 4 * half + 4):
                        dve.wait_ge(xn_hi, i * KB + (k + 1))
                        dve.scalar_tensor_tensor(pairs[n][1][:, k, :], bank(half, k % 4), gains[:, 0, k:k + 1],
                                                 pairs[n][0][:, k, :].bitcast(F32), ALU.mult, ALU.subtract).then_inc(xn_lo, 1)

                for half in range(4):
                    strips.split_lo(dve, 2 * half + 2, 0)
                    dve.wait_ge(kv_hi, KB + half + 1)
                    if half < 2:
                        b = slice(4 * half, 4 * half + 4)
                        dve.tensor_tensor(k_lo[:, b, :], bank(half % 2)[:, :, 0:MEM], k_hi[:, b, :].bitcast(F32),
                                          ALU.subtract).then_inc(kv_lo, 1)
                    else:
                        c = slice(T * (half - 2), T * (half - 1))
                        dve.tensor_tensor(v_lo[:, :, c], bank(half % 2)[:, 0:MB, :], v_hi[:, :, c].bitcast(F32),
                                          ALU.subtract).then_inc(kv_lo, 1)
                    strips.split_lo(dve, 2 * half + 3, 1)
                    if half == 1:
                        tile_norm(0, Chain(dve, chain_sem, 1))
                tile_lo(0, 0, 0)
                tile_lo(0, 0, 1)
                constants = Chain(dve, const_chain)
                dve.wait_ge(router_hi, 1)
                constants(dve.tensor_tensor(r_lo[:, :, :], r_raw[:, :, :], r_hi[:, :, :].bitcast(F32), ALU.subtract))
                dve.wait_ge(consts_made, 6)
                constants(dve.tensor_scalar(ints[:, :], ints[:, :], 15, None, ALU.bitwise_and))
                constants(dve.tensor_scalar(same_expert[:, :], ints[:, :], 0.0, None, ALU.is_equal))
                constants(dve.tensor_scalar(ints2[:, :], ints2[:, :], 4, None, ALU.logical_shift_right))
                constants(dve.tensor_scalar(own_block[:, :], ints2[:, :], 8.0, None, ALU.is_equal))

                PER = 5 + 2 * 6

                def conv_tile(i, n, last):
                    chain = Chain(dve, chain_sem, i * PER + 6)

                    def split(s):
                        strips.split_lo(dve, i * NS + (CONV0 + s), s % 2)

                    def half_work(half):
                        mb = slice(4 * half, 4 * half + 4)
                        f = 3 * half
                        chain(dve.tensor_copy(u[:, :, 0:2], u_carry[:, mb, :]))
                        strips.done(dve, i * NS + (CONV0 + 2 * f + 3))
                        dve.wait_ge(c_read, i * 2 + (half + 1))
                        dve.tensor_tensor(u[:, :, 2:T + 2], bank(GROUP[f + 1]), cgate, ALU.mult).then_inc(u_done, 1)
                        split(2 * f + 5)
                        dve.wait_ge(u_done, i * 2 + (half + 2))
                        dve.wait_ge(v_free, i * 2 + (half + 1))
                        for tap in range(3):
                            for m in range(4):
                                w = taps[:, tap, 4 * half + m:4 * half + m + 1]
                                if tap == 0:
                                    ins = dve.tensor_scalar(cv[:, m, :], u[:, m, 0:T], w, None, ALU.mult)
                                else:
                                    ins = dve.scalar_tensor_tensor(cv[:, m, :], u[:, m, tap:T + tap], w, cv[:, m, :],
                                                                   ALU.mult, ALU.add)
                            chain(ins)
                            if tap == 1:
                                split(2 * f + 6)
                        dve.tensor_copy(u_carry[:, mb, :], u[:, :, T:T + 2])
                        chain(dve.tensor_tensor(cv[:, :, 0], cv[:, :, 0], b_carry[:, mb], ALU.mult))
                        strips.done(dve, i * NS + (CONV0 + 2 * f + 5))
                        b = bank(GROUP[f + 2])
                        dve.tensor_tensor(cv[:, :, 1:T], cv[:, :, 1:T], b[:, :, 0:T - 1], ALU.mult)
                        chain(dve.tensor_copy(b_carry[:, mb], b[:, :, T - 1]))
                        dve.sem_inc(v_done, 1)
                        split(2 * f + 7)

                    split(2)
                    split(3)
                    split(4)
                    if not last:
                        tile_norm(i + 1, chain)
                    half_work(0)
                    split(8)
                    if last:
                        for k in range(KB):
                            dve.wait_ge(v_hi_done, k + 1)
                            dve.tensor_tensor(q_lo[:, k, :], v_tiles[0][:, k, :], q_hi[:, k, :].bitcast(F32),
                                              ALU.subtract).then_inc(v_lo_done, 1)
                    split(9)
                    if not last:
                        tile_lo(i + 1, 1 - n, 0)
                    split(10)
                    half_work(1)
                    if not last:
                        tile_lo(i + 1, 1 - n, 1)
                    assert last or chain.n == PER, chain.n
                tiles_loop(dve, conv_tile)
                chain = Chain(dve, chain_sem, (TILES - 1) * PER + 6 + 12)
                chain(dve.tensor_tensor(last_v, u_carry[:, :, 0], taps[:, 0, :], ALU.mult))
                chain(dve.tensor_tensor(last_t, u_carry[:, :, 1], taps[:, 1, :], ALU.mult))
                chain(dve.tensor_tensor(last_v, last_v, last_t, ALU.add))
                dve.tensor_tensor(last_v, last_v, b_carry, ALU.mult).then_inc(v_done, 1)

                dve.sem_inc(logits_read, 1)

                def add_half(n, half):
                    c = slice(T * half, T * half + T)
                    for t in (0, 2):
                        dve.tensor_tensor(tiles[n][:, t:t + 2, c], bank(half)[:, t:t + 2, :], tiles[n][:, t:t + 2, c],
                                          ALU.add).then_inc(added, 1)

                def rms(chain, count, number):
                    dve.wait_ge(at_squares, count)
                    chain(dve.tensor_tensor(tmp, ss, ss_b, ALU.add))
                    dve.tensor_scalar(var, tmp, 1.0 / D, RMS_EPS, ALU.mult, ALU.add).then_inc(at_var, 1)
                    dve.wait_ge(at_root, number)
                    refine_rstd(dve, chain, rstd, root, var, tmp, tmp2)

                def scale_rows(n, before_last=None):
                    dve.sem_inc(at_rstd, 1)
                    for t in range(TB - 1):
                        if t == 2 and before_last is not None:
                            before_last()
                        dve.tensor_scalar(xn[:, t, :], tiles[n][:, t, :], rstd[:, t:t + 1], None, ALU.mult).then_inc(
                            rows_vector, 1)

                def turned_lo(i):
                    for k in range(KB):
                        dve.wait_ge(n1_hi, i * KB + (k + 1))
                        dve.scalar_tensor_tensor(act_lo[:, k, :], bank(k // 4, k % 4), gains[:, 1, k:k + 1],
                                                 act_hi[:, k, :].bitcast(F32), ALU.mult, ALU.subtract).then_inc(n1_lo, 1)

                strips.split_lo(dve, ATT0 + 2, 0)
                strips.split_lo(dve, ATT0 + 3, 1)
                dve.wait_ge(at_x_loaded, STEP)
                strips.done(dve, ATT0 + 1)
                add_half(0, 0)
                strips.split_lo(dve, ATT0 + 4, 0)
                strips.done(dve, ATT0 + 3)
                add_half(0, 1)
                rms(Chain(dve, at_chain), 2 * TB, 1)
                scale_rows(0)
                turned_lo(0)
                strips.split_lo(dve, ATT0 + 5, 1)

                def attend_tile(i, n, last):
                    chain = Chain(dve, at_chain, i * BODY_CHAIN + 6)

                    def split(s):
                        if s < 8 or not last:
                            strips.split_lo(dve, i * NS + (BODY0 + s), s % 2)

                    for half in range(2):
                        split(2 + 2 * half)
                        for m in range(4):
                            dve.wait_ge(qh, i * KB + (4 * half + m + 1))
                            dve.scalar_tensor_tensor(q_lo[:, 4 * half + m, :], bank(half, m), HD ** -0.5,
                                                     q_hi[:, 4 * half + m, :].bitcast(F32), ALU.mult,
                                                     ALU.subtract).then_inc(ql, 1)
                        if half == 0:
                            split(3)
                    rt = r_tmp.rearrange("p (t e) -> p t e", t=TB)

                    def read_logits():
                        dve.wait_ge(logits_turned, i + 1)
                        dve.tensor_copy(r_tmp, bank(0 if last else 1, 0)[:, 0:TB * E]).then_inc(logits_read, 1)

                    def row_max(hd):
                        dve.wait_ge(scored, i * HEADS + (hd + 1))
                        dve.tensor_reduce(neg_max[:, hd, :], scores_bank(hd), axis=X, op=ALU.max,
                                          negate=True).then_inc(maxed, 1)

                    def scale_probs(hd):
                        dve.wait_ge(exped, i * HEADS * TB + (hd * TB + TB))
                        chain(dve.reciprocal(sums[:, hd, :], sums[:, hd, :]))
                        for t in range(TB):
                            ins = dve.tensor_scalar(pr[:, hd, t, :], pr[:, hd, t, :], sums[:, hd, t:t + 1], None, ALU.mult)
                        ins.then_inc(p_done, 1)

                    row_max(0)
                    for hd in range(1, HEADS):
                        row_max(hd)
                        scale_probs(hd - 1)
                    scale_probs(HEADS - 1)
                    for m in range(KB):
                        dve.wait_ge(pt_hi, i * KB + (m + 1))
                        dve.tensor_tensor(q_lo[:, m, :], bank(m // 4, m % 4), q_hi[:, m, :].bitcast(F32),
                                          ALU.subtract).then_inc(pt_lo, 1)
                    for m in range(KB):
                        dve.wait_ge(o_hi, i * KB + (m + 1))
                        dve.tensor_tensor(act_lo[:, m, :], bank(m // 4, m % 4), act_hi[:, m, :].bitcast(F32),
                                          ALU.subtract).then_inc(o_lo, 1)
                    split(5)
                    if not last:
                        for k in range(KB):
                            dve.wait_ge(v_hi_done, i * KB + (KB + k + 1))
                            dve.tensor_tensor(q_lo[:, k, :], v_tiles[1 - n][:, k, :], q_hi[:, k, :].bitcast(F32),
                                              ALU.subtract).then_inc(v_lo_done, 1)
                    split(6)
                    split(7)
                    strips.done(dve, i * NS + (BODY0 + 5))
                    add_half(n, 0)
                    split(8)
                    strips.done(dve, i * NS + (BODY0 + 7))
                    add_half(n, 1)
                    rms(chain, i * 16 + 16, i * 2 + 2)
                    split(9)
                    for t in range(TB):
                        dve.scalar_tensor_tensor(xn[:, t, :], tiles[n][:, t, :], rstd[:, t:t + 1], gain_row[:, :],
                                                 ALU.mult, ALU.mult).then_inc(rows_vector, 1)
                    split(10)
                    if not last:
                        dve.wait_ge(at_x_loaded, i * STEP + 2 * STEP)
                        strips.done(dve, i * NS + (BODY0 + 9))
                        add_half(1 - n, 0)
                    for k in range(KB):
                        dve.wait_ge(n3_hi, i * KB + (k + 1))
                        dve.tensor_tensor(act_lo[:, k, :], bank(1 - k // 4, k % 4), act_hi[:, k, :].bitcast(F32),
                                          ALU.subtract).then_inc(n3_lo, 1)
                    split(11)
                    split(12)
                    if not last:
                        strips.done(dve, i * NS + (BODY0 + 11))
                        add_half(1 - n, 1)
                        rms(chain, i * 16 + 24, i * 2 + 3)
                        dve.wait_ge(rows_free, i + 1)
                        scale_rows(1 - n, read_logits)
                        turned_lo(i + 1)
                        split(13)
                    else:
                        read_logits()
                    dve.wait_ge(logits_read, i + 2)
                    chain(dve.tensor_reduce(r_max, rt, axis=X, op=ALU.max))
                    dve.tensor_tensor(rt, rt, r_max.unsqueeze(2).to_broadcast([P, TB, E]),
                                      ALU.subtract).then_inc(shifted, 1)
                    dve.wait_ge(r_exp, i + 1)
                    chain(dve.tensor_reduce(r_sum, rt, axis=X, op=ALU.add))
                    chain(dve.reciprocal(r_sum, r_sum))
                    chain(dve.tensor_tensor(rt, rt, r_sum.unsqueeze(2).to_broadcast([P, TB, E]), ALU.mult))
                    chain(dve.tensor_copy(probs[:, bass.ds(i * TB * E, TB * E)], r_tmp))
                    dve.sem_inc(probs_done, 1)
                    assert last or chain.n == BODY_CHAIN, chain.n
                tiles_loop(dve, attend_tile)

            @block.tensor
            def _(pe):
                strips.open(pe=pe)
                pe.wait_ge(consts_made, 1)
                pe.wait_ge(mem_done, MB)
                for k in range(KB):
                    for t in range(MB):
                        ins = pe.transpose(bank(k // 4, k % 4)[:, t * P:(t + 1) * P], memx[:, t, k * P:(k + 1) * P],
                                           ident[:, :])
                    if k % 4 == 3:
                        ins.then_inc(filled, 1)
                for half in range(4):
                    pe.wait_ge(kv_lo, (4, KB, KB + 1, KB + 2)[half])
                    for kh in range(2):
                        g = 2 * half + kh
                        strips.ready(pe, g)
                        pe.wait_ge(kv_lo, max(4 * kh + 4, 4 + 4 * min(half, 1)))
                        hi, lo = strips.views(g % 2, 4)
                        for m in range(4 if half < 2 else MB):
                            for k in range(4):
                                kk = 4 * kh + k
                                if half < 2:
                                    f = slice(m * P, (m + 1) * P)
                                    ins = product(pe, bank(half % 2, m)[:, 0:MEM], (hi[:, k, f], lo[:, k, f]),
                                                  (act_hi[:, kk, 0:MEM], act_lo[:, kk, 0:MEM]), kk == 0, kk == KB - 1)
                                else:
                                    t = slice(m * P, (m + 1) * P)
                                    ins = product(pe, bank(half % 2, m), (act_hi[:, kk, t], act_lo[:, kk, t]),
                                                  (hi[:, k, :], lo[:, k, :]), kk == 0, kk == KB - 1)
                        ins.then_inc(strips.used, 1)

                def turn_x(half):
                    for k in range(4 * half, 4 * half + 4):
                        for t in range(TB):
                            ins = pe.transpose(bank(half, k % 4)[:, t * P:(t + 1) * P], xt[:, t, k * P:(k + 1) * P],
                                               ident[:, :])
                    ins.then_inc(transposed, 1)

                pe.wait_ge(xs_done, TB)
                pe.wait_ge(kv_lo, KB + 3)
                turn_x(0)
                pe.wait_ge(kv_lo, KB + 4)
                turn_x(1)

                def columns(group, first, pair, wait_data):
                    for kh in range(2):
                        strips.ready(pe, first + kh)
                        hi, lo = strips.views(kh, 4)
                        for m in range(4):
                            c = slice(m * P, (m + 1) * P)
                            for k in range(4):
                                kk = 4 * kh + k
                                if m == 0 and wait_data is not None:
                                    wait_data(kk)
                                ins = product(pe, bank(group, m), (hi[:, k, c], lo[:, k, c]),
                                              (pair[0][:, kk, :], pair[1][:, kk, :]), kk == 0, kk == KB - 1)
                        ins.then_inc(strips.used, 1)

                def conv_tile(i, n, last):
                    for f in range(6):
                        half, part = f // 3, f % 3
                        if f == 0:
                            pe.wait_ge(v_done, i * 2 + 1)
                        elif f == 1:
                            pe.wait_ge(xn_lo, i * KB + 8)
                        elif f == 5 and not last:
                            pe.wait_ge(xn_lo, i * KB + (KB + 4))
                        elif part == 2:
                            pe.wait_ge(c_read, i * 2 + 1)
                            if f == 5:
                                pe.wait_ge(v_done, i * 2 + 2)
                        elif part == 0:
                            pe.wait_ge(u_done, i * 2 + 2)
                        else:
                            pe.wait_ge(c_read, i * 2 + 2)

                        def normed(kk):
                            pe.wait_ge(xn_lo, i * KB + (kk + 1))
                        columns(GROUP[f], i * NS + (CONV0 + 2 * f), pairs[n], normed if f == 0 else None)
                        if f == 3 and not last:
                            pe.wait_ge(xs_done, i * TB + 2 * TB)
                            pe.wait_ge(v_done, i * 2 + 2)
                            turn_x(0)
                        if f == 5 and not last:
                            pe.wait_ge(u_done, i * 2 + 3)
                            turn_x(1)
                tiles_loop(pe, conv_tile)

                def turn_rows(half, group, wait_bank=None):
                    for k in range(4 * half, 4 * half + 4):
                        if wait_bank is not None and k % 2 == 0:
                            wait_bank(k % 4)
                        for t in range(TB):
                            ins = pe.transpose(bank(group, k % 4)[:, t * P:(t + 1) * P],
                                               xn[:, t, k * P:(k + 1) * P], ident[:, :])
                        ins.then_inc(turned, 1)

                def rows_out(first, pair, half, wait_data):
                    for kh in range(2):
                        strips.ready(pe, first + kh)
                        hi, lo = strips.views(kh, 4)
                        for t in range(TB):
                            c = slice(t * P, (t + 1) * P)
                            for k in range(4):
                                kk = 4 * kh + k
                                if half == 0 and t == 0:
                                    wait_data(kk)
                                if half == 1 and kk == 0 and wait_data is not None:
                                    wait_data(t)
                                ins = product(pe, bank(half, t), (pair[0][:, kk, c], pair[1][:, kk, c]),
                                              (hi[:, k, :], lo[:, k, :]), kk == 0, kk == KB - 1)
                        ins.then_inc(strips.used, 1)

                pe.wait_ge(v_done, 2 * TILES + 1)
                rows_out(ATT0, (q_hi, q_lo), 0, lambda kk: pe.wait_ge(v_lo_done, kk + 1))
                pe.wait_ge(u_done, 2 * TILES + 1)
                rows_out(ATT0 + 2, (q_hi, q_lo), 1, None)

                def attend_tile(i, n, last):
                    first = i * NS + BODY0
                    pe.wait_ge(rows_vector, i * (2 * TB - 1) + (TB - 1))
                    pe.wait_ge(rows_scalar, i + 1)
                    turn_rows(0, 0)
                    pe.wait_ge(added, i * 8 + 4)
                    pe.wait_ge(logits_read, i + 1)
                    turn_rows(1, 1)
                    for half in range(2):
                        if half == 1:
                            pe.wait_ge(n1_lo, i * KB + KB)
                        columns(half, first + 2 * half, (act_hi, act_lo),
                                (lambda kk: pe.wait_ge(n1_lo, i * KB + (kk + 1))) if half == 0 else None)
                    for hd in range(HEADS):
                        if hd % 2 == 0:
                            pe.wait_ge(ql, i * KB + (4 * (hd // 2) + 4))
                        sc = scores_bank(hd)
                        for t in range(TB):
                            c = slice(t * P, (t + 1) * P)
                            for b in range(HB):
                                m = HB * hd + b
                                ins = product(pe, sc[:, t, :], (q_hi[:, m, c], q_lo[:, m, c]),
                                              (k_hi[:, m, :], k_lo[:, m, :]), b == 0, b == HB - 1)
                        ins.then_inc(scored, 1)
                    for hd in range(HEADS):
                        if hd % 2 == 0:
                            pe.wait_ge(exped, i * HEADS * TB + (hd + 2) * TB)
                        pe.wait_ge(p_done, i * HEADS + (hd + 1))
                        for m in range(MB):
                            for t in range(TB):
                                ins = pe.transpose(bank(hd // 2, MB * (hd % 2) + m)[:, t * P:(t + 1) * P],
                                                   pr[:, hd, t, m * P:(m + 1) * P], ident[:, :])
                            ins.then_inc(turned, 1)
                    for hd in range(HEADS):
                        pe.wait_ge(pt_lo, i * KB + (MB * hd + MB))
                        for b in range(HB):
                            c = slice(hd * HD + b * P, hd * HD + (b + 1) * P)
                            for m in range(MB):
                                ins = product(pe, bank(hd // 2, HB * (hd % 2) + b), (v_hi[:, m, c], v_lo[:, m, c]),
                                              (q_hi[:, MB * hd + m, :], q_lo[:, MB * hd + m, :]), m == 0, m == MB - 1)
                        if hd % 2 == 1:
                            ins.then_inc(valued, 1)
                    rows_out(first + 4, (act_hi, act_lo), 0, lambda kk: pe.wait_ge(o_lo, i * KB + (kk + 1)))
                    rows_out(first + 6, (act_hi, act_lo), 1, None)
                    if not last:
                        pe.wait_ge(added, i * 8 + 6)
                        rows_out(first + 8, (q_hi, q_lo), 0, lambda kk: pe.wait_ge(v_lo_done, i * KB + (KB + kk + 1)))
                    pe.wait_ge(added, i * 8 + 8)
                    pe.wait_ge(rows_vector, i * (2 * TB - 1) + (2 * TB - 1))
                    turn_rows(0, 1)
                    turn_rows(1, 0, None if last else lambda k: pe.wait_ge(added, i * 8 + (9 + k // 2)))
                    if not last:
                        rows_out(first + 10, (q_hi, q_lo), 1, lambda t: pe.wait_ge(n3_lo, i * KB + (t + 1)))
                    g = 1 if last else 0
                    if not last:
                        pe.wait_ge(n3_lo, i * KB + KB)
                    for k in range(KB):
                        if last:
                            pe.wait_ge(n3_lo, i * KB + (k + 1))
                        ins = product(pe, bank(g, 0)[0:E, :], (r_hi[:, k, :], r_lo[:, k, :]),
                                      (act_hi[:, k, :], act_lo[:, k, :]), k == 0, k == KB - 1)
                    ins.then_inc(routed, 1)
                    if not last:
                        pe.wait_ge(added, i * 8 + 12)
                    pe.wait_ge(logits_out, i + 1)
                    for t in range(TB):
                        ins = pe.transpose(bank(1 - g, 0)[:, t * E:(t + 1) * E], logits_t[:, t * P:(t + 1) * P],
                                           ident[0:E, 0:E])
                    ins.then_inc(logits_turned, 1)
                tiles_loop(pe, attend_tile)
        pctx.close()

    def back():
        pctx = ExitStack()
        sem = lambda name: pctx.enter_context(nc.semaphore(name))
        strips = Strips(nc, pctx, "back", w_raw, w_hi, w_lo)

        BITS = 30
        ROUNDS = BITS // 2
        UNROLL = 5
        NT = SEQ // P
        BIG = 4096.0
        probs_turned, counted, totalled, bit_step, chain_sem, index_done = (
            sem("probs_turned"), sem("counted"), sem("totalled"), sem("bit_step"), sem("sl_chain"), sem("index_done"))
        spread_in, spread, masks_done, prefixed, hots_done, listed = (
            sem("spread_in"), sem("spread"), sem("masks_done"), sem("prefixed"), sem("hots_done"), sem("listed"))
        low_digits, numbered = sem("low_digits"), sem("numbered")
        z_done, z_stored, z_loaded, z_turned = sem("z_done"), sem("z_stored"), sem("z_loaded"), sem("z_turned")
        by_expert = vin[:, 0:256]
        compared = h[:, 2304:3072].rearrange("p (j n) -> p j n", j=3)
        count = stat[:, 24:27]
        stands = stat[:, 27:30]
        standing = stat[:, 30:31]
        unit = stat[:, 31:32]
        words = ints[:, 0:13].bitcast(U32)
        cand = words[:, 0:4]
        digits = words[:, 4:8]
        ahead = words[:, 8:12]
        won = words[:, 12:13]
        spread_rhs = vin[:, 512:528]
        thr_row = vin[:, 528:544]
        above_total = vin[:, 544:560]
        masks = vin[:, 1024:1280].bitcast(BF16).rearrange("p (s t e) -> p s t e", s=2, t=NT)
        before = h[:, 0:(NT + 1) * E].bitcast(BF16).rearrange("p (t s e) -> p t s e", t=NT + 1, s=2)
        a1 = vin[:, 1536:1792]
        b1 = vin[:, 1792:2048]
        pos = h[:, 1024:1280].bitcast(I32)
        low = h[:, 1280:1536].bitcast(I32)
        high = h[:, 1536:1792].bitcast(I32)
        hot = xs[:, :].rearrange("p (n b) -> p n b", b=E)
        CHUNKS = 4
        hot_high = q_hi[:, :, :].rearrange("p k c -> p (k c)")
        hot_low = q_lo[:, :, :].rearrange("p k c -> p (k c)")
        z_all = vin[:, 2048:2304].rearrange("p (h n) -> p h n", h=2)
        z = vin[:, 2304:2336].rearrange("p (h b) -> p h b", h=2)
        lists = h[0:E * CB, 2048:2048 + P]
        flat = index_d.rearrange("e c -> (e c)")
        prefix = bank(0, 1)

        NS = 12
        NF = 8
        gathered = [sem("gathered0"), sem("gathered1")]
        index_step, scattered, y_free = sem("index_step"), sem("scattered"), sem("y_free")
        turned, gate_read, freed = sem("ex_turned"), sem("gate_read"), sem("ex_freed")
        x_hi, low_copied, silu_done, hid_done, hid_hi_done, hid_lo_done, aff_done = (
            sem("ex_x_hi"), sem("low_copied"), sem("silu_done"), sem("hid_done"), sem("hid_hi_done"),
            sem("hid_lo_done"), sem("aff_done"))
        RW = CB * ROW
        xg = [t[:, 0:RW].rearrange("p (c r) -> p c r", c=CB) for t in (h, vin)]
        xt = [act_hi, act_lo]
        hid_hi = q_hi[:, :, 0:CAP]
        hid_lo = q_lo[:, :, 0:CAP]
        low_half = h[:, RW:RW + 4 * CAP].rearrange("p (b c) -> p b c", b=4)
        sums = vin[:, RW:RW + 4 * CAP].rearrange("p (b c) -> p b c", b=4)
        silu = h[:, RW + 4 * CAP:RW + 6 * CAP].rearrange("p (b c) -> p b c", b=2)
        hid = vin[:, RW + 4 * CAP:RW + 6 * CAP].rearrange("p (b c) -> p b c", b=2)
        y = [xs[:, n * CB * D:(n + 1) * CB * D].rearrange("p (c d) -> p c d", c=CB) for n in range(2)]
        aff = stat[:, 24:24 + CB]
        gather_index = [indices[:, 2 * n:2 * n + 2] for n in range(2)]
        scatter_index = [indices[:, 4 + 2 * n:6 + 2 * n] for n in range(2)]
        wg = w_gate[0].rearrange("e (k p) n -> p e k n", p=P)
        wu = w_up[0].rearrange("e (k p) n -> p e k n", p=P)
        wd = w_down[0].rearrange("e (k p) n -> p e k n", p=P)

        def turned_rows(j):
            return bank(0)[:, 2 * j:2 * j + 2, :].rearrange("p b (t c) -> p (b t) c", c=CAP)

        FT = 2
        PIECES = SEQ // (P * FT)
        EARLY = 3
        ROWS = PIECES
        ORDER = list(range(EARLY)) + [ROWS] + list(range(EARLY, PIECES))
        loaded = [sem(f"fn_loaded{c}") for c in range(PIECES + 1)]
        summed, gain_loaded, squares, var_done, root_done, final_chain, normed, stored, rows_stored = (
            sem("fn_summed"), sem("fn_gain"), sem("fn_squares"), sem("fn_var"), sem("fn_root"), sem("fn_chain"),
            sem("fn_normed"), sem("fn_stored"), sem("fn_rows_stored"))
        rows_asked = sem("fn_rows_asked")
        left = [sem(f"fn_left{c}") for c in range(EARLY)]
        halves = [[b[:, n * FT * D:(n + 1) * FT * D].rearrange("p (t d) -> p t d", t=FT) for n in range(2)]
                  for b in (h, xs, vin, w_raw[:, :, :].rearrange("p s n -> p (s n)"))]
        pieces = [halves[0][0], halves[1][0], halves[2][0],
                  halves[3][0], halves[3][1], halves[2][1], halves[1][0], halves[1][1], halves[0][0]]
        fn = probs[:, 0:6 * FT * (PIECES + 1)].rearrange("p (v c t) -> p v c t", v=6, t=FT)
        f_ss, f_var, f_root, f_rstd, f_tmp, f_tmp2 = (fn[:, v] for v in range(6))
        sum_v = sum_d.rearrange("(i t p) d -> i p t d", p=P, t=FT)
        out_v = out[0].rearrange("(i t p) d -> i p t d", p=P, t=FT)

        with nc.Block() as block:
            @block.sync
            def _(sp):
                def load(e, s):
                    g = e * NS + s
                    later, s = s // NS, s % NS
                    ex = bass.ds(e, 1)
                    if s < 8:
                        w, c = (wg, wu)[s % 2][:, later:], s // 2 * 256
                        source, blocks = w[:, ex, :, c:c + 256].rearrange("p e k n -> p (e k) n"), KB
                    else:
                        half, kh = s % 2, (s - 8) // 2
                        source = wd[:, ex, 4 * kh:4 * kh + 4, T * half:T * half + T].rearrange("p e k n -> p (e k) n")
                        blocks = 4
                    strips.load(sp, g, s % 2, source, blocks, spare)

                for s in range(4):
                    load(0, s)
                sp.dma_start(gain_row[:, :], norm_final.rearrange("(o d) -> o d", o=1).to_broadcast([P, D])).then_inc(
                    gain_loaded, STEP)
                sp.wait_ge(z_done, 1)
                sp.dma_start(flat.rearrange("(h r b) -> r h b", h=2, b=E), z).then_inc(z_stored, STEP)
                sp.wait_ge(z_stored, STEP)
                sp.dma_start(lists, flat.rearrange("(r c) -> r c", c=P)).then_inc(z_loaded, STEP)

                with sp.Fori(0, E - 1) as e:
                    for s in range(4, NS + 4):
                        load(e, s)
                for s in range(4, NS):
                    load(E - 1, s)
                    if s == 9:
                        sp.wait_ge(summed, 1)
                        sp.wait_ge(aff_done, E)
                    for c in range(EARLY):
                        if s == (9, 11, 11)[c]:
                            sp.dma_start(pieces[c], sum_v[c]).then_inc(loaded[c], STEP)
                for c in range(EARLY):
                    sp.wait_ge(normed, FT * (c + 1))
                    sp.dma_start(out_v[c], pieces[c]).then_inc(left[c], STEP)
                sp.wait_ge(summed, 2)
                for c in range(EARLY, PIECES):
                    if c == EARLY + 1:
                        sp.wait_ge(rows_asked, 1)
                        sp.wait_ge(left[1], STEP)
                        sp.wait_ge(left[2], STEP)
                    sp.dma_start(pieces[c], sum_v[c]).then_inc(loaded[c], STEP)
                sp.wait_ge(rows_stored, CB * STEP)
                for c in range(EARLY, PIECES):
                    sp.wait_ge(normed, FT * (ORDER.index(c) + 1))
                    sp.dma_start(out_v[c], pieces[c]).then_inc(stored, STEP)
                sp.wait_ge(stored, STEP * (PIECES - EARLY))

            @block.gpsimd
            def _(pool):
                strips.open(pool=pool)
                pool.sem_inc(y_free, 1)

                def gather(n):
                    for c in range(CB):
                        pool.indirect_dma_start(xg[n][:, c, :], None, row_d, bass.IndirectOffsetOnAxis(
                            ap=gather_index[n][:, c:c + 1], axis=0)).then_inc(gathered[n], STEP)

                for n in range(2):
                    strips.split_lo_pool(pool, n, n)
                pool.wait_ge(rows_written, (3 * TILES - 1) * STEP)
                pool.wait_ge(last_written, STEP)
                for c in range(CB):
                    pool.dma_start(primed[:, c, :], row_d[0:16, 0:16]).then_inc(scattered, STEP)
                pool.wait_ge(index_done, 1)
                for n in range(2):
                    pool.tensor_copy(gather_index[n], index[:, CB * n:CB * n + CB]).then_inc(index_step, 1)
                pool.wait_ge(index_step, 2)
                for n in range(2):
                    gather(n)

                def expert(e, n, steps, fills, has_next, has_second):
                    for s in range(2, NS + 2 if has_next else NS):
                        strips.split_lo_pool(pool, e * NS + s, s % 2)
                        if s == 6 and not has_next:
                            pool.wait_ge(scattered, E * CB * STEP)
                            pool.sem_inc(summed, 1)
                    pool.tensor_copy(scatter_index[n], index[:, bass.ds(e * CB, CB)]).then_inc(index_step, 1)
                    pool.wait_ge(index_step, steps + 1)
                    pool.wait_ge(freed, fills)
                    pool.wait_ge(scattered, e * CB * STEP + CB * STEP)
                    pool.sem_inc(y_free, 1)
                    if not has_next:
                        for c in range(EARLY):
                            pool.wait_ge(loaded[c], STEP)
                    for c in range(CB):
                        pool.indirect_dma_start(sum_d, bass.IndirectOffsetOnAxis(ap=scatter_index[n][:, c:c + 1], axis=0),
                                                y[n][:, c, :], None, compute_op=ALU.add).then_inc(scattered, STEP)
                    if has_second:
                        pool.tensor_copy(gather_index[n], index[:, bass.ds(e * CB + 2 * CB, CB)]).then_inc(index_step, 1)
                        pool.wait_ge(index_step, steps + 2)
                        apart(pool, spare)
                        gather(n)

                with pool.Fori(0, E // 2 - 1) as i:
                    for n in range(2):
                        e = i * 2 + n
                        expert(e, n, e * 2 + 2, e * NF + NF + 2, True, True)
                expert(E - 2, 0, 2 * E - 2, (E - 1) * NF + 2, True, False)
                expert(E - 1, 1, 2 * E - 1, E * NF, False, False)
                pool.wait_ge(scattered, E * CB * STEP + CB * STEP)
                pool.sem_inc(summed, 1)

                pool.wait_ge(left[0], STEP)
                for c in range(CB):
                    pool.indirect_dma_start(pieces[ROWS][:, c, :], None, sum_d, bass.IndirectOffsetOnAxis(
                        ap=scatter_index[1][:, c:c + 1], axis=0)).then_inc(loaded[ROWS], STEP)
                pool.sem_inc(rows_asked, 1)
                pool.wait_ge(normed, FT * (EARLY + 1))
                for n in range(1, EARLY):
                    pool.wait_ge(left[n], STEP)
                for c in range(CB):
                    pool.indirect_dma_start(out[0], bass.IndirectOffsetOnAxis(ap=scatter_index[1][:, c:c + 1], axis=0),
                                            pieces[ROWS][:, c, :], None).then_inc(rows_stored, STEP)
                pool.wait_ge(rows_stored, CB * STEP)

            @block.scalar
            def _(act):
                def turn_hi(n, at):
                    for j in range(2):
                        act.wait_ge(turned, at + j + 1)
                        act.activation(xt[n][:, 4 * j:4 * j + 4, 0:CAP], turned_rows(j), ACT.Copy).then_inc(x_hi, 1)

                def split(e, s):
                    g = e * NS + s
                    strips.split_hi(act, g, s % 2)

                def expert(e, n, has_next):
                    for f in range(4):
                        split(e, 2 * f + 2)
                        strips.done(act, e * NS + 2 * f + 1)
                        for part in range(2):
                            b = slice(2 * part, 2 * part + 2)
                            act.activation(low_half[:, b, :], bank(f % 2)[:, b, CAP:2 * CAP],
                                           ACT.Copy).then_inc(low_copied, 1)
                        split(e, 2 * f + 3)
                        act.wait_ge(gate_read, e * 4 + f + 1)
                        act.activation(silu, sums[:, 0:2, :], ACT.Silu).then_inc(silu_done, 1)
                        act.wait_ge(hid_done, e * 4 + f + 1)
                        act.activation(hid_hi[:, 2 * f:2 * f + 2, :], hid, ACT.Copy).then_inc(hid_hi_done, 1)
                    if has_next:
                        turn_hi(1 - n, e * 2 + 2)
                    if not has_next:
                        prime(act, primer, 4, ACT.Sqrt)
                    for s in range(10, 14 if has_next else 12):
                        split(e, s)
                        if not has_next:
                            piece_squares(s - 10)
                            piece_root(s - 10)

                def piece_squares(c):
                    act.wait_ge(loaded[c], STEP if c != ROWS else CB * STEP)
                    for t in range(FT):
                        act.activation(junk[:, 2 * (ORDER.index(c) % 2) + t, :], pieces[c][:, t, :], ACT.Square,
                                       accum_out=f_ss[:, c, t:t + 1]).then_inc(squares, 1)

                def piece_root(c):
                    act.wait_ge(var_done, ORDER.index(c) + 1)
                    act.activation(f_root[:, c, :], f_var[:, c, :], ACT.Sqrt).then_inc(root_done, 1)

                split(0, 0)
                split(0, 1)
                for t in range(NT):
                    act.wait_ge(low_digits, t // (NT // CHUNKS) + 1)
                    act.activation(hot_low[:, t * 256:t * 256 + 256], xs[:, t * 256:t * 256 + 256], ACT.Copy,
                                   scale=token_id[:, t:t + 1]).then_inc(numbered, 1)
                turn_hi(0, 0)
                with act.Fori(0, E // 2 - 1) as i:
                    for n in range(2):
                        expert(i * 2 + n, n, True)
                expert(E - 2, 0, True)
                expert(E - 1, 1, False)

                for c in range(2, EARLY):
                    piece_squares(c)
                    piece_root(c)
                rest = ORDER[EARLY:]
                piece_squares(rest[0])
                for c, following in zip(rest, rest[1:] + [None]):
                    if following is not None:
                        piece_squares(following)
                    piece_root(c)

            @block.vector
            def _(dve):
                strips.open(dve=dve)
                chain = Chain(dve, chain_sem)
                for j in range(4):
                    dve.memset(cand[:, j:j + 1], j << (BITS - 2))
                    ins = dve.memset(digits[:, j:j + 1], j << (BITS - 2))
                chain(ins)
                chain(dve.memset(unit, float(1 << (BITS - 2))))
                dve.wait_ge(probs_turned, 1)
                chain(dve.tensor_copy(by_expert, bank(0, 0)[:, 0:256]))
                with dve.Fori(0, ROUNDS // UNROLL) as b:
                    for n in range(UNROLL):
                        step = b * (6 * UNROLL) + 6 * n
                        for j in range(3):
                            ins = dve.tensor_scalar(compared[:, j, :], by_expert, cand[:, j + 1:j + 2].bitcast(F32), None,
                                                    ALU.is_ge, ALU.add, accum_out=count[:, j:j + 1])
                        ins.then_inc(counted, 1)
                        dve.tensor_scalar(digits, digits, 2, None, ALU.logical_shift_right).then_inc(bit_step, 1)
                        dve.wait_ge(bit_step, step + 1)
                        dve.tensor_tensor(ahead, digits, cand[:, 0:1].to_broadcast([P, 4]),
                                          ALU.bitwise_or).then_inc(bit_step, 1)
                        dve.wait_ge(totalled, b * UNROLL + (n + 1))
                        dve.tensor_scalar(stands, bank(1, 0)[:, 0:3], CAP - 0.5, None, ALU.is_ge, ALU.add,
                                          accum_out=standing).then_inc(bit_step, 1)
                        dve.wait_ge(bit_step, step + 3)
                        dve.tensor_scalar(won, standing, unit, None, ALU.mult).then_inc(bit_step, 1)
                        dve.wait_ge(bit_step, step + 4)
                        dve.tensor_tensor(cand, ahead, won.to_broadcast([P, 4]), ALU.bitwise_or).then_inc(bit_step, 1)
                        dve.tensor_scalar(unit, unit, 0.25, None, ALU.mult).then_inc(bit_step, 1)
                        dve.wait_ge(bit_step, step + 6)
                dve.tensor_scalar(spread_rhs, ident[:, 0:E], cand[:, 0:1].bitcast(F32), None, ALU.mult).then_inc(spread_in, 1)
                chain(dve.memset(before[:, 0, :, :], 0.0))
                dve.wait_ge(spread, 1)
                chain(dve.tensor_copy(thr_row, bank(1, 1)[:, 0:E]))
                by_token = probs[:, :].rearrange("p (t e) -> p t e", e=E)
                row = thr_row.unsqueeze(1).to_broadcast([P, NT, E])
                dve.tensor_tensor(masks[:, 0, :, :], by_token, row, ALU.is_gt)
                chain(dve.tensor_tensor(masks[:, 1, :, :], by_token, row, ALU.is_equal))
                for t in range(NT):
                    chain(dve.tensor_tensor(before[:, t + 1, :, :], before[:, t, :, :], masks[:, :, t, :], ALU.add))
                dve.sem_inc(masks_done, 1)
                strips.split_lo(dve, 0, 0)
                dve.wait_ge(prefixed, 1)
                above = masks[:, 0, :, :].rearrange("p t e -> p (t e)")
                equal = masks[:, 1, :, :].rearrange("p t e -> p (t e)")
                chain(dve.tensor_copy(above_total, bank(1, 2)[:, 0:E]))
                dve.scalar_tensor_tensor(a1, prefix[:, 0:256], -BIG, above, ALU.add, ALU.mult)
                chain(dve.tensor_tensor(b1.rearrange("p (t e) -> p t e", e=E),
                                        prefix[:, 256:512].rearrange("p (t e) -> p t e", e=E),
                                        above_total.unsqueeze(1).to_broadcast([P, NT, E]), ALU.add))
                chain(dve.scalar_tensor_tensor(b1, b1, -BIG, equal, ALU.add, ALU.mult))
                chain(dve.scalar_tensor_tensor(pos, a1, BIG, b1, ALU.add, ALU.add))
                dve.tensor_scalar(low, pos, 15, None, ALU.bitwise_and)
                chain(dve.tensor_scalar(high, pos, 4, None, ALU.logical_shift_right))
                n = NT // CHUNKS * E
                ramps = ramp[:, :].unsqueeze(1).to_broadcast([P, n, E])
                for c in range(CHUNKS):
                    b = slice(c * n, c * n + n)
                    dve.tensor_tensor(hot[:, b, :], low[:, b].unsqueeze(2).to_broadcast([P, n, E]), ramps,
                                      ALU.is_equal).then_inc(low_digits, 1)
                    dve.tensor_tensor(hot_high.rearrange("p (n a) -> p n a", a=E)[:, b, :],
                                      high[:, b].unsqueeze(2).to_broadcast([P, n, E]), ramps,
                                      ALU.is_equal).then_inc(hots_done, 1)
                    if c == 1:
                        strips.split_lo(dve, 1, 1)
                dve.wait_ge(listed, 1)
                for half in range(2):
                    chain(dve.tensor_tensor(z_all[:, half, :], bank(0, 2 + half)[:, half * P:half * P + P], own_block[:, :], ALU.mult))
                    chain(dve.tensor_reduce(z[:, half, :], z_all[:, half, :].rearrange("p (e b) -> p b e", b=E),
                                            axis=X, op=ALU.add))
                dve.sem_inc(z_done, 1)
                dve.wait_ge(z_turned, 1)
                chain(dve.tensor_copy(index[:, :], bank(1, 3)[:, 0:E * CB]))
                dve.sem_inc(index_done, 1)


                def turn_lo(n, at):
                    for j in range(2):
                        dve.wait_ge(x_hi, at + j + 1)
                        dve.tensor_tensor(xt[n][:, 4 * j:4 * j + 4, CAP:2 * CAP], turned_rows(j),
                                          xt[n][:, 4 * j:4 * j + 4, 0:CAP].bitcast(F32), ALU.subtract).then_inc(freed, 1)

                def split(e, s):
                    strips.split_lo(dve, e * NS + s, s % 2)

                def expert(e, n, has_next):
                    for f in range(4):
                        split(e, 2 * f + 2)
                        for part in range(2):
                            b = slice(2 * part, 2 * part + 2)
                            dve.wait_ge(low_copied, e * 8 + (2 * f + part + 1))
                            dve.tensor_tensor(sums[:, b, :], bank(f % 2)[:, b, 0:CAP], low_half[:, b, :],
                                              ALU.add).then_inc((gate_read, freed)[part], 1)
                        split(e, 2 * f + 3)
                        dve.wait_ge(silu_done, e * 4 + f + 1)
                        dve.wait_ge(freed, e * NF + f + 3)
                        if f == 0:
                            dve.tensor_copy(aff.rearrange("p (c o) -> p c o", o=1),
                                            xg[n][:, :, bass.ds(e + D, 1)]).then_inc(aff_done, 1)
                        dve.tensor_tensor(hid, silu, sums[:, 2:4, :], ALU.mult).then_inc(hid_done, 1)
                        dve.wait_ge(hid_hi_done, e * 4 + f + 1)
                        dve.tensor_tensor(hid_lo[:, 2 * f:2 * f + 2, :], hid,
                                          hid_hi[:, 2 * f:2 * f + 2, :].bitcast(F32), ALU.subtract).then_inc(hid_lo_done, 1)
                    if has_next:
                        turn_lo(1 - n, e * 2 + 2)
                    dve.wait_ge(aff_done, e + 1)
                    split(e, 10)
                    if not has_next:
                        dve.wait_ge(gain_loaded, STEP)
                        piece_var(0)
                        piece_norm(0)
                    split(e, 11)
                    if has_next:
                        split(e, 12)
                    else:
                        piece_var(1)
                        piece_norm(1)
                    dve.wait_ge(y_free, e + 1)
                    for half in range(2):
                        strips.done(dve, e * NS + 10 + half)
                        for c in range(CB):
                            ins = dve.tensor_scalar(y[n][:, c, T * half:T * half + T], bank(1, 2 * half + c), aff[:, c:c + 1],
                                                    None, ALU.mult)
                        ins.then_inc(freed, 1)
                    if has_next:
                        split(e, 13)

                chain = Chain(dve, final_chain)

                def piece_var(c):
                    dve.wait_ge(squares, FT * (ORDER.index(c) + 1))
                    dve.tensor_scalar(f_var[:, c, :], f_ss[:, c, :], 1.0 / D, RMS_EPS, ALU.mult, ALU.add).then_inc(
                        var_done, 1)

                def piece_norm(c):
                    dve.wait_ge(root_done, ORDER.index(c) + 1)
                    refine_rstd(dve, chain, f_rstd[:, c, :], f_root[:, c, :], f_var[:, c, :], f_tmp[:, c, :],
                                f_tmp2[:, c, :])
                    for t in range(FT):
                        dve.scalar_tensor_tensor(pieces[c][:, t, :], pieces[c][:, t, :], f_rstd[:, c, t:t + 1],
                                                 gain_row[:, :], ALU.mult, ALU.mult).then_inc(normed, 1)

                turn_lo(0, 0)
                with dve.Fori(0, E // 2 - 1) as i:
                    for n in range(2):
                        expert(i * 2 + n, n, True)
                expert(E - 2, 0, True)
                expert(E - 1, 1, False)

                for c in range(2, EARLY):
                    piece_var(c)
                    piece_norm(c)
                rest = ORDER[EARLY:]
                piece_var(rest[0])
                for c, following in zip(rest, rest[1:] + [None]):
                    if following is not None:
                        piece_var(following)
                    piece_norm(c)

            @block.tensor
            def _(pe):
                strips.open(pe=pe)
                for n in range(2):
                    last = pe.transpose(bank(0, 0)[:, n * P:(n + 1) * P], probs[:, n * P:(n + 1) * P], ident[:, :])
                last.then_inc(probs_turned, 1)
                with pe.Fori(0, ROUNDS) as b:
                    pe.wait_ge(counted, b + 1)
                    pe.matmul(bank(1, 0)[:, 0:3], same_expert[:, :], count, start=True, stop=True).then_inc(totalled, 1)
                pe.wait_ge(spread_in, 1)
                pe.matmul(bank(1, 1)[:, 0:E], ones[:, :], spread_rhs, start=True, stop=True).then_inc(spread, 1)
                pe.wait_ge(masks_done, 1)
                pe.matmul(prefix, upper[:, :], masks.rearrange("p s t e -> p (s t e)"), start=True, stop=False)
                pe.matmul(prefix.rearrange("p (s t e) -> p s t e", s=2, t=NT)[:, 0, :, :], ones_b[:, :],
                          before[:, 0:NT, 0, :], start=False, stop=False)
                pe.matmul(prefix.rearrange("p (s t e) -> p s t e", s=2, t=NT)[:, 1, :, :], ones_b[:, :],
                          before[:, 0:NT, 1, :], start=False, stop=True)
                pe.matmul(bank(1, 2)[:, 0:E], ones_b[:, :], before[:, NT, 0, :], start=True, stop=True).then_inc(prefixed, 1)
                for t in range(NT):
                    if t % (NT // CHUNKS) == 0:
                        pe.wait_ge(hots_done, t // (NT // CHUNKS) + 1)
                        pe.wait_ge(numbered, t + NT // CHUNKS)
                    for half in range(2):
                        c = slice(t * 256 + half * P, t * 256 + half * P + P)
                        last = pe.matmul(bank(0, 2 + half)[:, 0:256], hot_high[:, c], hot_low[:, t * 256:t * 256 + 256],
                                         start=t == 0, stop=t == NT - 1)
                last.then_inc(listed, 1)
                pe.wait_ge(z_loaded, STEP)
                pe.transpose(bank(1, 3)[:, 0:E * CB], lists, ident[0:E * CB, 0:E * CB]).then_inc(z_turned, 1)


                def turn(n, wait_rows, at):
                    wait_rows()
                    if at is not None:
                        pe.wait_ge(freed, at)
                    for j in range(2):
                        for k in range(4 * j, 4 * j + 4):
                            for c in range(CB):
                                last = pe.transpose(turned_rows(j)[:, k - 4 * j, c * P:(c + 1) * P],
                                                    xg[n][:, c, k * P:(k + 1) * P], ident[:, :])
                        last.then_inc(turned, 1)

                def expert(e, n, gathers, has_next):
                    for f in range(4):
                        pe.wait_ge(freed, e * NF + f + 1)
                        for part in range(2):
                            s = 2 * f + part
                            strips.ready(pe, e * NS + s)
                            hi, lo = strips.views(s % 2, KB)
                            for m in range(2):
                                o = bank(f % 2, 2 * part + m)
                                c = slice(m * P, (m + 1) * P)
                                for k in range(KB):
                                    pe.matmul(o, hi[:, k, c], xt[n][:, k, :], start=k == 0, stop=False)
                                    last = pe.matmul(o[:, 0:CAP], lo[:, k, c], xt[n][:, k, 0:CAP], start=False,
                                                     stop=k == KB - 1)
                            last.then_inc(strips.used, 1)
                    if has_next:
                        turn(1 - n, gathers, e * NF + 5)
                    pe.wait_ge(gate_read, e * 4 + 4)
                    for kh in range(2):
                        pe.wait_ge(hid_lo_done, e * 4 + 2 * kh + 2)
                        for half in range(2):
                            if kh == 0 and half == 1:
                                pe.wait_ge(freed, e * NF + 6)
                            s = 8 + half + 2 * kh
                            strips.ready(pe, e * NS + s)
                            hi, lo = strips.views(s % 2, 4)
                            for c in range(CB):
                                t = slice(c * P, (c + 1) * P)
                                for k in range(4):
                                    kk = 4 * kh + k
                                    last = product(pe, bank(1, 2 * half + c), (hid_hi[:, kk, t], hid_lo[:, kk, t]),
                                                   (hi[:, k, :], lo[:, k, :]), kk == 0, kk == FB - 1)
                            last.then_inc(strips.used, 1)

                turn(0, lambda: pe.wait_ge(gathered[0], CB * STEP), None)
                pe.wait_ge(freed, 2)
                with pe.Fori(0, E // 2 - 1) as i:
                    expert(i * 2, 0, lambda: pe.wait_ge(gathered[1], i * CB * STEP + CB * STEP), True)
                    expert(i * 2 + 1, 1, lambda: pe.wait_ge(gathered[0], i * CB * STEP + 2 * CB * STEP), True)
                expert(E - 2, 0, lambda: pe.wait_ge(gathered[1], E // 2 * CB * STEP), True)
                expert(E - 1, 1, None, False)
        pctx.close()

    front()
    back()
    ctx.close()


_INS = ["x", "mem", "norm_mix", "norm_xattn", "norm_mem", "norm_ffn", "norm_final", "conv_w_in", "conv_w",
        "conv_w_out", "xattn_w_q", "xattn_w_kv", "xattn_w_o", "moe_router", "moe_w_gate", "moe_w_up", "moe_w_down"]


def kernel(**inputs):
    import numpy as np
    import concourse.bacc as bacc
    from concourse.bass_utils import run_bass_kernel_spmd

    nc = bacc.Bacc("TRN2", target_bir_lowering=False, num_devices=1)
    arrays, args = {}, []
    for name in _INS:
        a = np.ascontiguousarray(inputs[name])
        arrays[f"in_{name}"] = a
        args.append(nc.dram_tensor(f"in_{name}", a.shape, mybir.dt.from_np(a.dtype), kind="ExternalInput").ap())
    out = nc.dram_tensor("out", (1, SEQ, D), F32, kind="ExternalOutput").ap()
    build(nc, *args, out)
    return run_bass_kernel_spmd(nc, [arrays], core_ids=[0]).results[0]["out"]
```
